# Optimizing a Trainium2 kernel written in Bass

```python
import math
import jax, jax.numpy as jnp
from jax import lax
import numpy as np

D_MODEL = 1024
BATCH = 1
SEQ = 512
DEPTH = 1

CHUNK = 64
GMLP_BLOCK = 128
GMLP_GROUPS = 4
GMLP_WIDTH = D_MODEL
GMLP_GROUP_DIM = GMLP_WIDTH // GMLP_GROUPS
SB_HEADS = 16
SB_HEAD_DIM = 64
SB_WIDTH = SB_HEADS * SB_HEAD_DIM
SB_QBLOCK = 128
D_FF = 2816
N_BRANCHES = 2
D_IN = 2 * GMLP_WIDTH + 3 * SB_WIDTH + N_BRANCHES * D_MODEL
EPS = 1e-6


def rmsnorm(x, g):
    xf = x.astype(jnp.float32)
    y = xf * lax.rsqrt(jnp.mean(xf * xf, axis=-1, keepdims=True) + EPS)
    return (y * g.astype(jnp.float32)).astype(x.dtype)

def layernorm(x, g, b):
    xf = x.astype(jnp.float32)
    mu = jnp.mean(xf, axis=-1, keepdims=True)
    var = jnp.mean(jnp.square(xf - mu), axis=-1, keepdims=True)
    y = (xf - mu) * lax.rsqrt(var + EPS)
    return (y * g.astype(jnp.float32) + b.astype(jnp.float32)).astype(x.dtype)

def swiglu(x, w_gate, w_up, w_down):
    return (jax.nn.silu(x @ w_gate) * (x @ w_up)) @ w_down

def gmlp_spatial_gating(a, ln_g, ln_b, w_s, b_s):
    bsz, seq, _ = a.shape
    nblk = seq // GMLP_BLOCK
    u, v = jnp.split(a, 2, axis=-1)
    u = u.reshape(bsz, nblk, GMLP_BLOCK, GMLP_GROUPS, GMLP_GROUP_DIM)
    v = v.reshape(bsz, nblk, GMLP_BLOCK, GMLP_GROUPS, GMLP_GROUP_DIM)
    v = layernorm(v, ln_g, ln_b)
    pos = jnp.arange(GMLP_BLOCK)
    mask = (pos[None, :] // CHUNK) <= (pos[:, None] // CHUNK)
    w_masked = jnp.where(mask[None], w_s, jnp.zeros((), w_s.dtype))
    s_mix = jnp.einsum('gts,bnsgc->bntgc', w_masked, v) + jnp.transpose(b_s)[None, None, :, :, None]
    return (u * s_mix).reshape(bsz, seq, GMLP_WIDTH)

def stick_breaking_attention(q, k, v):
    q = jnp.transpose(q, (0, 2, 1, 3))
    k = jnp.transpose(k, (0, 2, 1, 3))
    v = jnp.transpose(v, (0, 2, 1, 3))
    seq = q.shape[2]
    scale = 1.0 / math.sqrt(SB_HEAD_DIM)
    outs = []
    for blk in range(seq // SB_QBLOCK):
        q0 = blk * SB_QBLOCK
        kend = q0 + SB_QBLOCK
        qb = q[:, :, q0:kend]
        kb = k[:, :, :kend]
        vb = v[:, :, :kend]
        z = jnp.einsum('bhtd,bhsd->bhts', qb, kb).astype(jnp.float32) * scale
        t_idx = q0 + jnp.arange(SB_QBLOCK)[:, None]
        s_idx = jnp.arange(kend)[None, :]
        causal = s_idx < t_idx
        log_keep = jnp.where(causal, -jax.nn.softplus(z), 0.0)
        log_w = jax.nn.log_sigmoid(z) + lax.cumsum(log_keep, axis=3, reverse=True) - log_keep
        w = jnp.where(causal, jnp.exp(log_w), 0.0)
        outs.append(jnp.einsum('bhts,bhsd->bhtd', w.astype(vb.dtype), vb))
    o = jnp.concatenate(outs, axis=2)
    return jnp.transpose(o, (0, 2, 1, 3))

def first_inputs(seed: int = 0) -> dict:
    key = jax.random.key(seed)
    ks = jax.random.split(key, 24)
    f32 = jnp.float32

    def nrm(k, shape, fan_in):
        return jax.random.normal(k, shape, f32) * (fan_in ** -0.5)

    def gain(k, shape):
        return 1.0 + 0.05 * jax.random.normal(k, shape, f32)

    L = DEPTH
    return {
        "x": jax.random.normal(ks[0], (BATCH, SEQ, D_MODEL), f32),
        "ff1_norm": gain(ks[1], (L, D_MODEL)),
        "ff1_w_gate": nrm(ks[2], (L, D_MODEL, D_FF), D_MODEL),
        "ff1_w_up": nrm(ks[3], (L, D_MODEL, D_FF), D_MODEL),
        "ff1_w_down": nrm(ks[4], (L, D_FF, D_MODEL), D_FF),
        "mix_norm": gain(ks[5], (L, D_MODEL)),
        "w_in": nrm(ks[6], (L, D_MODEL, D_IN), D_MODEL),
        "b_gate": 0.05 * jax.random.normal(ks[7], (L, N_BRANCHES * D_MODEL), f32),
        "gmlp_ln_g": gain(ks[8], (L, GMLP_GROUPS, GMLP_GROUP_DIM)),
        "gmlp_ln_b": 0.05 * jax.random.normal(ks[9], (L, GMLP_GROUPS, GMLP_GROUP_DIM), f32),
        "gmlp_w_s": nrm(ks[10], (L, GMLP_GROUPS, GMLP_BLOCK, GMLP_BLOCK), GMLP_BLOCK),
        "gmlp_b_s": 1.0 + 0.1 * jax.random.normal(ks[11], (L, GMLP_GROUPS, GMLP_BLOCK), f32),
        "w_branch_a": nrm(ks[12], (L, GMLP_WIDTH, D_MODEL), GMLP_WIDTH),
        "w_branch_b": nrm(ks[13], (L, SB_WIDTH, D_MODEL), SB_WIDTH),
        "w_out": nrm(ks[14], (L, D_MODEL, D_MODEL), D_MODEL),
        "ff2_norm": gain(ks[15], (L, D_MODEL)),
        "ff2_w_gate": nrm(ks[16], (L, D_MODEL, D_FF), D_MODEL),
        "ff2_w_up": nrm(ks[17], (L, D_MODEL, D_FF), D_MODEL),
        "ff2_w_down": nrm(ks[18], (L, D_FF, D_MODEL), D_FF),
        "final_norm": gain(ks[19], (D_MODEL,)),
    }

def first_block(x, ff1_norm, ff1_w_gate, ff1_w_up, ff1_w_down, mix_norm, w_in, b_gate,
              gmlp_ln_g, gmlp_ln_b, gmlp_w_s, gmlp_b_s, w_branch_a, w_branch_b, w_out,
              ff2_norm, ff2_w_gate, ff2_w_up, ff2_w_down, final_norm):
    bsz, seq, _ = x.shape
    splits = [2 * GMLP_WIDTH, 2 * GMLP_WIDTH + SB_WIDTH, 2 * GMLP_WIDTH + 2 * SB_WIDTH,
              2 * GMLP_WIDTH + 3 * SB_WIDTH]
    for l in range(DEPTH):
        x = x + 0.5 * swiglu(rmsnorm(x, ff1_norm[l]), ff1_w_gate[l], ff1_w_up[l], ff1_w_down[l])

        h = rmsnorm(x, mix_norm[l])
        proj = h @ w_in[l]
        a_in, q, k, v, g_logits = jnp.split(proj, splits, axis=-1)
        y_a = gmlp_spatial_gating(jax.nn.gelu(a_in, approximate=False),
                                  gmlp_ln_g[l], gmlp_ln_b[l], gmlp_w_s[l], gmlp_b_s[l])
        q = q.reshape(bsz, seq, SB_HEADS, SB_HEAD_DIM)
        k = k.reshape(bsz, seq, SB_HEADS, SB_HEAD_DIM)
        v = v.reshape(bsz, seq, SB_HEADS, SB_HEAD_DIM)
        y_b = stick_breaking_attention(q, k, v).reshape(bsz, seq, SB_WIDTH)
        gates = jax.nn.sigmoid(g_logits + b_gate[l])
        g_a, g_b = jnp.split(gates, 2, axis=-1)
        merged = g_a * (y_a @ w_branch_a[l]) + g_b * (y_b @ w_branch_b[l])
        x = x + merged @ w_out[l]

        x = x + 0.5 * swiglu(rmsnorm(x, ff2_norm[l]), ff2_w_gate[l], ff2_w_up[l], ff2_w_down[l])
    return rmsnorm(x, final_norm)


HEAD_DIM = 64
N_SWA_HEADS = 8
N_SWA_KV = 2
WINDOW = 128
BLOCK = 128
N_DSA_HEADS = 4
N_IDX_HEADS = 4
IDX_DIM = 64
TOPK_MAX = 256
N_MEM_HEADS = 4
MEM_LEN = 256
N_BRANCH = 3
D_FF_2 = 4 * D_MODEL
ROPE_THETA = 10000.0

SWA_WIDTH = N_SWA_HEADS * HEAD_DIM
SWA_KV_WIDTH = N_SWA_KV * HEAD_DIM
DSA_WIDTH = N_DSA_HEADS * HEAD_DIM
MEM_WIDTH = N_MEM_HEADS * HEAD_DIM
IN_SPLITS = (SWA_WIDTH, SWA_KV_WIDTH, SWA_KV_WIDTH,
             DSA_WIDTH, HEAD_DIM, HEAD_DIM,
             N_IDX_HEADS * IDX_DIM, IDX_DIM, N_IDX_HEADS,
             MEM_WIDTH, N_BRANCH * D_MODEL)
D_IN_2 = sum(IN_SPLITS)


def rmsnorm_2(x, g):
    xf = x.astype(jnp.float32)
    y = xf * lax.rsqrt(jnp.mean(xf * xf, axis=-1, keepdims=True) + EPS)
    return (y * g.astype(jnp.float32)).astype(x.dtype)

def rope(x, pos):
    half = x.shape[-1] // 2
    inv_freq = jnp.power(ROPE_THETA, -jnp.arange(half, dtype=jnp.float32) / half)
    ang = pos.astype(jnp.float32)[..., None] * inv_freq
    cos = jnp.cos(ang)[:, :, None, :].astype(x.dtype)
    sin = jnp.sin(ang)[:, :, None, :].astype(x.dtype)
    x1, x2 = x[..., :half], x[..., half:]
    return jnp.concatenate([x1 * cos - x2 * sin, x2 * cos + x1 * sin], axis=-1)

def sliding_window_attention(q, k, v, sinks):
    B, S, Hq, D = q.shape
    Hkv = k.shape[2]
    G = Hq // Hkv
    nb = S // BLOCK
    qb = q.reshape(B, nb, BLOCK, Hkv, G, D)

    def with_prev(t):
        tb = t.reshape(B, nb, BLOCK, Hkv, D)
        prev = jnp.concatenate([jnp.zeros_like(tb[:, :1]), tb[:, :-1]], axis=1)
        return jnp.concatenate([prev, tb], axis=2)

    kw, vw = with_prev(k), with_prev(v)
    scores = jnp.einsum("bnqkgd,bnskd->bnkgqs", qb, kw).astype(jnp.float32) * (D ** -0.5)
    qi = jnp.arange(BLOCK)[:, None]
    sj = jnp.arange(2 * BLOCK)[None, :]
    dist = qi + BLOCK - sj
    blk = jnp.arange(nb)[:, None, None]
    valid = (dist >= 0) & (dist < WINDOW) & ((blk > 0) | (sj >= BLOCK))
    scores = jnp.where(valid[None, :, None, None], scores, -jnp.inf)
    sink = jnp.broadcast_to(
        sinks.reshape(Hkv, G)[None, None, :, :, None, None].astype(jnp.float32),
        scores.shape[:-1] + (1,))
    probs = jax.nn.softmax(jnp.concatenate([scores, sink], axis=-1), axis=-1)[..., :-1]
    out = jnp.einsum("bnkgqs,bnskd->bnqkgd", probs.astype(vw.dtype), vw)
    return out.reshape(B, S, Hq * D)

def dsa_attention(q, k, v, q_idx, k_idx, w_idx):
    B, S = q.shape[:2]
    nb = S // BLOCK
    top_k = min(TOPK_MAX, S // 4)
    key_pos = jnp.arange(S)
    gather = jax.vmap(lambda t, i: t[i])

    def to_blocks(t):
        return jnp.moveaxis(t.reshape((B, nb, BLOCK) + t.shape[2:]), 1, 0)

    def block_fn(args):
        qb, qib, wb, blk = args
        qpos = blk * BLOCK + jnp.arange(BLOCK)
        rel = jax.nn.relu(jnp.einsum("bqhd,bsd->bqhs", qib, k_idx).astype(jnp.float32))
        iscore = jnp.einsum("bqhs,bqh->bqs", rel, wb.astype(jnp.float32))
        iscore = jnp.where(key_pos[None, None, :] <= qpos[None, :, None], iscore, -jnp.inf)
        _, sel = lax.top_k(iscore, top_k)
        kg = gather(k, sel)
        vg = gather(v, sel)
        s = jnp.einsum("bqhd,bqkd->bhqk", qb, kg).astype(jnp.float32) * (HEAD_DIM ** -0.5)
        s = jnp.where((sel <= qpos[None, :, None])[:, None], s, -jnp.inf)
        p = jax.nn.softmax(s, axis=-1)
        return jnp.einsum("bhqk,bqkd->bqhd", p.astype(vg.dtype), vg)

    out = lax.map(block_fn, (to_blocks(q), to_blocks(q_idx), to_blocks(w_idx), jnp.arange(nb)))
    return jnp.moveaxis(out, 0, 1).reshape(B, S, -1)

def memory_cross_attention(q, mem_k, mem_v):
    B, S = q.shape[:2]
    s = jnp.einsum("bqhd,bmhd->bhqm", q, mem_k).astype(jnp.float32) * (HEAD_DIM ** -0.5)
    p = jax.nn.softmax(s, axis=-1)
    return jnp.einsum("bhqm,bmhd->bqhd", p.astype(mem_v.dtype), mem_v).reshape(B, S, -1)

def second_inputs(seed: int = 0) -> dict:
    key = jax.random.key(seed)
    ks = jax.random.split(key, 20)
    f32 = jnp.float32

    def nrm(k, shape, scale):
        return jax.random.normal(k, shape, f32) * scale

    def gain(k, shape):
        return 1.0 + 0.02 * jax.random.normal(k, shape, f32)

    return {
        "x": nrm(ks[0], (BATCH, SEQ, D_MODEL), 1.0),
        "mem": nrm(ks[1], (BATCH, MEM_LEN, D_MODEL), 1.0),
        "positions": jnp.broadcast_to(jnp.arange(SEQ, dtype=jnp.int32)[None], (BATCH, SEQ)),
        "g_mix": gain(ks[2], (DEPTH, D_MODEL)),
        "w_in": nrm(ks[3], (DEPTH, D_MODEL, D_IN_2), D_MODEL ** -0.5),
        "b_gate": nrm(ks[4], (DEPTH, N_BRANCH * D_MODEL), 0.01),
        "sinks": nrm(ks[5], (DEPTH, N_SWA_HEADS), 0.5),
        "g_mem": gain(ks[6], (DEPTH, D_MODEL)),
        "w_mem_kv": nrm(ks[7], (DEPTH, D_MODEL, 2 * MEM_WIDTH), D_MODEL ** -0.5),
        "w_proj_swa": nrm(ks[8], (DEPTH, SWA_WIDTH, D_MODEL), SWA_WIDTH ** -0.5),
        "w_proj_dsa": nrm(ks[9], (DEPTH, DSA_WIDTH, D_MODEL), DSA_WIDTH ** -0.5),
        "w_proj_mem": nrm(ks[10], (DEPTH, MEM_WIDTH, D_MODEL), MEM_WIDTH ** -0.5),
        "w_out": nrm(ks[11], (DEPTH, D_MODEL, D_MODEL), D_MODEL ** -0.5),
        "g_mlp": gain(ks[12], (DEPTH, D_MODEL)),
        "w_mlp_in": nrm(ks[13], (DEPTH, D_MODEL, D_FF_2), D_MODEL ** -0.5),
        "w_mlp_out": nrm(ks[14], (DEPTH, D_FF_2, D_MODEL), D_FF_2 ** -0.5),
        "g_final": gain(ks[15], (D_MODEL,)),
    }

def second_block(x, mem, positions, g_mix, w_in, b_gate, sinks, g_mem, w_mem_kv,
              w_proj_swa, w_proj_dsa, w_proj_mem, w_out, g_mlp, w_mlp_in, w_mlp_out,
              g_final):
    B, S, _ = x.shape
    M = mem.shape[1]
    split_points = np.cumsum(IN_SPLITS)[:-1].tolist()
    idx_scale = (N_IDX_HEADS ** -0.5) * (IDX_DIM ** -0.5)
    for l in range(DEPTH):
        h = rmsnorm_2(x, g_mix[l])
        proj = jnp.einsum("bsd,de->bse", h, w_in[l])
        (q_s, k_s, v_s, q_d, k_d, v_d, q_i, k_i, w_i, q_m, gate_logits) = jnp.split(
            proj, split_points, axis=-1)

        q_s = rope(q_s.reshape(B, S, N_SWA_HEADS, HEAD_DIM), positions)
        k_s = rope(k_s.reshape(B, S, N_SWA_KV, HEAD_DIM), positions)
        v_s = v_s.reshape(B, S, N_SWA_KV, HEAD_DIM)
        o_swa = sliding_window_attention(q_s, k_s, v_s, sinks[l])

        q_d = rope(q_d.reshape(B, S, N_DSA_HEADS, HEAD_DIM), positions)
        k_d = rope(k_d[:, :, None, :], positions)[:, :, 0]
        q_i = rope(q_i.reshape(B, S, N_IDX_HEADS, IDX_DIM), positions)
        k_i = rope(k_i[:, :, None, :], positions)[:, :, 0]
        o_dsa = dsa_attention(q_d, k_d, v_d, q_i, k_i, w_i * idx_scale)

        m = rmsnorm_2(mem, g_mem[l])
        mkv = jnp.einsum("bmd,de->bme", m, w_mem_kv[l]).reshape(B, M, 2, N_MEM_HEADS, HEAD_DIM)
        o_mem = memory_cross_attention(q_m.reshape(B, S, N_MEM_HEADS, HEAD_DIM),
                                       mkv[:, :, 0], mkv[:, :, 1])

        gates = jax.nn.sigmoid(gate_logits + b_gate[l]).reshape(B, S, N_BRANCH, D_MODEL)
        merged = (gates[:, :, 0] * jnp.einsum("bse,ed->bsd", o_swa, w_proj_swa[l])
                  + gates[:, :, 1] * jnp.einsum("bse,ed->bsd", o_dsa, w_proj_dsa[l])
                  + gates[:, :, 2] * jnp.einsum("bse,ed->bsd", o_mem, w_proj_mem[l]))
        x = x + jnp.einsum("bsd,de->bse", merged, w_out[l])

        h = rmsnorm_2(x, g_mlp[l])
        hid = jnp.square(jax.nn.relu(jnp.einsum("bsd,df->bsf", h, w_mlp_in[l])))
        x = x + jnp.einsum("bsf,fd->bsd", hid, w_mlp_out[l])
    return rmsnorm_2(x, g_final)


def setup_inputs(seed=0):
    out = dict(first_inputs(seed))
    for name, value in second_inputs(seed + 1).items():
        if name != "x":
            out[name + "_2"] = value
    return out


def reference(
    x, ff1_norm, ff1_w_gate, ff1_w_up, ff1_w_down, mix_norm, w_in, b_gate, gmlp_ln_g, gmlp_ln_b,
    gmlp_w_s, gmlp_b_s, w_branch_a, w_branch_b, w_out, ff2_norm, ff2_w_gate, ff2_w_up,
    ff2_w_down, final_norm, mem_2, positions_2, g_mix_2, w_in_2, b_gate_2, sinks_2, g_mem_2,
    w_mem_kv_2, w_proj_swa_2, w_proj_dsa_2, w_proj_mem_2, w_out_2, g_mlp_2, w_mlp_in_2,
    w_mlp_out_2, g_final_2,
):
    x = first_block(
        x, ff1_norm, ff1_w_gate, ff1_w_up, ff1_w_down, mix_norm, w_in, b_gate, gmlp_ln_g,
        gmlp_ln_b, gmlp_w_s, gmlp_b_s, w_branch_a, w_branch_b, w_out, ff2_norm, ff2_w_gate,
        ff2_w_up, ff2_w_down, final_norm,
    )
    return second_block(
        x, mem_2, positions_2, g_mix_2, w_in_2, b_gate_2, sinks_2, g_mem_2, w_mem_kv_2,
        w_proj_swa_2, w_proj_dsa_2, w_proj_mem_2, w_out_2, g_mlp_2, w_mlp_in_2, w_mlp_out_2,
        g_final_2,
    )


_drawn_inputs = setup_inputs


def setup_inputs(seed=0):
    import zlib

    import numpy as np

    out = dict(_drawn_inputs(seed))
    spreads = {}
    factors = {'b_gate': 4.069,
     'gmlp_ln_g': 3.45,
     'gmlp_ln_b': 3.111,
     'g_mix_2': 4.772,
     'b_gate_2': 28.043,
     'sinks_2': 64.0,
     'g_mem_2': 8.0,
     'g_mlp_2': 8.763,
     'g_final_2': 8.246}
    for name, (base, spread) in spreads.items():
        noise = np.random.default_rng([zlib.crc32(name.encode()), seed]).standard_normal(out[name].shape)
        drawn = base * np.exp(spread * noise) if base else spread * noise
        out[name] = __import__('jax').numpy.asarray(drawn.astype(out[name].dtype))
    for name, factor in factors.items():
        out[name] = (out[name] * factor).astype(out[name].dtype)
    return out
```

```python
from contextlib import ExitStack

import concourse.bass as bass
from concourse import mybir
from concourse.alu_op_type import AluOpType as ALU

ACT = mybir.ActivationFunctionType
AX = mybir.AxisListType
F32 = mybir.dt.float32
FR = mybir.dt.float32r
I32 = mybir.dt.int32

P = 128
BANK = 512
HD = 64
EPS = 1e-6
SCALE = HD ** -0.5
MASKED = -1e30
OUT_OF_REACH = -1e37
TAKEN = -3e38
ROUND = 1.5 * 2.0 ** 23
TWO_PI = (6.28125, 1.9350051879882812e-03, 3.0199159819567e-07)
PI = 3.1415925


CREDIT = ("pv_done", "wT_copied", "o_copied")


class Tally:

    def __init__(self):
        self.steps, self.i, self.per = dict.fromkeys(CREDIT, 1), None, {}

    def now(self, key, add=0):
        per = self.per.get(key, 0)
        return self.i * per + (self.steps.get(key, 0) + add) if per else self.steps.get(key, 0) + add

    def next(self, key, by=1):
        assert self.i is None or key in self.per, key
        self.steps[key] = self.steps.get(key, 0) + by
        return self.now(key)

    def unit(self):
        u = self.next("unit") - 1
        c, per = self.steps["unit"] - 1, self.per.get("unit", 0)
        assert per % 2 == 0
        landed = self.i * (16 * per) + 32 * (c // 2 + 1) if per else 32 * (c // 2 + 1)
        return u, c % 2, landed

    def loop(self, eng, turns, **per):
        return _Loop(self, eng, turns, per)


class _Loop:
    def __init__(self, tally, eng, turns, per):
        self.t, self.turns, self.per = tally, turns, per
        self.ctx = eng.Fori(0, turns)

    def __enter__(self):
        self.t.i, self.t.per = self.ctx.__enter__(), self.per
        self.before = dict(self.t.steps)
        return self.t.i

    def __exit__(self, *a):
        t = self.t
        if a[0] is None:
            made = {k: n - self.before.get(k, 0) for k, n in t.steps.items()}
            assert {k: n for k, n in made.items() if n} == self.per, (made, self.per)
            for k, n in self.per.items():
                t.steps[k] = self.before.get(k, 0) + n * self.turns
        t.i, t.per = None, {}
        return self.ctx.__exit__(*a)


def build(nc, A, out):
    D, S = A["x"].shape[2], A["x"].shape[1]
    KT, TT = D // P, S // P
    M_LEN = A["mem_2"].shape[1]
    PCOLS = 1732
    V_S, K_D, V_D, Q_I, K_I, W_I, Q_M = 640, 1024, 1088, 1152, 1408, 1472, 1476
    KDUP = PCOLS
    TILE_COLS = [0, 128, 256, 384, 768, 896, Q_I, Q_I + 128, Q_M, Q_M + 128] + [KDUP + P * j for j in range(4)]
    QS, QD, QI, QM, KS, KD, KI = 0, 4, 6, 8, 10, 12, 13
    ROWS = [("ff1_norm", 8), ("mix_norm", 8), ("ff2_norm", 8), ("g_mix_2", 8), ("g_mem_2", 8),
            ("g_mlp_2", 8), ("b_gate", 16), ("b_gate_2", 24)]
    COL = {name: sum(r for _, r in ROWS[:j]) for j, (name, _) in enumerate(ROWS)}
    NCOLS = sum(r for _, r in ROWS)
    HALVES_FF2, HALVES_MLP = 70, 138
    OB = [P * b * (b + 1) // 2 for b in range(TT)]

    ctx = ExitStack()
    with ctx:
        def sb(name, shape, dt=F32):
            return ctx.enter_context(nc.sbuf_tensor(name, shape, dt))

        def sem(name):
            return ctx.enter_context(nc.semaphore(name))

        x = sb("resid", [P, TT, D])
        h_hi = sb("h_hi", [P, KT, S], FR)
        h_lo = sb("h_lo", [P, KT, S], FR)
        raw = sb("raw", [P, 2, 4, BANK])
        w_hi = sb("w_hi", [P, 2, 4, BANK], FR)
        w_lo = sb("w_lo", [P, 2, 4, BANK], FR)
        tmp = sb("tmp", [P, 2, 2, BANK])
        ident = sb("ident", [P, P])
        cols = sb("cols", [P, NCOLS])
        wsT = sb("wsT", [P, 4, P])
        swa_mask = wsT[:, 0:2, :].rearrange("p a b -> p (a b)")
        before = wsT[:, 0, :]
        stat = sb("stat", [P, 100])
        pos_i = sb("pos_i", [P, TT], I32)
        memT = sb("memT", [P, 2, M_LEN])
        memv = sb("memv", [P, 2, 4 * HD])
        SS, VAR, REC, ROOT, NEW, R = (stat[:, 4 * j:4 * j + 4] for j in range(6))
        mv = stat[:, 24:32]
        bn = stat[:, 32:56].rearrange("p (g s) -> p g s", g=4)
        mx, neg, tot, snk, snk_e = (stat[:, 56 + 8 * j:64 + 8 * j] for j in range(5))
        rec = stat[:, 24:32]
        w_idx = stat[:, 32:48].rearrange("p (t h) -> p t h", t=TT)

        def layout(gap, *tensors):
            with ExitStack() as c:
                if gap:
                    c.enter_context(nc.sbuf_tensor("gap_" + tensors[0][0], [P, gap], F32))
                return [c.enter_context(nc.sbuf_tensor(n, s, d)) for n, s, d in tensors]

        T16 = KT * S
        hid_hi, hid_lo, rows, mem_tok = layout(
            0, ("hid_hi", [P, 16, S], FR), ("hid_lo", [P, 16, S], FR), ("rows", [P, D], F32),
            ("mem_tok", [P, 2, D], F32))
        qT, kT, v_tok, vg, ya_hi, ya_lo = layout(
            0, ("qT", [P, KT, S], F32), ("kT", [P, KT, S], F32), ("v_tok", [P, TT, D], F32),
            ("vg", [P, KT, TT, P], F32), ("ya_hi", [P, KT, S], FR), ("ya_lo", [P, KT, S], FR))
        ln_g, ln_b, col_rows, ws_raw, bs_row, ones_row = layout(
            4 * T16, ("ln_g", [P, D], F32), ("ln_b", [P, D], F32), ("col_rows", [P, P], F32),
            ("ws_raw", [P, 4, P], F32), ("bs_row", [1, 4 * P], F32), ("ones_row", [1, P], F32))
        beta, keep, wT, pair = layout(
            4 * T16, ("beta", [P, 2, 1280], F32), ("keep", [P, 2, 1284], F32), ("wT", [P, 1280], F32),
            ("pair", [P, 3, S], F32))
        m_hi, m_lo = layout(T16, ("m_hi", [P, KT, S], FR), ("m_lo", [P, KT, S], FR))
        gate_b, = layout(4 * T16, ("gate_b", [P, KT, S], F32))
        merged = vg[:, :, :, :].rearrange("p k n t -> p k (n t)")
        proj, qkT = layout(0, ("proj", [P, TT, PCOLS + 512], F32), ("qkT", [P, 14, S], F32))
        rope_t, trig = layout(4 * T16, ("rope_t", [P, 4, 1280], F32), ("trig", [P, 7, TT * 32], F32))
        logits, pT, oT = layout(
            4 * T16, ("logits", [P, 2048], F32), ("pT", [P, 2048], F32), ("oT", [P, 8, S], F32))
        o_hi, o_lo = layout(4 * T16, ("o_hi", [P, 8, S], FR), ("o_lo", [P, 8, S], FR))
        gates2, merged2 = layout(0, ("gates2", [P, 24, S], F32), ("merged2", [P, KT, S], F32))
        m2_hi, m2_lo = layout(0, ("m2_hi", [P, KT, S], FR), ("m2_lo", [P, KT, S], FR))
        flat = tmp[:, :, :, :].rearrange("p a b c -> p (a b c)")
        ang, turns, r_sin, r_cos, sin_t, cos_t, misc = (trig[:, j, :] for j in range(7))
        freq, pos_f = misc[:, 0:32], misc[:, 32:36]

        ps = ctx.enter_context(nc.psum_tensor("ps", [P, 8, BANK], F32))

        x_in = sem("x_in")
        const_in = sem("const_in")
        rows_in = sem("rows_in")
        raw_ready = [sem("raw_ready0"), sem("raw_ready1")]
        hi_ready = sem("hi_ready")
        lo_ready = sem("lo_ready")
        weights_used = sem("weights_used")
        half_ready = sem("half_ready")
        half_freed = sem("half_freed")
        prod_ready = sem("prod_ready")
        acthi_ready = sem("acthi_ready")
        operand_ready = sem("operand_ready")
        made = sem("made")
        masks_made = sem("masks_made")
        cols_tr = sem("cols_tr")
        cols_ready = sem("cols_ready")
        sq_ready = sem("sq_ready")
        var_ready = sem("var_ready")
        root_ready = sem("root_ready")
        xn_ready = sem("xn_ready")
        xn_used = sem("xn_used")
        out_ready = sem("out_ready")
        dve_step = sem("dve_step")
        vg_copied = sem("vg_copied")
        ln_ready = sem("ln_ready")
        mix_ready = sem("mix_ready")
        mix_copied = sem("mix_copied")
        pair_ready = sem("pair_ready")
        z_ready = sem("z_ready")
        sig_ready = sem("sig_ready")
        masked_ready = sem("masked_ready")
        w_ready = sem("w_ready")
        wT_ready = sem("wT_ready")
        wT_copied = sem("wT_copied")
        pv_done = sem("pv_done")
        o_copied = sem("o_copied")
        trig_ready = sem("trig_ready")
        sin_ready = sem("sin_ready")
        rope_ready = sem("rope_ready")
        tr_ready = sem("tr_ready")
        tr_copied = sem("tr_copied")
        z_freed = sem("z_freed")
        iscore_ready = sem("iscore_ready")
        causal_ready = sem("causal_ready")
        logit_ready = sem("logit_ready")
        exp_ready = sem("exp_ready")
        prob_ready = sem("prob_ready")
        pT_ready = sem("pT_ready")
        pT_copied = sem("pT_copied")
        o_ready = sem("o_ready")
        stored = sem("stored")

        def kpn(name):
            return A[name][0].rearrange("(k p) n -> p k n", p=P)

        JOBS = []
        for b in range(TT):
            JOBS += [("index", b, 4, P * (b + 1))] if b else []
            JOBS += [("window", b, 8, P * min(b + 1, 2)), ("chosen", b, 4, P * (b + 1)), ("memory", b, 4, M_LEN)]
        O_TILE = {"window": 0, "chosen": 4, "memory": 6}

        def place(kind, heads, g):
            return (BANK * g) if kind in ("chosen", "index") else 256 * ((g % 2) * (heads // 2) + g // 2)

        block = ctx.enter_context(nc.Block())

        @block.sync
        def _(sp):
            n = Tally()

            def unit(parts):
                u, slot, _ = n.unit()
                if n.i is not None or u >= 2:
                    sp.wait_ge(lo_ready, u - 1)
                for dst, src in parts(raw[:, slot]):
                    sp.dma_start(dst, src).then_inc(raw_ready[slot], 16)

            def slabs(w, k0, m, c0, width=BANK):
                a = (m + 1) // 2
                unit(lambda r: [(r[:, 0:a, 0:width], w[:, k0:k0 + a, bass.ds(c0, width)]),
                                (r[:, a:m, 0:width], w[:, k0 + a:k0 + m, bass.ds(c0, width)])])

            def gate_up(name, c0):
                gate, up = kpn(name + "_w_gate"), kpn(name + "_w_up")
                for k0 in (0, 4):
                    unit(lambda r: [(r[:, :, 0:256], gate[:, k0:k0 + 4, bass.ds(c0, 256)]),
                                    (r[:, :, 256:512], up[:, k0:k0 + 4, bass.ds(c0, 256)])])

            def groups(name, turns, c0, width=BANK, k0=0, kt=KT):
                w = kpn(name)
                with n.loop(sp, turns, unit=kt // 4) as i:
                    for k in range(k0, k0 + kt, 4):
                        slabs(w, k, 4, i * width + c0, width)

            def ffn(name, first):
                down = kpn(name + "_w_down")
                if first:
                    gate_up(name, 0)
                with n.loop(sp, 8 - first, unit=2) as i:
                    gate_up(name, i * 256 + 256 * first)
                groups(name + "_w_down", 2, 0, kt=16)
                with n.loop(sp, 3, unit=2) as i:
                    gate_up(name, i * 256 + 2048)
                with n.loop(sp, 2, unit=2) as i:
                    for k0 in (16, 19):
                        slabs(down, k0, 3, i * BANK)

            for t in range(TT):
                sp.dma_start(x[:, t, :], A["x"][0, t * P:(t + 1) * P, :]).then_inc(x_in, 16)
            ffn("ff1", 1)
            groups("w_in", 2, 1024)
            groups("w_in", 4, 2048)
            groups("w_in", 2, 4096)
            groups("w_in", 2, 0)
            groups("w_in", 2, 5120)
            groups("w_branch_a", 2, 0)
            groups("w_in", 2, 6144)
            groups("w_branch_b", 2, 0)
            groups("w_out", 2, 0)
            ffn("ff2", 0)
            for k0 in (0, 4):
                slabs(kpn("w_mem_kv_2"), k0, 4, 0)
            groups("w_in_2", 2, 0)
            groups("w_in_2", 2, 1024, 354)
            groups("w_in_2", 6, PCOLS)
            for c0 in (0, BANK):
                slabs(kpn("w_proj_swa_2"), 0, 4, c0)
                slabs(kpn("w_proj_dsa_2"), 0, 2, c0)
                slabs(kpn("w_proj_mem_2"), 0, 2, c0)
            groups("w_out_2", 2, 0)
            for c in range(2):
                groups("w_mlp_in_2", 4, c * 2048)
                groups("w_mlp_out_2", 2, 0, k0=16 * c, kt=16)
            for t in range(TT):
                sp.wait_ge(out_ready, TT + t + 1)
                sp.dma_start(out[0, t * P:(t + 1) * P, :], x[:, t, :]).then_inc(stored, 16)
            sp.wait_ge(stored, 16 * TT)

        @block.gpsimd
        def _(pool):
            n = Tally()
            row = 0
            for name, r in ROWS:
                pool.dma_start(col_rows[row:row + r, :], A[name][0].rearrange("(r p) -> r p", p=P)).then_inc(const_in, 16)
                row += r
            pool.dma_start(ws_raw[:], A["gmlp_w_s"][0].rearrange("g t s -> t g s")).then_inc(const_in, 16)
            pool.dma_start(bs_row[:], A["gmlp_b_s"].rearrange("a g t -> a (g t)")).then_inc(const_in, 16)
            pool.dma_start(ln_g[:], A["gmlp_ln_g"][0].rearrange("g c -> (g c)").partition_broadcast(P)).then_inc(const_in, 16)
            pool.dma_start(ln_b[:], A["gmlp_ln_b"][0].rearrange("g c -> (g c)").partition_broadcast(P)).then_inc(const_in, 16)
            for e in range(2):
                pool.dma_start(snk[:, 4 * e:4 * e + 4],
                               A["sinks_2"][0].rearrange("(a e) -> e a", e=2)[e].partition_broadcast(P),
                               allow_slow_non_contiguous=True).then_inc(const_in, 16)
            pool.dma_start(pos_i[:], A["positions_2"][0].rearrange("(t p) -> p t", p=P),
                           allow_slow_non_contiguous=True).then_inc(const_in, 16)
            pool.memset(ident[:], 0.0).then_inc(made, 1)
            pool.memset(ones_row[:], 1.0).then_inc(made, 1)
            pool.wait_ge(made, n.next("made", 2))
            pool.affine_select(out=ident[:], in_=ident[:], compare_op=ALU.not_equal, fill=1.0, base=0,
                               pattern=[[-1, P]], channel_multiplier=1).then_inc(made, 1)

            n.next("half_freed", 30 + 28)
            pool.wait_ge(half_freed, n.now("half_freed"))
            pool.memset(before, 1.0).then_inc(made, 1)
            pool.wait_ge(made, 4)
            pool.affine_select(out=before, in_=before, compare_op=ALU.is_gt, fill=0.0, base=0,
                               pattern=[[-1, P]], channel_multiplier=1).then_inc(made, 1)
            pool.wait_ge(made, 5)
            with n.loop(pool, KT, pv_done=2, sig_ready=8) as i:
                pool.wait_ge(pv_done, n.now("pv_done"))
                pool.tensor_copy(pair[:, 0, :], qT[:, bass.ds(i, 1), :]).then_inc(pair_ready, 1)
                pool.tensor_copy(pair[:, 1, :], kT[:, bass.ds(i, 1), :]).then_inc(pair_ready, 1)
                pool.tensor_copy(pair[:, 2, :].rearrange("p (t c) -> p t c", t=TT),
                                 v_tok[:, :, bass.ds(i * P, P)]).then_inc(pair_ready, 1)
                for hh in range(2):
                    for b in range(TT):
                        pool.wait_ge(sig_ready, n.next("sig_ready"))
                        w = beta[:, hh, OB[b] + P * b:OB[b] + P * b + P]
                        k = keep[:, hh, OB[b] + b + P * b:OB[b] + b + P * b + P]
                        pool.tensor_tensor(w, w, before, ALU.mult).then_inc(masked_ready, 1)
                        pool.affine_select(out=k, in_=k, compare_op=ALU.is_gt, fill=1.0, base=0,
                                           pattern=[[-1, P]], channel_multiplier=1).then_inc(masked_ready, 1)
                n.next("pv_done", 2)

            pool.wait_ge(half_freed, HALVES_FF2)
            pool.dma_start(rows[:], A["final_norm"].partition_broadcast(P)).then_inc(rows_in, 16)
            pool.dma_start(mem_tok[:], A["mem_2"][0].rearrange("(t p) d -> p t d", p=P)).then_inc(rows_in, 16)
            pool.dma_start(freq, A["inv_freq"].partition_broadcast(P)).then_inc(rows_in, 16)
            pool.memset(swa_mask, 0.0).then_inc(masks_made, 1)
            pool.wait_ge(masks_made, 1)
            pool.affine_select(out=swa_mask, in_=swa_mask, compare_op=ALU.is_ge, fill=MASKED, base=P,
                               pattern=[[-1, 2 * P]], channel_multiplier=1).then_inc(masks_made, 1)
            pool.wait_ge(masks_made, 2)
            pool.affine_select(out=swa_mask, in_=swa_mask, compare_op=ALU.is_gt, fill=MASKED, base=0,
                               pattern=[[1, 2 * P]], channel_multiplier=-1).then_inc(masks_made, 1)
            pool.wait_ge(rope_ready, 1)
            pool.memset(flat[:, 0:P], 0.0).then_inc(masks_made, 1)
            pool.wait_ge(masks_made, 4)
            pool.affine_select(out=flat[:, 0:P], in_=flat[:, 0:P], compare_op=ALU.is_ge, fill=MASKED, base=0,
                               pattern=[[-1, P]], channel_multiplier=1).then_inc(causal_ready, 1)
            for b in range(1, TT):
                pool.wait_ge(iscore_ready, n.next("iscore_ready"))
                diag = flat[:, P * b:P * b + P]
                pool.affine_select(out=diag, in_=diag, compare_op=ALU.is_ge, fill=OUT_OF_REACH, base=0,
                                   pattern=[[-1, P]], channel_multiplier=1).then_inc(causal_ready, 1)
            pool.wait_ge(half_freed, HALVES_MLP)
            pool.dma_start(rows[:], A["g_final_2"].partition_broadcast(P)).then_inc(rows_in, 16)

        @block.tensor
        def _(pe):
            n = Tally()

            def three(out_, w, a, weights_first, first, last):
                (wh, wl), (ah, al) = w, a
                for j, (p, q) in enumerate(((wh, ah), (wh, al), (wl, ah))):
                    lhs, rhs = (p, q) if weights_first else (q, p)
                    mm = pe.matmul(out_, lhs, rhs, start=first and j == 0, stop=last and j == 2)
                return mm

            def group(act, units, weights_first, width=BANK, first_group=False, operands=()):
                k, kt = 0, sum(units)
                for j, m in enumerate(units):
                    u, slot, _ = n.unit()
                    pe.wait_ge(lo_ready, u + 1)
                    if operands:
                        pe.wait_ge(operand_ready, operands[j])
                    for s in range(m):
                        for b in range(4):
                            if k == 0 and b in (0, 2) and not first_group:
                                pe.wait_ge(half_freed, n.now("half_freed", -1 if b == 0 else 0))
                            wc = slice(b * P, (b + 1) * P) if weights_first else slice(0, width)
                            ac = slice(0, S) if weights_first else slice(b * P, (b + 1) * P)
                            mm = three(ps[:, b, 0:S if weights_first else width],
                                       (w_hi[:, slot, s, wc], w_lo[:, slot, s, wc]),
                                       (act[0][:, k, ac], act[1][:, k, ac]), weights_first, k == 0, k == kt - 1)
                            if k == kt - 1 and b in (1, 3):
                                mm.then_inc(half_ready, 1)
                        k += 1
                    if j < len(units) - 1:
                        mm.then_inc(weights_used, 1)
                n.next("half_freed", 2)

            def groups(turns, act, units, weights_first, width=BANK, new=()):
                operands = fresh(*new)
                with n.loop(pe, turns, unit=len(units), half_freed=2):
                    group(act, units, weights_first, width, operands=operands)

            def fresh(*new):
                before = n.now("operand_ready")
                if new:
                    n.next("operand_ready", new[-1])
                return [before + k for k in new]

            def norm_transposes(tiles):
                for t in range(tiles):
                    pe.wait_ge(xn_ready, n.next("xn_ready"))
                    for k in range(KT):
                        tr = pe.transpose(ps[:, k, t * P:(t + 1) * P],
                                          tmp[:, t % 2, k // 4, (k % 4) * P:(k % 4 + 1) * P], ident[:])
                    tr.then_inc(xn_used, 1)

            h = (h_hi, h_lo)
            hid = (hid_hi, hid_lo)

            def ffn(first):
                norm_transposes(TT)
                if first:
                    group(h, (4, 4), True, first_group=True, operands=fresh(4, 8))
                    groups(7, h, (4, 4), True)
                else:
                    groups(8, h, (4, 4), True, new=(4, 8))
                groups(2, hid, (4, 4, 4, 4), False, new=(2, 4, 6, 8))
                groups(3, h, (4, 4), True)
                groups(2, hid, (3, 3), False, new=(2, 3))

            pe.wait_ge(made, 3)
            pe.wait_ge(const_in, 16 * (len(ROWS) + 7))
            pe.transpose(ps[:, 4, 0:NCOLS], col_rows[0:NCOLS, :], ident[0:NCOLS, 0:NCOLS]).then_inc(pv_done, 1)
            for g in range(4):
                tr = pe.transpose(ps[:, 5, g * P:(g + 1) * P], ws_raw[:, g, :], ident[:])
            tr.then_inc(cols_tr, 1)
            pe.wait_ge(cols_ready, 2)

            ffn(True)

            norm_transposes(TT)
            groups(2, h, (4, 4), False, new=(4, 8))
            groups(4, h, (4, 4), True)
            groups(2, h, (4, 4), False)
            pe.wait_ge(ln_ready, TT)
            for j in range(KT):
                if j >= 4:
                    pe.wait_ge(mix_copied, j - 3)
                for t in range(TT):
                    o = ps[:, 4 + j % 4, t * P:(t + 1) * P]
                    pe.matmul(o, vg[:, j, t, :], wsT[:, j // 2, :], start=True, stop=False)
                    mm = pe.matmul(o, ones_row[0:1, :], bs_row[0:1, (j // 2) * P:(j // 2 + 1) * P],
                                   start=False, stop=True)
                mm.then_inc(mix_ready, 1)
            groups(2, h, (4, 4), True)
            groups(2, h, (4, 4), True)
            groups(2, (ya_hi, ya_lo), (4, 4), True, new=(2, 4))

            pe.wait_ge(half_freed, n.now("half_freed"))
            with n.loop(pe, KT, pair_ready=3, sig_ready=8, w_ready=8, wT_copied=2, o_copied=1):
                pe.wait_ge(pair_ready, n.next("pair_ready", 3))
                for hh in range(2):
                    half = slice(HD * hh, HD * hh + HD)
                    for b in range(TT):
                        if hh:
                            pe.wait_ge(sig_ready, n.next("sig_ready"))
                        pe.matmul(ps[:, 4 + b, 0:P * (b + 1)], pair[half, 0, b * P:(b + 1) * P],
                                  pair[half, 1, 0:P * (b + 1)], start=True, stop=True).then_inc(z_ready, 1)
                n.next("sig_ready", 4)
                for hh in range(2):
                    pe.wait_ge(wT_copied, n.now("wT_copied"))
                    for b in range(TT):
                        pe.wait_ge(w_ready, n.next("w_ready"))
                        for s in range(b + 1):
                            bank, col = ((0, b), (1, b - 1), (2, b - 2), (2, 2))[s]
                            tr = pe.transpose(ps[:, bank, col * P:(col + 1) * P],
                                              beta[:, hh, OB[b] + s * P:OB[b] + (s + 1) * P], ident[:])
                    tr.then_inc(wT_ready, 1)
                    pe.wait_ge(wT_copied, n.next("wT_copied"))
                    if hh == 0:
                        pe.wait_ge(o_copied, n.now("o_copied"))
                    for s, at in enumerate((0, 512, 896, 1152)):
                        mm = pe.matmul(ps[HD * hh:HD * hh + HD, 3, s * P:S],
                                       pair[:, 2, s * P + HD * hh:s * P + HD * hh + HD],
                                       wT[:, at:at + S - s * P], start=s == 0, stop=s == TT - 1,
                                       skip_group_check=True)
                    mm.then_inc(pv_done, 1)
                n.next("o_copied")
            pe.wait_ge(o_copied, n.now("o_copied"))

            groups(2, h, (4, 4), True)
            groups(2, h, (4, 4), True, new=(1, 2))
            groups(2, (m_hi, m_lo), (4, 4), False, new=(2, 4))

            ffn(False)

            norm_transposes(M_LEN // P)
            operands = fresh(4, 8)
            for j in range(2):
                u, slot, _ = n.unit()
                pe.wait_ge(lo_ready, u + 1)
                pe.wait_ge(operand_ready, operands[j])
                for s in range(4):
                    k = 4 * j + s
                    for b in range(4):
                        if k == 0 and b in (0, 2):
                            pe.wait_ge(half_freed, n.now("half_freed", -1 if b == 0 else 0))
                        keys = b < 2
                        wc = slice(b * P, (b + 1) * P) if keys else slice(256, 512)
                        ac = slice(0, M_LEN) if keys else slice((b - 2) * P, (b - 1) * P)
                        mm = three(ps[:, b, 0:256], (w_hi[:, slot, s, wc], w_lo[:, slot, s, wc]),
                                   (h_hi[:, k, ac], h_lo[:, k, ac]), keys, k == 0, k == KT - 1)
                        if k == KT - 1 and b in (1, 3):
                            mm.then_inc(half_ready, 1)
                if j == 0:
                    mm.then_inc(weights_used, 1)
            n.next("half_freed", 2)

            norm_transposes(TT)
            groups(2, h, (4, 4), False, new=(4, 8))
            groups(2, h, (4, 4), False, 354)

            pe.wait_ge(rope_ready, 1)
            pe.wait_ge(half_freed, n.now("half_freed"))
            for j, c in enumerate(TILE_COLS):
                if j >= 8:
                    pe.wait_ge(tr_copied, j - 7)
                for t in range(TT):
                    tr = pe.transpose(ps[:, j % 8, t * P:(t + 1) * P], proj[:, t, c:c + P], ident[:])
                tr.then_inc(tr_ready, 1)
            pe.wait_ge(tr_copied, len(TILE_COLS))

            def scores(j):
                kind, b, heads, nk = JOBS[j]
                if j:
                    pe.wait_ge(z_freed, j)
                for g in range(heads):
                    half = slice(HD * (g % 2), HD * (g % 2) + HD)
                    q0 = {"window": QS, "chosen": QD, "index": QI, "memory": QM}[kind] + g // 2
                    q = qkT[half, q0, b * P:(b + 1) * P]
                    if kind == "window":
                        k = qkT[half, KS + g // 4, (b + 1) * P - nk:(b + 1) * P]
                    elif kind == "memory":
                        k = memT[half, g // 2, :]
                    else:
                        k = qkT[half, KI if kind == "index" else KD, 0:nk]
                    at = place(kind, heads, g)
                    o = ps[:, 4 + at // BANK, at % BANK:at % BANK + nk]
                    mm = pe.matmul(o, q, k, start=True, stop=True)
                mm.then_inc(z_ready, 1)

            def values(j):
                kind, b, heads, nk = JOBS[j]
                pe.wait_ge(prob_ready, n.next("prob_ready"))
                pe.wait_ge(o_copied, n.now("o_copied"))
                for g in range(heads):
                    at = place(kind, heads, g)
                    for kb in range(nk // P):
                        bank = kb * 2 + g // 4 if kind == "window" else kb
                        tr = pe.transpose(ps[:, bank, (g % 4) * P:(g % 4 + 1) * P],
                                          logits[:, at + kb * P:at + (kb + 1) * P], ident[:])
                tr.then_inc(pT_ready, 1)
                pe.wait_ge(pT_copied, n.next("pT_copied"))
                for g in range({"window": 2, "chosen": 1, "memory": 4}[kind]):
                    for kb in range(nk // P):
                        if kind == "window":
                            v = proj[:, b + 1 - nk // P + kb, V_S + HD * g:V_S + HD * g + HD]
                            o, w = ps[0:HD, g, :], pT[:, (kb * 2 + g) * BANK:(kb * 2 + g + 1) * BANK]
                        elif kind == "chosen":
                            v = proj[:, kb, V_D:V_D + HD]
                            o, w = ps[0:HD, 0, :], pT[:, kb * BANK:(kb + 1) * BANK]
                        else:
                            v = memv[:, kb, HD * g:HD * g + HD]
                            o, w = ps[0:HD, 0, g * P:(g + 1) * P], pT[:, kb * BANK + g * P:kb * BANK + (g + 1) * P]
                        mm = pe.matmul(o, v, w, start=kb == 0, stop=kb == nk // P - 1)
                mm.then_inc(o_ready, 1)
                n.next("o_copied")

            scores(0)
            for j, job in enumerate(JOBS):
                if j + 1 < len(JOBS):
                    scores(j + 1)
                if job[0] != "index":
                    values(j)
            pe.wait_ge(o_copied, n.now("o_copied"))

            groups(6, h, (4, 4), True)
            swa, rest = fresh(1, 2)
            for _ in range(2):
                group((o_hi[:, 0:4, :], o_lo[:, 0:4, :]), (4,), True, operands=[swa])
                group((o_hi[:, 4:6, :], o_lo[:, 4:6, :]), (2,), True, operands=[rest])
                group((o_hi[:, 6:8, :], o_lo[:, 6:8, :]), (2,), True)
            groups(2, (m2_hi, m2_lo), (4, 4), False, new=(2, 4))
            norm_transposes(TT)
            for c in range(2):
                groups(4, h, (4, 4), True, new=() if c else (4, 8))
                groups(2, hid, (4, 4, 4, 4), False, new=(2, 4, 6, 8))

        @block.scalar
        def _(act):
            n = Tally()

            def split(units):
                for j in range(units):
                    _, slot, landed = n.unit()
                    if j:
                        act.wait_ge(weights_used, n.next("weights_used"))
                    elif n.i is not None or n.now("half_ready"):
                        act.wait_ge(half_ready, n.now("half_ready"))
                    act.wait_ge(raw_ready[slot], landed)
                    act.activation(w_hi[:, slot], raw[:, slot], ACT.Copy).then_inc(hi_ready, 1)

            def complete():
                act.wait_ge(half_ready, n.next("half_ready"))

            def passed(halves=2):
                n.next("half_ready", halves)
                n.next("half_freed", halves)

            def dve_groups(turns, units):
                with n.loop(act, turns, unit=units, weights_used=units - 1, half_ready=2, half_freed=2):
                    split(units)
                    passed()

            def copy_groups(turns, dst):
                with n.loop(act, turns, unit=2, weights_used=1, half_ready=2, half_freed=2) as i:
                    split(2)
                    for hf in range(2):
                        complete()
                        to = dst(i, hf)
                        act.activation(to, ps[:, 2 * hf:2 * hf + 2, 0:to.shape[2]], ACT.Copy).then_inc(half_freed, 1)
                        n.next("half_freed")

            def high(dst, src):
                act.wait_ge(prod_ready, n.next("prod_ready"))
                act.activation(dst, src, ACT.Copy).then_inc(acthi_ready, 1)

            def root():
                act.wait_ge(var_ready, n.next("var_ready"))
                act.activation(ROOT, REC, ACT.Sqrt).then_inc(root_ready, 1)

            def squares(src):
                act.activation(stat[:, 96:97], ident[:, 0:1], ACT.Sqrt)
                if n.now("half_freed"):
                    act.wait_ge(half_freed, n.now("half_freed", -1))
                for t in range(2):
                    act.activation(ps[:, 4 + 2 * t:6 + 2 * t, :],
                                   src[:, t, :].rearrange("p (a b) -> p a b", a=2), ACT.Square,
                                   accum_out=SS[:, t:t + 1]).then_inc(sq_ready, 1)
                root()

            def norm(src, tiles, gain):
                squares(src)
                act.wait_ge(xn_used, n.next("xn_used", tiles))
                for k in range(KT):
                    act.activation(h_hi[:, k, 0:tiles * P], ps[:, k, 0:tiles * P], ACT.Copy,
                                   scale=cols[:, gain + k:gain + k + 1]).then_inc(acthi_ready, 1)

            def gate_groups(turns, dst, bias, tile0=0):
                with n.loop(act, turns, unit=2, weights_used=1, half_ready=2, half_freed=2) as i:
                    split(2)
                    for b in range(4):
                        if b % 2 == 0:
                            complete()
                        a = act.activation(dst[:, bass.ds(i * 4 + (b + tile0), 1), :], ps[:, b:b + 1, :], ACT.Sigmoid,
                                           bias=cols[:, bass.ds(i * 4 + (b + bias), 1)])
                        if b % 2:
                            a.then_inc(half_freed, 1)
                            n.next("half_freed")

            def gate_up(i, tile0):
                split(2)
                complete()
                act.activation(tmp[:, 0], ps[:, 0:2, :], ACT.Silu).then_inc(half_freed, 1)
                n.next("half_ready")
                act.wait_ge(half_freed, n.next("half_freed", 2))
                act.activation(hid_hi[:, bass.ds(i * 2 + tile0, 2), :], tmp[:, 1], ACT.Copy).then_inc(acthi_ready, 1)

            def gates_up(turns, tile0):
                with n.loop(act, turns, unit=2, weights_used=1, half_ready=2, half_freed=2) as i:
                    gate_up(i, tile0)

            def ffn(gain, first=0):
                norm(x, TT, gain)
                if first:
                    gate_up(0, 0)
                gates_up(8 - first, 2 * first)
                dve_groups(2, 4)
                gates_up(3, 0)
                dve_groups(2, 2)

            act.wait_ge(raw_ready[0], n.unit()[2])
            act.activation(w_hi[:, 0], raw[:, 0], ACT.Copy).then_inc(hi_ready, 1)
            act.wait_ge(x_in, 16 * TT)
            act.wait_ge(cols_ready, 2)
            ffn(COL["ff1_norm"], 1)

            norm(x, TT, COL["mix_norm"])
            with n.loop(act, 2, unit=2, weights_used=1, half_ready=2, half_freed=2) as i:
                split(2)
                for t in range(TT):
                    if t % 2 == 0:
                        complete()
                    a = act.activation(vg[:, bass.ds(i * 4, 4), t, :],
                                       ps[:, t, :].rearrange("p (c k) -> p c k", c=4), ACT.Gelu)
                    if t % 2:
                        a.then_inc(half_freed, 1)
                        n.next("half_freed")
            for dst in (qT, kT):
                with n.loop(act, 2, unit=2, weights_used=1, half_ready=2, half_freed=2, var_ready=1) as i:
                    split(2)
                    root()
                    for hf in range(2):
                        complete()
                        act.activation(dst[:, bass.ds(i * 4 + 2 * hf, 2), :], ps[:, 2 * hf:2 * hf + 2, :],
                                       ACT.Copy).then_inc(half_freed, 1)
                        n.next("half_freed")
            copy_groups(2, lambda i, hf: v_tok[:, 2 * hf:2 * hf + 2, bass.ds(i * BANK, BANK)])
            for j in range(KT):
                act.wait_ge(mix_ready, j + 1)
                act.activation(vg[:, j].rearrange("p n t -> p (n t)"), ps[:, 4 + j % 4, :], ACT.Copy).then_inc(mix_copied, 1)
            with n.loop(act, 2, unit=2, weights_used=1, half_ready=2, half_freed=2, prod_ready=2) as i:
                split(2)
                for hf in range(2):
                    complete()
                    act.activation(tmp[:, 0], ps[:, 2 * hf:2 * hf + 2, :], ACT.Gelu).then_inc(half_freed, 1)
                    n.next("half_freed")
                    high(ya_hi[:, bass.ds(i * 4 + 2 * hf, 2), :], tmp[:, 1])
            act.wait_ge(operand_ready, 8 + 11 + 8 + 4)
            gate_groups(2, merged, COL["b_gate"])
            dve_groups(2, 2)

            with n.loop(act, KT, z_ready=8, wT_ready=2, pv_done=2):
                for hh in range(2):
                    for b in range(TT):
                        nk = P * (b + 1)
                        act.wait_ge(z_ready, n.next("z_ready"))
                        act.activation(beta[:, hh, OB[b]:OB[b] + nk], ps[:, 4 + b, 0:nk], ACT.Sigmoid, scale=SCALE)
                        act.activation(keep[:, hh, OB[b] + b:OB[b] + b + nk], ps[:, 4 + b, 0:nk], ACT.Sigmoid,
                                       scale=-SCALE).then_inc(sig_ready, 1)
                for hh in range(2):
                    act.wait_ge(wT_ready, n.next("wT_ready"))
                    act.wait_ge(pv_done, n.now("pv_done"))
                    n.next("pv_done")
                    act.activation(wT[:, 0:512], ps[:, 0, :], ACT.Copy)
                    act.activation(wT[:, 512:1280].rearrange("p (a b) -> p a b", a=2), ps[:, 1:3, 0:384],
                                   ACT.Copy).then_inc(wT_copied, 1)

            gate_groups(2, gate_b, COL["b_gate"] + 8)
            act.wait_ge(o_copied, 1 + KT)
            for j in range(2):
                act.activation(h_hi[:, 4 * j:4 * j + 4, :], qT[:, 4 * j:4 * j + 4, :], ACT.Copy).then_inc(acthi_ready, 1)
            with n.loop(act, 2, unit=2, weights_used=1, half_ready=2, half_freed=2, prod_ready=2) as i:
                split(2)
                for hf in range(2):
                    passed(1)
                    high(m_hi[:, bass.ds(i * 4 + 2 * hf, 2), :], merged[:, bass.ds(i * 4 + 2 * hf, 2), :])
            dve_groups(2, 2)
            ffn(COL["ff2_norm"])

            squares(x)
            act.wait_ge(rows_in, 48)
            act.wait_ge(out_ready, TT)
            norm(mem_tok, M_LEN // P, COL["g_mem_2"])
            split(2)
            complete()
            act.activation(memT[:], ps[:, 0:2, 0:256], ACT.Copy).then_inc(half_freed, 1)
            complete()
            act.activation(memv[:], ps[:, 2:4, 0:256], ACT.Copy).then_inc(half_freed, 1)
            n.next("half_freed", 2)
            norm(x, TT, COL["g_mix_2"])
            copy_groups(2, lambda i, hf: proj[:, 2 * hf:2 * hf + 2, bass.ds(i * BANK, BANK)])
            copy_groups(2, lambda i, hf: proj[:, 2 * hf:2 * hf + 2, bass.ds(i * 354 + 1024, 354)])

            act.wait_ge(trig_ready, 1)
            act.activation(sin_t, r_sin, ACT.Sin)
            act.activation(cos_t, r_cos, ACT.Sin).then_inc(sin_ready, 1)
            for j in range(len(TILE_COLS)):
                act.wait_ge(tr_ready, j + 1)
                act.activation(qkT[:, j, :], ps[:, j % 8, :], ACT.Copy).then_inc(tr_copied, 1)

            z0 = n.now("z_ready")
            for j, (kind, b, heads, nk) in enumerate(JOBS):
                if kind == "index":
                    act.wait_ge(z_ready, z0 + j + 1)
                    act.wait_ge(prob_ready, n.now("prob_ready"))
                    act.activation(flat.rearrange("p (h s) -> p h s", h=4)[:, :, 0:nk], ps[:, 4:8, 0:nk],
                                   ACT.Relu).then_inc(z_freed, 1)
                    continue
                row = BANK if kind == "chosen" else 256
                act.wait_ge(logit_ready, n.next("logit_ready"))
                for g in range(heads):
                    e = act.activation(logits[:, g * row:g * row + nk], logits[:, g * row:g * row + nk], ACT.Exp,
                                       bias=neg[:, g:g + 1], accum_out=tot[:, g:g + 1])
                if kind == "window":
                    e = act.activation(snk_e, snk_e, ACT.Exp)
                e.then_inc(exp_ready, 1)
                n.next("prob_ready")
                act.wait_ge(pT_ready, n.next("pT_ready"))
                banks = (nk // P) * (2 if kind == "window" else 1)
                act.activation(pT[:, 0:banks * BANK].rearrange("p (a b) -> p a b", b=BANK), ps[:, 0:banks, :],
                               ACT.Copy).then_inc(pT_copied, 1)

            act.wait_ge(o_copied, 1 + KT + 12)
            for j in range(2):
                act.activation(o_hi[:, 4 * j:4 * j + 4, :], oT[:, 4 * j:4 * j + 4, :], ACT.Copy).then_inc(acthi_ready, 1)
            gate_groups(6, gates2, COL["b_gate_2"])
            for c in range(2):
                for kind in range(3):
                    split(1)
                    for hf in range(2):
                        passed(1)
                        if kind == 2:
                            t = slice(4 * c + 2 * hf, 4 * c + 2 * hf + 2)
                            high(m2_hi[:, t, :], merged2[:, t, :])
            dve_groups(2, 2)
            norm(x, TT, COL["g_mlp_2"])
            for c in range(2):
                with n.loop(act, 4, unit=2, weights_used=1, half_ready=2, half_freed=2, prod_ready=2) as i:
                    split(2)
                    for hf in range(2):
                        complete()
                        act.activation(tmp[:, 0], ps[:, 2 * hf:2 * hf + 2, :], ACT.Relu).then_inc(half_freed, 1)
                        n.next("half_freed")
                        high(hid_hi[:, bass.ds(i * 4 + 2 * hf, 2), :], tmp[:, 1])
                if c == 0:
                    dve_groups(2, 4)
                else:
                    split(4)
                    passed()
                    split(3)
                    passed()
            squares(x)

        @block.vector
        def _(dve):
            n = Tally()

            def step(ins):
                ins.then_inc(dve_step, 1)
                dve.wait_ge(dve_step, n.next("dve_step"))

            def split(units):
                for _ in range(units):
                    _, slot, _ = n.unit()
                    dve.wait_ge(hi_ready, n.next("hi_ready"))
                    dve.tensor_tensor(w_lo[:, slot], raw[:, slot], w_hi[:, slot].bitcast(F32),
                                      ALU.subtract).then_inc(lo_ready, 1)

            def complete():
                dve.wait_ge(half_ready, n.next("half_ready"))

            def freed(ins):
                ins.then_inc(half_freed, 1)
                n.next("half_freed")

            def low(dst, src, hi):
                dve.wait_ge(acthi_ready, n.next("acthi_ready"))
                dve.tensor_tensor(dst, src, hi.bitcast(F32), ALU.subtract).then_inc(operand_ready, 1)
                n.next("operand_ready")

            def act_groups(turns):
                with n.loop(dve, turns, unit=2, hi_ready=2, half_ready=2, half_freed=2):
                    split(2)
                    n.next("half_ready", 2)
                    n.next("half_freed", 2)

            def rsqrt(w, src, scale):
                V, C, Q, N_, O = (a[:, 0:w] for a in (VAR, REC, ROOT, NEW, R))
                step(dve.tensor_scalar(V, src, scale, EPS, ALU.mult, ALU.add))
                dve.reciprocal(C, V).then_inc(var_ready, 1)
                dve.wait_ge(root_ready, n.next("root_ready"))
                step(dve.tensor_tensor(N_, Q, Q, ALU.mult))
                step(dve.tensor_tensor(N_, N_, V, ALU.mult))
                step(dve.tensor_scalar(N_, N_, -0.5, 1.5, ALU.mult, ALU.add))
                step(dve.tensor_tensor(O, Q, N_, ALU.mult))

            def squares(src, tiles):
                if tiles > 2 and n.now("half_freed"):
                    dve.wait_ge(half_freed, n.now("half_freed"))
                for t in range(2, tiles):
                    ins = dve.tensor_tensor_reduce(ps[:, 2 * t - 4:2 * t - 2, :].rearrange("p a b -> p (a b)"),
                                                   src[:, t, :], src[:, t, :], 1.0, 0.0, ALU.mult, ALU.add,
                                                   SS[:, t:t + 1])
                if tiles > 2:
                    step(ins)
                dve.wait_ge(sq_ready, n.next("sq_ready", 2))
                rsqrt(4, SS, 1.0 / D)

            def norm(src, tiles, gain):
                squares(src, tiles)
                for t in range(tiles):
                    if t >= 2:
                        dve.wait_ge(xn_used, n.now("xn_used", t - 1))
                    dve.tensor_scalar(tmp[:, t % 2].rearrange("p a b -> p (a b)"), src[:, t, :], R[:, t:t + 1],
                                      None, ALU.mult).then_inc(xn_ready, 1)
                n.next("xn_used", tiles)
                for k in range(KT):
                    dve.wait_ge(acthi_ready, n.next("acthi_ready"))
                    dve.scalar_tensor_tensor(out=h_lo[:, k, 0:tiles * P], in0=ps[:, k, 0:tiles * P],
                                             scalar=cols[:, gain + k:gain + k + 1],
                                             in1=h_hi[:, k, 0:tiles * P].bitcast(F32), op0=ALU.mult,
                                             op1=ALU.subtract).then_inc(operand_ready, 1)
                    n.next("operand_ready")

            def last_norm(rows_at):
                squares(x, TT)
                dve.wait_ge(rows_in, rows_at)
                for t in range(TT):
                    dve.scalar_tensor_tensor(out=x[:, t, :], in0=x[:, t, :], scalar=R[:, t:t + 1], in1=rows[:],
                                             op0=ALU.mult, op1=ALU.mult).then_inc(out_ready, 1)

            def gate_up(turns):
                with n.loop(dve, turns, unit=2, hi_ready=2, half_ready=2, half_freed=2, acthi_ready=1, operand_ready=1) as i:
                    split(2)
                    dve.wait_ge(half_freed, n.next("half_freed"))
                    n.next("half_ready")
                    complete()
                    freed(dve.tensor_tensor(tmp[:, 1], tmp[:, 0], ps[:, 2:4, :], ALU.mult))
                    low(hid_lo[:, bass.ds(i * 2, 2), :], tmp[:, 1], hid_hi[:, bass.ds(i * 2, 2), :])

            def residual(turns, units, scale):
                with n.loop(dve, turns, unit=units, hi_ready=units, half_ready=2, half_freed=2) as i:
                    split(units)
                    add(i, scale)

            def add(i, scale):
                for hf in range(2):
                    complete()
                    to = x[:, 2 * hf:2 * hf + 2, bass.ds(i * BANK, BANK)]
                    freed(dve.scalar_tensor_tensor(out=to, in0=ps[:, 2 * hf:2 * hf + 2, :], scalar=scale, in1=to,
                                                   op0=ALU.mult, op1=ALU.add))

            def ffn(gain):
                norm(x, TT, gain)
                gate_up(8)
                residual(2, 4, 0.5)
                gate_up(3)
                residual(2, 2, 0.5)

            dve.wait_ge(cols_tr, 1)
            dve.tensor_copy(cols[:], ps[:, 4, 0:NCOLS]).then_inc(cols_ready, 1)
            wsrc = ps[:, 5, :].rearrange("p (g t) -> p g t", g=4)
            dve.tensor_copy(wsT[0:64], wsrc[0:64]).then_inc(wT_copied, 1)
            dve.memset(wsT[64:128, :, 0:64], 0.0).then_inc(o_copied, 1)
            dve.tensor_copy(wsT[64:128, :, 64:128], wsrc[64:128, :, 64:128]).then_inc(cols_ready, 1)
            split(1)
            dve.wait_ge(x_in, 16 * TT)
            ffn(COL["ff1_norm"])

            norm(x, TT, COL["mix_norm"])
            act_groups(2)
            with n.loop(dve, 4, unit=2, hi_ready=2, half_ready=2, half_freed=2, dve_step=9, root_ready=1) as i:
                split(1)
                dve.wait_ge(half_freed, 34)
                tiles = [vg[:, 2 * g:2 * g + 2, bass.ds(i, 1), :].rearrange("p c o k -> p (c o) k") for g in range(4)]
                for g in range(4):
                    ins = dve.bn_stats(bn[:, g, :], tiles[g])
                step(ins)
                dve.tensor_copy(NEW, SS)
                for g in range(4):
                    ins = dve.bn_aggr(mv[:, 2 * g:2 * g + 2], bn[:, g, :])
                step(ins)
                rsqrt(4, mv.rearrange("p (g s) -> p g s", s=2)[:, :, 1], 1.0)
                for g in range(4):
                    ins = dve.tensor_scalar(tiles[g], tiles[g], mv[:, 2 * g:2 * g + 1], R[:, g:g + 1],
                                            ALU.subtract, ALU.mult)
                step(ins)
                whole = vg[:, :, bass.ds(i, 1), :].rearrange("p c o k -> p (c o) k")
                step(dve.tensor_tensor(whole, whole, ln_g[:].rearrange("p (c k) -> p c k", c=KT), ALU.mult))
                dve.tensor_tensor(whole, whole, ln_b[:].rearrange("p (c k) -> p c k", c=KT),
                                  ALU.add).then_inc(ln_ready, 1)
                split(1)
                n.next("half_ready", 2)
                n.next("half_freed", 2)
            act_groups(2)
            with n.loop(dve, 2, unit=2, hi_ready=2, half_ready=2, half_freed=2, acthi_ready=2, operand_ready=2) as i:
                split(2)
                for hf in range(2):
                    t = bass.ds(i * 4 + 2 * hf, 2)
                    dve.wait_ge(mix_copied, KT)
                    n.next("half_ready")
                    dve.wait_ge(half_freed, n.next("half_freed"))
                    dve.wait_ge(operand_ready, n.now("operand_ready"))
                    dve.tensor_tensor(tmp[:, 1], tmp[:, 0], merged[:, t, :], ALU.mult).then_inc(prod_ready, 1)
                    low(ya_lo[:, t, :], tmp[:, 1], ya_hi[:, t, :])
            act_groups(2)
            with n.loop(dve, 2, unit=2, hi_ready=2, half_ready=2, half_freed=2) as i:
                split(2)
                for hf in range(2):
                    t = bass.ds(i * 4 + 2 * hf, 2)
                    complete()
                    freed(dve.tensor_tensor(merged[:, t, :], merged[:, t, :], ps[:, 2 * hf:2 * hf + 2, :], ALU.mult))

            for hh in range(2):
                for b in range(TT):
                    at = OB[b] + b + P * (b + 1)
                    ins = dve.memset(keep[:, hh, at:at + 1], 1.0)
            step(ins)
            with n.loop(dve, KT, masked_ready=16, dve_step=8, pv_done=2) as i:
                for hh in range(2):
                    for b in range(TT):
                        nk, at = P * (b + 1), OB[b] + b
                        dve.wait_ge(masked_ready, n.next("masked_ready", 2))
                        k = keep[:, hh, at:at + nk][:, ::-1]
                        step(dve.tensor_tensor_scan(k, k, k, 1.0, ALU.mult, ALU.bypass))
                        w = beta[:, hh, OB[b]:OB[b] + nk]
                        dve.tensor_tensor(w, w, keep[:, hh, at + 1:at + 1 + nk], ALU.mult).then_inc(w_ready, 1)
                dve.wait_ge(pv_done, n.next("pv_done", 2))
                dve.tensor_copy(qT[:, bass.ds(i, 1), :], ps[:, 3:4, :]).then_inc(o_copied, 1)

            act_groups(2)
            for j in range(2):
                t = slice(4 * j, 4 * j + 4)
                low(h_lo[:, t, :], qT[:, t, :], h_hi[:, t, :])
            with n.loop(dve, 2, unit=2, hi_ready=2, half_ready=2, half_freed=2, acthi_ready=2, operand_ready=2) as i:
                split(2)
                for hf in range(2):
                    t = bass.ds(i * 4 + 2 * hf, 2)
                    complete()
                    dve.tensor_tensor(tmp[:, 0], gate_b[:, t, :], ps[:, 2 * hf:2 * hf + 2, :],
                                      ALU.mult).then_inc(half_freed, 1)
                    dve.wait_ge(half_freed, n.next("half_freed"))
                    dve.tensor_tensor(merged[:, t, :], merged[:, t, :], tmp[:, 0], ALU.add).then_inc(prod_ready, 1)
                    low(m_lo[:, t, :], merged[:, t, :], m_hi[:, t, :])
            residual(2, 2, 1.0)
            ffn(COL["ff2_norm"])

            last_norm(48)
            norm(mem_tok, M_LEN // P, COL["g_mem_2"])
            split(2)
            n.next("half_ready", 2)
            n.next("half_freed", 2)
            norm(x, TT, COL["g_mix_2"])
            step(dve.tensor_copy(pos_f, pos_i[:]))
            for t in range(TT):
                ins = dve.tensor_scalar(ang[:, 32 * t:32 * t + 32], freq, pos_f[:, t:t + 1], None, ALU.mult)
            step(ins)
            step(dve.tensor_scalar(turns, ang, 1.0 / (2 * 3.141592653589793), ROUND, ALU.mult, ALU.add))
            step(dve.tensor_scalar(turns, turns, -ROUND, None, ALU.add))
            for part in TWO_PI:
                step(dve.scalar_tensor_tensor(out=ang, in0=turns, scalar=-part, in1=ang, op0=ALU.mult, op1=ALU.add))
            dve.tensor_scalar(r_sin, ang, PI, -PI, ALU.min, ALU.max)
            step(dve.tensor_scalar(r_cos, ang, 3.141592653589793 / 2, None, ALU.add))
            step(dve.tensor_scalar(turns, r_cos, 3.141592653589793, -2 * 3.141592653589793, ALU.is_gt, ALU.mult))
            step(dve.tensor_tensor(r_cos, r_cos, turns, ALU.add))
            dve.tensor_scalar(r_cos, r_cos, PI, -PI, ALU.min, ALU.max).then_inc(trig_ready, 1)
            act_groups(4)

            dve.wait_ge(sin_ready, 1)
            dve.wait_ge(half_freed, n.now("half_freed"))
            for c0, heads in ((0, 10), (768, 5), (Q_I, 5)):
                both = proj[:, :, c0:c0 + HD * heads].rearrange("p t (h w) -> p t h w", w=HD)
                x1, x2 = both[:, :, :, 0:32], both[:, :, :, 32:64]
                c, s = (a.rearrange("p (t w) -> p t w", t=TT).unsqueeze(2).broadcast_to([P, TT, heads, 32])
                        for a in (cos_t, sin_t))
                a1, a2, a3, a4 = (rope_t[:, j, 0:TT * heads * 32].rearrange("p (t h w) -> p t h w", t=TT, h=heads)
                                  for j in range(4))
                dve.tensor_tensor(a1, x1, c, ALU.mult)
                dve.tensor_tensor(a2, x2, s, ALU.mult)
                dve.tensor_tensor(a3, x2, c, ALU.mult)
                step(dve.tensor_tensor(a4, x1, s, ALU.mult))
                dve.tensor_tensor(x1, a1, a2, ALU.subtract)
                step(dve.tensor_tensor(x2, a3, a4, ALU.add))
            for j, c0 in enumerate((512, 576, K_D, K_I)):
                for r in range(2):
                    dve.tensor_copy(proj[:, :, KDUP + P * j + HD * r:KDUP + P * j + HD * r + HD], proj[:, :, c0:c0 + HD])
            dve.tensor_scalar(w_idx, proj[:, :, W_I:W_I + 4], 1.0 / 16, None, ALU.mult).then_inc(rope_ready, 1)

            z0 = 8 * KT

            def outputs(j):
                kind, b, heads, nk = JOBS[j]
                dve.wait_ge(o_ready, n.next("o_ready"))
                for bank in range(heads // 4):
                    t0 = O_TILE[kind] + 2 * bank
                    src = ps[0:HD, bank, :].rearrange("p (a e t) -> p a e t", a=2, e=2)
                    for e in range(2):
                        ins = dve.tensor_copy(oT[HD * e:HD * e + HD, t0:t0 + 2, b * P:(b + 1) * P], src[:, :, e, :])
                ins.then_inc(o_copied, 1)

            before = None
            for j, (kind, b, heads, nk) in enumerate(JOBS):
                if kind == "index":
                    dve.wait_ge(z_freed, j + 1)
                    sc = flat[:, 0:nk]
                    step(dve.tensor_scalar(sc, sc, w_idx[:, b, 0:1], None, ALU.mult))
                    for g in range(1, 4):
                        ins = dve.scalar_tensor_tensor(out=sc, in0=flat[:, g * BANK:g * BANK + nk],
                                                       scalar=w_idx[:, b, g:g + 1], in1=sc, op0=ALU.mult, op1=ALU.add)
                        if g < 3:
                            step(ins)
                    ins.then_inc(iscore_ready, 1)
                    dve.wait_ge(causal_ready, b + 1)
                    for r in range(P // 8):
                        step(dve.max(mx, sc))
                        step(dve.match_replace(sc, mx, sc, TAKEN))
                    step(dve.tensor_scalar(sc, sc, 10 * OUT_OF_REACH, MASKED, ALU.is_gt, ALU.mult))
                    continue
                row = BANK if kind == "chosen" else 256
                lg = logits[:, 0:heads * row].rearrange("p (h s) -> p h s", s=row)[:, :, 0:nk]
                z = ps[:, 4:8, :].rearrange("p a (c s) -> p (a c) s", s=row)[:, 0:heads, 0:nk]
                dve.wait_ge(z_ready, z0 + j + 1)
                dve.wait_ge(pT_ready, n.now("pT_ready"))
                n.next("pT_ready")
                if kind == "memory":
                    ins = dve.tensor_scalar(lg, z, SCALE, None, ALU.mult)
                else:
                    if kind == "chosen" and b == 0:
                        dve.wait_ge(causal_ready, 1)
                    if kind == "window":
                        dve.wait_ge(masks_made, 3)
                    mask = swa_mask[:, 256 - nk:256] if kind == "window" else flat[:, 0:nk]
                    ins = dve.scalar_tensor_tensor(out=lg, in0=z, scalar=SCALE,
                                                   in1=mask.unsqueeze(1).broadcast_to([P, heads, nk]),
                                                   op0=ALU.mult, op1=ALU.add)
                ins.then_inc(z_freed, 1)
                dve.wait_ge(z_freed, j + 1)
                step(dve.tensor_reduce(mx[:, 0:heads], lg, AX.X, ALU.max))
                if kind == "window":
                    step(dve.tensor_tensor(mx, mx, snk, ALU.max))
                    dve.tensor_tensor(snk_e, snk, mx, ALU.subtract)
                dve.tensor_scalar(neg[:, 0:heads], mx[:, 0:heads], -1.0, None, ALU.mult).then_inc(logit_ready, 1)
                if before is not None:
                    outputs(before)
                before = j
                dve.wait_ge(exp_ready, n.next("exp_ready"))
                if kind == "window":
                    step(dve.tensor_tensor(tot, tot, snk_e, ALU.add))
                step(dve.reciprocal(rec[:, 0:heads], tot[:, 0:heads]))
                dve.tensor_tensor(lg, lg, rec[:, 0:heads].unsqueeze(2).broadcast_to([P, heads, nk]),
                                  ALU.mult).then_inc(prob_ready, 1)
            outputs(before)

            for j in range(2):
                t = slice(4 * j, 4 * j + 4)
                low(o_lo[:, t, :], oT[:, t, :], o_hi[:, t, :])
            act_groups(6)
            for c in range(2):
                for kind in range(3):
                    split(1)
                    for hf in range(2):
                        complete()
                        t = slice(4 * c + 2 * hf, 4 * c + 2 * hf + 2)
                        g = slice(8 * kind + 4 * c + 2 * hf, 8 * kind + 4 * c + 2 * hf + 2)
                        banks = ps[:, 2 * hf:2 * hf + 2, :]
                        if kind == 0:
                            freed(dve.tensor_tensor(merged2[:, t, :], gates2[:, g, :], banks, ALU.mult))
                            continue
                        dve.tensor_tensor(tmp[:, 0], gates2[:, g, :], banks, ALU.mult).then_inc(half_freed, 1)
                        dve.wait_ge(half_freed, n.next("half_freed"))
                        ins = dve.tensor_tensor(merged2[:, t, :], merged2[:, t, :], tmp[:, 0], ALU.add)
                        if kind == 1:
                            step(ins)
                        else:
                            ins.then_inc(prod_ready, 1)
                            low(m2_lo[:, t, :], merged2[:, t, :], m2_hi[:, t, :])
            residual(2, 2, 1.0)
            norm(x, TT, COL["g_mlp_2"])
            for c in range(2):
                with n.loop(dve, 4, unit=2, hi_ready=2, half_ready=2, half_freed=2, acthi_ready=2, operand_ready=2) as i:
                    split(2)
                    for hf in range(2):
                        t = bass.ds(i * 4 + 2 * hf, 2)
                        n.next("half_ready")
                        dve.wait_ge(half_freed, n.next("half_freed"))
                        dve.wait_ge(operand_ready, n.now("operand_ready"))
                        dve.tensor_tensor(tmp[:, 1], tmp[:, 0], tmp[:, 0], ALU.mult).then_inc(prod_ready, 1)
                        low(hid_lo[:, t, :], tmp[:, 1], hid_hi[:, t, :])
                if c == 0:
                    residual(2, 4, 1.0)
                else:
                    for i in range(2):
                        split(4 - i)
                        add(i, 1.0)
            last_norm(64)


_INS = ["x", "ff1_norm", "ff1_w_gate", "ff1_w_up", "ff1_w_down", "mix_norm", "w_in", "b_gate",
        "gmlp_ln_g", "gmlp_ln_b", "gmlp_w_s", "gmlp_b_s", "w_branch_a", "w_branch_b", "w_out",
        "ff2_norm", "ff2_w_gate", "ff2_w_up", "ff2_w_down", "final_norm", "mem_2", "positions_2",
        "g_mix_2", "w_in_2", "b_gate_2", "sinks_2", "g_mem_2", "w_mem_kv_2", "w_proj_swa_2",
        "w_proj_dsa_2", "w_proj_mem_2", "w_out_2", "g_mlp_2", "w_mlp_in_2", "w_mlp_out_2", "g_final_2"]


def kernel(**inputs):
    import numpy as np
    import concourse.bacc as bacc
    from concourse.bass_utils import run_bass_kernel_spmd

    nc = bacc.Bacc("TRN2", target_bir_lowering=False, num_devices=1)
    arrays, aps = {}, {}

    def give(name, a):
        arrays[f"in_{name}"] = a
        aps[name] = nc.dram_tensor(f"in_{name}", a.shape, mybir.dt.from_np(a.dtype), kind="ExternalInput").ap()

    for name in _INS:
        give(name, np.ascontiguousarray(inputs[name]))
    half = HD // 2
    give("inv_freq", np.power(np.float32(10000.0), -np.arange(half, dtype=np.float32) / np.float32(half)).astype(np.float32))
    shape = tuple(inputs["x"].shape)
    out = nc.dram_tensor("out_0", shape, F32, kind="ExternalOutput").ap()
    build(nc, aps, out)
    r = run_bass_kernel_spmd(nc, [arrays], core_ids=[0])
    return r.results[0]["out_0"]
```

```python
from contextlib import ExitStack

import concourse.bass as bass
from concourse import mybir
from concourse.alu_op_type import AluOpType as ALU

ACT = mybir.ActivationFunctionType
AX = mybir.AxisListType
F32 = mybir.dt.float32
FR = mybir.dt.float32r
I32 = mybir.dt.int32

P = 128
BANK = 512
HD = 64
EPS = 1e-6
SCALE = HD ** -0.5
MASKED = -1e30
OUT_OF_REACH = -1e37
TAKEN = -3e38
ROUND = 1.5 * 2.0 ** 23
TWO_PI = (6.28125, 1.9350051879882812e-03, 3.0199159819567e-07)
PI = 3.1415925


CREDIT = ("pv_done", "wT_copied", "o_copied")


class Tally:

    def __init__(self):
        self.steps, self.i, self.per = dict.fromkeys(CREDIT, 1), None, {}

    def now(self, key, add=0):
        per = self.per.get(key, 0)
        return self.i * per + (self.steps.get(key, 0) + add) if per else self.steps.get(key, 0) + add

    def next(self, key, by=1):
        assert self.i is None or key in self.per, key
        self.steps[key] = self.steps.get(key, 0) + by
        return self.now(key)

    def unit(self):
        u = self.next("unit") - 1
        c, per = self.steps["unit"] - 1, self.per.get("unit", 0)
        assert per % 2 == 0
        landed = self.i * (16 * per) + 32 * (c // 2 + 1) if per else 32 * (c // 2 + 1)
        return u, c % 2, landed

    def loop(self, eng, turns, **per):
        return _Loop(self, eng, turns, per)


class _Loop:
    def __init__(self, tally, eng, turns, per):
        self.t, self.turns, self.per = tally, turns, per
        self.ctx = eng.Fori(0, turns)

    def __enter__(self):
        self.t.i, self.t.per = self.ctx.__enter__(), self.per
        self.before = dict(self.t.steps)
        return self.t.i

    def __exit__(self, *a):
        t = self.t
        if a[0] is None:
            made = {k: n - self.before.get(k, 0) for k, n in t.steps.items()}
            assert {k: n for k, n in made.items() if n} == self.per, (made, self.per)
            for k, n in self.per.items():
                t.steps[k] = self.before.get(k, 0) + n * self.turns
        t.i, t.per = None, {}
        return self.ctx.__exit__(*a)


def build(nc, A, out):
    D, S = A["x"].shape[2], A["x"].shape[1]
    KT, TT = D // P, S // P
    M_LEN = A["mem_2"].shape[1]
    PCOLS = 1732
    V_S, K_D, V_D, Q_I, K_I, W_I, Q_M = 640, 1024, 1088, 1152, 1408, 1472, 1476
    KDUP = PCOLS
    TILE_COLS = [0, 128, 256, 384, 768, 896, Q_I, Q_I + 128, Q_M, Q_M + 128] + [KDUP + P * j for j in range(4)]
    QS, QD, QI, QM, KS, KD, KI = 0, 4, 6, 8, 10, 12, 13
    ROWS = [("ff1_norm", 8), ("mix_norm", 8), ("ff2_norm", 8), ("g_mix_2", 8), ("g_mem_2", 8),
            ("g_mlp_2", 8), ("b_gate", 16), ("b_gate_2", 24)]
    COL = {name: sum(r for _, r in ROWS[:j]) for j, (name, _) in enumerate(ROWS)}
    NCOLS = sum(r for _, r in ROWS)
    HALVES_FF2, HALVES_MLP = 70, 138
    OB = [P * b * (b + 1) // 2 for b in range(TT)]

    ctx = ExitStack()
    with ctx:
        def sb(name, shape, dt=F32):
            return ctx.enter_context(nc.sbuf_tensor(name, shape, dt))

        def sem(name):
            return ctx.enter_context(nc.semaphore(name))

        x = sb("resid", [P, TT, D])
        h_hi = sb("h_hi", [P, KT, S], FR)
        h_lo = sb("h_lo", [P, KT, S], FR)
        raw = sb("raw", [P, 2, 4, BANK])
        w_hi = sb("w_hi", [P, 2, 4, BANK], FR)
        w_lo = sb("w_lo", [P, 2, 4, BANK], FR)
        tmp = sb("tmp", [P, 2, 2, BANK])
        ident = sb("ident", [P, P])
        cols = sb("cols", [P, NCOLS])
        wsT = sb("wsT", [P, 4, P])
        swa_mask = wsT[:, 0:2, :].rearrange("p a b -> p (a b)")
        before = wsT[:, 0, :]
        stat = sb("stat", [P, 100])
        pos_i = sb("pos_i", [P, TT], I32)
        memT = sb("memT", [P, 2, M_LEN])
        memv = sb("memv", [P, 2, 4 * HD])
        SS, VAR, REC, ROOT, NEW, R = (stat[:, 4 * j:4 * j + 4] for j in range(6))
        mv = stat[:, 24:32]
        bn = stat[:, 32:56].rearrange("p (g s) -> p g s", g=4)
        mx, neg, tot, snk, snk_e = (stat[:, 56 + 8 * j:64 + 8 * j] for j in range(5))
        rec, mx8 = stat[:, 24:32], stat[:, 48:56]
        w_idx = stat[:, 32:48].rearrange("p (t h) -> p t h", t=TT)

        def layout(gap, *tensors):
            with ExitStack() as c:
                if gap:
                    c.enter_context(nc.sbuf_tensor("gap_" + tensors[0][0], [P, gap], F32))
                return [c.enter_context(nc.sbuf_tensor(n, s, d)) for n, s, d in tensors]

        T16 = KT * S
        hid_hi, hid_lo, rows, mem_tok = layout(
            0, ("hid_hi", [P, 16, S], FR), ("hid_lo", [P, 16, S], FR), ("rows", [P, D], F32),
            ("mem_tok", [P, 2, D], F32))
        qT, kT, v_tok, vg, ya_hi, ya_lo = layout(
            0, ("qT", [P, KT, S], F32), ("kT", [P, KT, S], F32), ("v_tok", [P, TT, D], F32),
            ("vg", [P, KT, TT, P], F32), ("ya_hi", [P, KT, S], FR), ("ya_lo", [P, KT, S], FR))
        ln_g, ln_b, col_rows, ws_raw, bs_row, ones_row = layout(
            4 * T16, ("ln_g", [P, D], F32), ("ln_b", [P, D], F32), ("col_rows", [P, P], F32),
            ("ws_raw", [P, 4, P], F32), ("bs_row", [1, 4 * P], F32), ("ones_row", [1, P], F32))
        beta, keep, wT, pair = layout(
            4 * T16, ("beta", [P, 2, 1280], F32), ("keep", [P, 2, 1284], F32), ("wT", [P, 1280], F32),
            ("pair", [P, 3, S], F32))
        pairs = [pair, tmp[:, :, :, :].rearrange("p a b c -> p (a b) c")]
        m_hi, m_lo = layout(T16, ("m_hi", [P, KT, S], FR), ("m_lo", [P, KT, S], FR))
        gate_b, = layout(4 * T16, ("gate_b", [P, KT, S], F32))
        merged = vg[:, :, :, :].rearrange("p k n t -> p k (n t)")
        proj, qkT = layout(0, ("proj", [P, TT, PCOLS + 512], F32), ("qkT", [P, 14, S], F32))
        rope_t, trig = layout(4 * T16, ("rope_t", [P, 4, 1280], F32), ("trig", [P, 7, TT * 32], F32))
        logits, pT, vals = layout(
            4 * T16, ("logits", [P, 1024], F32), ("pT", [P, 1024], F32), ("vals", [P, TT, 3 * HD], F32))
        mask, = layout(4 * T16 + 2048 + 3 * TT * HD, ("mask", [P, S], F32))
        oT, = layout(4 * T16 + 4096, ("oT", [P, 8, S], F32))
        o_hi, o_lo = layout(4 * T16, ("o_hi", [P, 8, S], FR), ("o_lo", [P, 8, S], FR))
        gates2, merged2 = layout(0, ("gates2", [P, 24, S], F32), ("merged2", [P, KT, S], F32))
        m2_hi, m2_lo = layout(0, ("m2_hi", [P, KT, S], FR), ("m2_lo", [P, KT, S], FR))
        flat = tmp[:, :, :, :].rearrange("p a b c -> p (a b c)")
        ang, turns, r_sin, r_cos, sin_t, cos_t, misc = (trig[:, j, :] for j in range(7))
        freq, pos_f = misc[:, 0:32], misc[:, 32:36]

        ps = ctx.enter_context(nc.psum_tensor("ps", [P, 8, BANK], F32))

        x_in = sem("x_in")
        const_in = sem("const_in")
        rows_in = sem("rows_in")
        raw_ready = [sem("raw_ready0"), sem("raw_ready1")]
        hi_ready = sem("hi_ready")
        lo_ready = sem("lo_ready")
        weights_used = sem("weights_used")
        half_ready = sem("half_ready")
        half_freed = sem("half_freed")
        prod_ready = sem("prod_ready")
        acthi_ready = sem("acthi_ready")
        operand_ready = sem("operand_ready")
        made = sem("made")
        masks_made = sem("masks_made")
        cols_tr = sem("cols_tr")
        cols_ready = sem("cols_ready")
        sq_ready = sem("sq_ready")
        var_ready = sem("var_ready")
        root_ready = sem("root_ready")
        xn_ready = sem("xn_ready")
        xn_used = sem("xn_used")
        out_ready = sem("out_ready")
        dve_step = sem("dve_step")
        vg_copied = sem("vg_copied")
        ln_ready = sem("ln_ready")
        mix_ready = sem("mix_ready")
        mix_copied = sem("mix_copied")
        pair_ready = sem("pair_ready")
        z_ready = sem("z_ready")
        sig_ready = sem("sig_ready")
        masked_ready = sem("masked_ready")
        w_ready = sem("w_ready")
        wT_ready = sem("wT_ready")
        wT_copied = sem("wT_copied")
        pv_done = sem("pv_done")
        o_copied = sem("o_copied")
        trig_ready = sem("trig_ready")
        sin_ready = sem("sin_ready")
        rope_ready = sem("rope_ready")
        tr_ready = sem("tr_ready")
        tr_copied = sem("tr_copied")
        z_freed = sem("z_freed")
        iscore_ready = sem("iscore_ready")
        causal_ready = sem("causal_ready")
        logit_ready = sem("logit_ready")
        exp_ready = sem("exp_ready")
        prob_ready = sem("prob_ready")
        pT_ready = sem("pT_ready")
        pT_copied = sem("pT_copied")
        o_ready = sem("o_ready")
        stored = sem("stored")

        def kpn(name):
            return A[name][0].rearrange("(k p) n -> p k n", p=P)

        JOBS, EARLY, LATE, CHOICE = [], [], [], []
        for b in range(TT):
            last = b == TT - 1
            if not last:
                JOBS += [("index", b + 1, c, P * (b + 2)) for c in range(2)]
                EARLY, LATE, CHOICE = EARLY + [0, 2], LATE + [0, 0], CHOICE + [0, 0]
            JOBS += [("window", b, c, P * min(b + 1, 2)) for c in range(2)]
            JOBS += [("chosen", b, c, P * (b + 1)) for c in range(2)] + [("memory", b, 0, M_LEN)]
            EARLY += [1, 1, 2, 2, 1] if last else [1] * 5
            LATE += [1] * 5
            CHOICE += [0] * 5 if last else [3, 3, 3, 3, 4]
        DONE = [sum(EARLY[:j]) + sum(LATE[:j]) for j in range(len(JOBS) + 1)]
        GROUPS_BETWEEN = 6
        assert DONE[-1] == 8 * GROUPS_BETWEEN and all(8 * g in DONE for g in range(GROUPS_BETWEEN))

        def heads_of(kind, c):
            if kind in ("chosen", "index"):
                return [(2 * c + e, BANK * e) for e in range(2)]
            return [(4 * c + g, BANK * (g % 2) + 256 * (g // 2)) for g in range(4)]

        block = ctx.enter_context(nc.Block())

        @block.sync
        def _(sp):
            n = Tally()

            def unit(parts):
                u, slot, _ = n.unit()
                if n.i is not None or u >= 2:
                    sp.wait_ge(lo_ready, u - 1)
                for dst, src in parts(raw[:, slot]):
                    sp.dma_start(dst, src).then_inc(raw_ready[slot], 16)

            def slabs(w, k0, m, c0, width=BANK):
                a = (m + 1) // 2
                unit(lambda r: [(r[:, 0:a, 0:width], w[:, k0:k0 + a, bass.ds(c0, width)]),
                                (r[:, a:m, 0:width], w[:, k0 + a:k0 + m, bass.ds(c0, width)])])

            def gate_up(name, c0):
                gate, up = kpn(name + "_w_gate"), kpn(name + "_w_up")
                for k0 in (0, 4):
                    unit(lambda r: [(r[:, :, 0:256], gate[:, k0:k0 + 4, bass.ds(c0, 256)]),
                                    (r[:, :, 256:512], up[:, k0:k0 + 4, bass.ds(c0, 256)])])

            def groups(name, turns, c0, width=BANK, k0=0, kt=KT):
                w = kpn(name)
                with n.loop(sp, turns, unit=kt // 4) as i:
                    for k in range(k0, k0 + kt, 4):
                        slabs(w, k, 4, i * width + c0, width)

            def ffn(name, first):
                down = kpn(name + "_w_down")
                if first:
                    gate_up(name, 0)
                with n.loop(sp, 8 - first, unit=2) as i:
                    gate_up(name, i * 256 + 256 * first)
                groups(name + "_w_down", 2, 0, kt=16)
                with n.loop(sp, 3, unit=2) as i:
                    gate_up(name, i * 256 + 2048)
                with n.loop(sp, 2, unit=2) as i:
                    for k0 in (16, 19):
                        slabs(down, k0, 3, i * BANK)

            for t in range(TT):
                sp.dma_start(x[:, t, :], A["x"][0, t * P:(t + 1) * P, :]).then_inc(x_in, 16)
            ffn("ff1", 1)
            groups("w_in", 2, 1024)
            groups("w_in", 4, 2048)
            groups("w_in", 2, 4096)
            groups("w_in", 2, 0)
            groups("w_in", 2, 5120)
            groups("w_branch_a", 2, 0)
            groups("w_in", 2, 6144)
            groups("w_branch_b", 2, 0)
            groups("w_out", 2, 0)
            ffn("ff2", 0)
            for k0 in (0, 4):
                slabs(kpn("w_mem_kv_2"), k0, 4, 0)
            groups("w_in_2", 2, 0)
            groups("w_in_2", 2, 1024, 354)
            groups("w_in_2", 6, PCOLS)
            for c0 in (0, BANK):
                slabs(kpn("w_proj_swa_2"), 0, 4, c0)
                slabs(kpn("w_proj_dsa_2"), 0, 2, c0)
                slabs(kpn("w_proj_mem_2"), 0, 2, c0)
            groups("w_out_2", 2, 0)
            for c in range(2):
                groups("w_mlp_in_2", 4, c * 2048)
                groups("w_mlp_out_2", 2, 0, k0=16 * c, kt=16)
            for t in range(TT):
                sp.wait_ge(out_ready, TT + t + 1)
                sp.dma_start(out[0, t * P:(t + 1) * P, :], x[:, t, :]).then_inc(stored, 16)
            sp.wait_ge(stored, 16 * TT)

        @block.gpsimd
        def _(pool):
            n = Tally()
            row = 0
            for name, r in ROWS:
                pool.dma_start(col_rows[row:row + r, :], A[name][0].rearrange("(r p) -> r p", p=P)).then_inc(const_in, 16)
                row += r
            pool.dma_start(ws_raw[:], A["gmlp_w_s"][0].rearrange("g t s -> t g s")).then_inc(const_in, 16)
            pool.dma_start(bs_row[:], A["gmlp_b_s"].rearrange("a g t -> a (g t)")).then_inc(const_in, 16)
            pool.dma_start(ln_g[:], A["gmlp_ln_g"][0].rearrange("g c -> (g c)").partition_broadcast(P)).then_inc(const_in, 16)
            pool.dma_start(ln_b[:], A["gmlp_ln_b"][0].rearrange("g c -> (g c)").partition_broadcast(P)).then_inc(const_in, 16)
            for e in range(2):
                for c in range(2):
                    pool.dma_start(snk[:, 4 * c + 2 * e:4 * c + 2 * e + 2],
                                   A["sinks_2"][0].rearrange("(c a e) -> e c a", c=2, e=2)[e, c].partition_broadcast(P),
                                   allow_slow_non_contiguous=True).then_inc(const_in, 16)
            pool.dma_start(pos_i[:], A["positions_2"][0].rearrange("(t p) -> p t", p=P),
                           allow_slow_non_contiguous=True).then_inc(const_in, 16)
            pool.memset(ident[:], 0.0).then_inc(made, 1)
            pool.memset(ones_row[:], 1.0).then_inc(made, 1)
            pool.wait_ge(made, n.next("made", 2))
            pool.affine_select(out=ident[:], in_=ident[:], compare_op=ALU.not_equal, fill=1.0, base=0,
                               pattern=[[-1, P]], channel_multiplier=1).then_inc(made, 1)

            n.next("half_freed", 30 + 28)
            pool.wait_ge(half_freed, n.now("half_freed"))
            pool.memset(before, 1.0).then_inc(made, 1)
            pool.wait_ge(made, 4)
            pool.affine_select(out=before, in_=before, compare_op=ALU.is_gt, fill=0.0, base=0,
                               pattern=[[-1, P]], channel_multiplier=1).then_inc(made, 1)
            pool.wait_ge(made, 5)

            def stage(to, tile):
                pool.tensor_copy(to[:, 0, :], qT[:, tile(1), :]).then_inc(pair_ready, 1)
                pool.tensor_copy(to[:, 1, :], kT[:, tile(1), :]).then_inc(pair_ready, 1)
                pool.tensor_copy(to[:, 2, :].rearrange("p (t c) -> p t c", t=TT),
                                 v_tok[:, :, tile(P)]).then_inc(pair_ready, 1)

            def diagonals(hh):
                for b in range(TT):
                    pool.wait_ge(sig_ready, n.next("sig_ready"))
                    w = beta[:, hh, OB[b] + P * b:OB[b] + P * b + P]
                    k = keep[:, hh, OB[b] + b + P * b:OB[b] + b + P * b + P]
                    pool.tensor_tensor(w, w, before, ALU.mult).then_inc(masked_ready, 1)
                    pool.affine_select(out=k, in_=k, compare_op=ALU.is_gt, fill=1.0, base=0,
                                       pattern=[[-1, P]], channel_multiplier=1).then_inc(masked_ready, 1)

            stage(pairs[0], lambda w: slice(0, w))
            with n.loop(pool, KT // 2 - 1, pv_done=4, sig_ready=16) as i:
                for c in range(2):
                    diagonals(0)
                    pool.wait_ge(pv_done, n.now("pv_done"))
                    n.next("pv_done", 2)
                    stage(pairs[(c + 1) % 2], lambda w: bass.ds(i * (2 * w) + w * (c + 1), w))
                    diagonals(1)
            diagonals(0)
            pool.wait_ge(pv_done, n.now("pv_done"))
            stage(pairs[1], lambda w: slice(w * (KT - 1), w * KT))
            for hh in (1, 0, 1):
                diagonals(hh)

            pool.wait_ge(half_freed, HALVES_FF2)
            pool.dma_start(rows[:], A["final_norm"].partition_broadcast(P)).then_inc(rows_in, 16)
            pool.dma_start(mem_tok[:], A["mem_2"][0].rearrange("(t p) d -> p t d", p=P)).then_inc(rows_in, 16)
            pool.dma_start(freq, A["inv_freq"].partition_broadcast(P)).then_inc(rows_in, 16)
            pool.memset(swa_mask, 0.0).then_inc(masks_made, 1)
            pool.wait_ge(masks_made, 1)
            pool.affine_select(out=swa_mask, in_=swa_mask, compare_op=ALU.is_ge, fill=MASKED, base=P,
                               pattern=[[-1, 2 * P]], channel_multiplier=1).then_inc(masks_made, 1)
            pool.wait_ge(masks_made, 2)
            pool.affine_select(out=swa_mask, in_=swa_mask, compare_op=ALU.is_gt, fill=MASKED, base=0,
                               pattern=[[1, 2 * P]], channel_multiplier=-1).then_inc(masks_made, 1)
            pool.wait_ge(rope_ready, 1)
            pool.memset(mask[:, 0:P], 0.0).then_inc(masks_made, 1)
            pool.wait_ge(masks_made, 4)
            pool.affine_select(out=mask[:, 0:P], in_=mask[:, 0:P], compare_op=ALU.is_ge, fill=MASKED, base=0,
                               pattern=[[-1, P]], channel_multiplier=1).then_inc(causal_ready, 1)
            for b in range(1, TT):
                pool.wait_ge(iscore_ready, n.next("iscore_ready"))
                diag = flat[:, P * b:P * b + P]
                pool.affine_select(out=diag, in_=diag, compare_op=ALU.is_ge, fill=OUT_OF_REACH, base=0,
                                   pattern=[[-1, P]], channel_multiplier=1).then_inc(causal_ready, 1)
            pool.wait_ge(half_freed, HALVES_MLP)
            pool.dma_start(rows[:], A["g_final_2"].partition_broadcast(P)).then_inc(rows_in, 16)

        @block.tensor
        def _(pe):
            n = Tally()

            def three(out_, w, a, weights_first, first, last):
                (wh, wl), (ah, al) = w, a
                for j, (p, q) in enumerate(((wh, ah), (wh, al), (wl, ah))):
                    lhs, rhs = (p, q) if weights_first else (q, p)
                    mm = pe.matmul(out_, lhs, rhs, start=first and j == 0, stop=last and j == 2)
                return mm

            def group(act, units, weights_first, width=BANK, first_group=False, operands=()):
                k, kt = 0, sum(units)
                for j, m in enumerate(units):
                    u, slot, _ = n.unit()
                    pe.wait_ge(lo_ready, u + 1)
                    if operands:
                        pe.wait_ge(operand_ready, operands[j])
                    for s in range(m):
                        for b in range(4):
                            if k == 0 and b in (0, 2) and not first_group:
                                pe.wait_ge(half_freed, n.now("half_freed", -1 if b == 0 else 0))
                            wc = slice(b * P, (b + 1) * P) if weights_first else slice(0, width)
                            ac = slice(0, S) if weights_first else slice(b * P, (b + 1) * P)
                            mm = three(ps[:, b, 0:S if weights_first else width],
                                       (w_hi[:, slot, s, wc], w_lo[:, slot, s, wc]),
                                       (act[0][:, k, ac], act[1][:, k, ac]), weights_first, k == 0, k == kt - 1)
                            if k == kt - 1 and b in (1, 3):
                                mm.then_inc(half_ready, 1)
                        k += 1
                    if j < len(units) - 1:
                        mm.then_inc(weights_used, 1)
                n.next("half_freed", 2)

            def groups(turns, act, units, weights_first, width=BANK, new=()):
                operands = fresh(*new)
                with n.loop(pe, turns, unit=len(units), half_freed=2):
                    group(act, units, weights_first, width, operands=operands)

            def fresh(*new):
                before = n.now("operand_ready")
                if new:
                    n.next("operand_ready", new[-1])
                return [before + k for k in new]

            def norm_transposes(tiles):
                for t in range(tiles):
                    pe.wait_ge(xn_ready, n.next("xn_ready"))
                    for k in range(KT):
                        tr = pe.transpose(ps[:, k, t * P:(t + 1) * P],
                                          tmp[:, t % 2, k // 4, (k % 4) * P:(k % 4 + 1) * P], ident[:])
                    tr.then_inc(xn_used, 1)

            h = (h_hi, h_lo)
            hid = (hid_hi, hid_lo)

            def ffn(first):
                norm_transposes(TT)
                if first:
                    group(h, (4, 4), True, first_group=True, operands=fresh(4, 8))
                    groups(7, h, (4, 4), True)
                else:
                    groups(8, h, (4, 4), True, new=(4, 8))
                groups(2, hid, (4, 4, 4, 4), False, new=(2, 4, 6, 8))
                groups(3, h, (4, 4), True)
                groups(2, hid, (3, 3), False, new=(2, 3))

            pe.wait_ge(made, 3)
            pe.wait_ge(const_in, 16 * (len(ROWS) + 9))
            pe.transpose(ps[:, 4, 0:NCOLS], col_rows[0:NCOLS, :], ident[0:NCOLS, 0:NCOLS]).then_inc(pv_done, 1)
            for g in range(4):
                tr = pe.transpose(ps[:, 5, g * P:(g + 1) * P], ws_raw[:, g, :], ident[:])
            tr.then_inc(cols_tr, 1)
            pe.wait_ge(cols_ready, 2)

            ffn(True)

            norm_transposes(TT)
            groups(2, h, (4, 4), False, new=(4, 8))
            groups(4, h, (4, 4), True)
            groups(2, h, (4, 4), False)
            pe.wait_ge(ln_ready, TT)
            for j in range(KT):
                if j >= 4:
                    pe.wait_ge(mix_copied, j - 3)
                for t in range(TT):
                    o = ps[:, 4 + j % 4, t * P:(t + 1) * P]
                    pe.matmul(o, vg[:, j, t, :], wsT[:, j // 2, :], start=True, stop=False)
                    mm = pe.matmul(o, ones_row[0:1, :], bs_row[0:1, (j // 2) * P:(j // 2 + 1) * P],
                                   start=False, stop=True)
                mm.then_inc(mix_ready, 1)
            groups(2, h, (4, 4), True)
            groups(2, h, (4, 4), True)
            groups(2, (ya_hi, ya_lo), (4, 4), True, new=(2, 4))

            pe.wait_ge(half_freed, n.now("half_freed"))

            def logits1(c, hh, first=False):
                if hh == 0:
                    pe.wait_ge(pair_ready, n.next("pair_ready", 3))
                half = slice(HD * hh, HD * hh + HD)
                for b in range(TT):
                    if not first:
                        pe.wait_ge(sig_ready, n.next("sig_ready"))
                    pe.matmul(ps[:, 4 + b, 0:P * (b + 1)], pairs[c][half, 0, b * P:(b + 1) * P],
                              pairs[c][half, 1, 0:P * (b + 1)], start=True, stop=True).then_inc(z_ready, 1)

            def outputs1(c, hh):
                pe.wait_ge(wT_copied, n.now("wT_copied"))
                for b in range(TT):
                    pe.wait_ge(w_ready, n.next("w_ready"))
                    for s in range(b + 1):
                        bank, col = ((0, b), (1, b - 1), (2, b - 2), (2, 2))[s]
                        tr = pe.transpose(ps[:, bank, col * P:(col + 1) * P],
                                          beta[:, hh, OB[b] + s * P:OB[b] + (s + 1) * P], ident[:])
                tr.then_inc(wT_ready, 1)
                pe.wait_ge(wT_copied, n.next("wT_copied"))
                if hh == 0:
                    pe.wait_ge(o_copied, n.now("o_copied"))
                    n.next("o_copied")
                for s, at in enumerate((0, 512, 896, 1152)):
                    mm = pe.matmul(ps[HD * hh:HD * hh + HD, 3, s * P:S],
                                   pairs[c][:, 2, s * P + HD * hh:s * P + HD * hh + HD],
                                   wT[:, at:at + S - s * P], start=s == 0, stop=s == TT - 1,
                                   skip_group_check=True)
                mm.then_inc(pv_done, 1)

            heads4 = [(c, hh) for c in range(2) for hh in range(2)]
            logits1(0, 0, True)
            with n.loop(pe, KT // 2 - 1, pair_ready=6, sig_ready=16, w_ready=16, wT_copied=4, o_copied=2):
                for g in range(4):
                    logits1(*heads4[(g + 1) % 4])
                    outputs1(*heads4[g])
            for g in range(4):
                if g < 3:
                    logits1(*heads4[g + 1])
                outputs1(*heads4[g])
            pe.wait_ge(o_copied, n.now("o_copied"))

            groups(2, h, (4, 4), True)
            groups(2, h, (4, 4), True, new=(1, 2))
            groups(2, (m_hi, m_lo), (4, 4), False, new=(2, 4))

            ffn(False)

            norm_transposes(M_LEN // P)
            operands = fresh(4, 8)
            for j in range(2):
                u, slot, _ = n.unit()
                pe.wait_ge(lo_ready, u + 1)
                pe.wait_ge(operand_ready, operands[j])
                for s in range(4):
                    k = 4 * j + s
                    for b in range(4):
                        if k == 0 and b in (0, 2):
                            pe.wait_ge(half_freed, n.now("half_freed", -1 if b == 0 else 0))
                        keys = b < 2
                        wc = slice(b * P, (b + 1) * P) if keys else slice(256, 512)
                        ac = slice(0, M_LEN) if keys else slice((b - 2) * P, (b - 1) * P)
                        mm = three(ps[:, b, 0:256], (w_hi[:, slot, s, wc], w_lo[:, slot, s, wc]),
                                   (h_hi[:, k, ac], h_lo[:, k, ac]), keys, k == 0, k == KT - 1)
                        if k == KT - 1 and b in (1, 3):
                            mm.then_inc(half_ready, 1)
                if j == 0:
                    mm.then_inc(weights_used, 1)
            n.next("half_freed", 2)

            norm_transposes(TT)
            groups(2, h, (4, 4), False, new=(4, 8))
            groups(2, h, (4, 4), False, 354)

            pe.wait_ge(rope_ready, 1)
            pe.wait_ge(half_freed, n.now("half_freed"))
            for j, c in enumerate(TILE_COLS):
                if j >= 8:
                    pe.wait_ge(tr_copied, j - 7)
                for t in range(TT):
                    tr = pe.transpose(ps[:, j % 8, t * P:(t + 1) * P], proj[:, t, c:c + P], ident[:])
                tr.then_inc(tr_ready, 1)
            pe.wait_ge(tr_copied, len(TILE_COLS))

            def scores(j):
                kind, b, c, nk = JOBS[j]
                if j:
                    pe.wait_ge(z_freed, j)
                for g, at in heads_of(kind, c):
                    half = slice(HD * (g % 2), HD * (g % 2) + HD)
                    q0 = {"window": QS, "chosen": QD, "index": QI, "memory": QM}[kind] + g // 2
                    if kind == "window":
                        k = qkT[half, KS + c, (b + 1) * P - nk:(b + 1) * P]
                    elif kind == "memory":
                        k = memT[half, g // 2, :]
                    else:
                        k = qkT[half, KI if kind == "index" else KD, 0:nk]
                    mm = pe.matmul(ps[:, 4 + at // BANK, at % BANK:at % BANK + nk],
                                   qkT[half, q0, b * P:(b + 1) * P], k, start=True, stop=True)
                mm.then_inc(z_ready, 1)

            def transposes(j):
                kind, b, c, nk = JOBS[j]
                pe.wait_ge(prob_ready, n.next("prob_ready"))
                pe.wait_ge(o_copied, n.now("o_copied"))
                heads = heads_of(kind, c)
                for g, at in heads:
                    for kb in range(nk // P):
                        to = kb * len(heads) * P + (g % len(heads)) * P
                        tr = pe.transpose(ps[:, 6 + to // BANK, to % BANK:to % BANK + P],
                                          logits[:, at + kb * P:at + (kb + 1) * P], ident[:])
                tr.then_inc(pT_ready, 1)

            def values(j):
                kind, b, c, nk = JOBS[j]
                pe.wait_ge(pT_copied, n.next("pT_copied"))
                for g in range(4 if kind == "memory" else 1):
                    for kb in range(nk // P):
                        if kind == "window":
                            v = vals[:, b + 1 - nk // P + kb, HD * c:HD * c + HD]
                            w = slice(kb * BANK, (kb + 1) * BANK)
                        elif kind == "chosen":
                            v, w = vals[:, kb, 2 * HD:3 * HD], slice(kb * 256, (kb + 1) * 256)
                        else:
                            v = memv[:, kb, HD * g:HD * g + HD]
                            w = slice(kb * BANK + g * P, kb * BANK + (g + 1) * P)
                        mm = pe.matmul(ps[0:HD, 6, g * P:g * P + w.stop - w.start], v, pT[:, w],
                                       start=kb == 0, stop=kb == nk // P - 1)
                mm.then_inc(o_ready, 1)
                n.next("o_copied")

            def slab(at):
                nonlocal slot
                k = at % KT
                if k % 4 == 0:
                    u, slot, _ = n.unit()
                    pe.wait_ge(lo_ready, u + 1)
                for b in range(4):
                    if k == 0 and b in (0, 2):
                        pe.wait_ge(half_freed, n.now("half_freed", -1 if b == 0 else 0))
                    mm = three(ps[:, b, :], (w_hi[:, slot, k % 4, b * P:(b + 1) * P], w_lo[:, slot, k % 4, b * P:(b + 1) * P]),
                               (h_hi[:, k, :], h_lo[:, k, :]), True, k == 0, k == KT - 1)
                    if k == KT - 1 and b in (1, 3):
                        mm.then_inc(half_ready, 1)
                if k == 3:
                    mm.then_inc(weights_used, 1)
                if k == KT - 1:
                    n.next("half_freed", 2)

            slot = 0
            scores(0)
            for j, job in enumerate(JOBS):
                if j + 1 < len(JOBS):
                    scores(j + 1)
                for at in range(DONE[j], DONE[j] + EARLY[j]):
                    slab(at)
                if job[0] != "index":
                    transposes(j)
                    for at in range(DONE[j] + EARLY[j], DONE[j + 1]):
                        slab(at)
                    values(j)

            swa, rest = fresh(1, 2)
            for _ in range(2):
                group((o_hi[:, 0:4, :], o_lo[:, 0:4, :]), (4,), True, operands=[swa])
                group((o_hi[:, 4:6, :], o_lo[:, 4:6, :]), (2,), True, operands=[rest])
                group((o_hi[:, 6:8, :], o_lo[:, 6:8, :]), (2,), True)
            groups(2, (m2_hi, m2_lo), (4, 4), False, new=(2, 4))
            norm_transposes(TT)
            for c in range(2):
                groups(4, h, (4, 4), True, new=() if c else (4, 8))
                groups(2, hid, (4, 4, 4, 4), False, new=(2, 4, 6, 8))

        @block.scalar
        def _(act):
            n = Tally()

            def split(units):
                for j in range(units):
                    _, slot, landed = n.unit()
                    if j:
                        act.wait_ge(weights_used, n.next("weights_used"))
                    elif n.i is not None or n.now("half_ready"):
                        act.wait_ge(half_ready, n.now("half_ready"))
                    act.wait_ge(raw_ready[slot], landed)
                    act.activation(w_hi[:, slot], raw[:, slot], ACT.Copy).then_inc(hi_ready, 1)

            def complete():
                act.wait_ge(half_ready, n.next("half_ready"))

            def passed(halves=2):
                n.next("half_ready", halves)
                n.next("half_freed", halves)

            def dve_groups(turns, units):
                with n.loop(act, turns, unit=units, weights_used=units - 1, half_ready=2, half_freed=2):
                    split(units)
                    passed()

            def copy_groups(turns, dst):
                with n.loop(act, turns, unit=2, weights_used=1, half_ready=2, half_freed=2) as i:
                    split(2)
                    for hf in range(2):
                        complete()
                        to = dst(i, hf)
                        act.activation(to, ps[:, 2 * hf:2 * hf + 2, 0:to.shape[2]], ACT.Copy).then_inc(half_freed, 1)
                        n.next("half_freed")

            def high(dst, src):
                act.wait_ge(prod_ready, n.next("prod_ready"))
                act.activation(dst, src, ACT.Copy).then_inc(acthi_ready, 1)

            def root():
                act.wait_ge(var_ready, n.next("var_ready"))
                act.activation(ROOT, REC, ACT.Sqrt).then_inc(root_ready, 1)

            def squares(src):
                act.activation(stat[:, 96:97], ident[:, 0:1], ACT.Sqrt)
                if n.now("half_freed"):
                    act.wait_ge(half_freed, n.now("half_freed", -1))
                for t in range(2):
                    act.activation(ps[:, 4 + 2 * t:6 + 2 * t, :],
                                   src[:, t, :].rearrange("p (a b) -> p a b", a=2), ACT.Square,
                                   accum_out=SS[:, t:t + 1]).then_inc(sq_ready, 1)
                root()

            def norm(src, tiles, gain):
                squares(src)
                act.wait_ge(xn_used, n.next("xn_used", tiles))
                for k in range(KT):
                    act.activation(h_hi[:, k, 0:tiles * P], ps[:, k, 0:tiles * P], ACT.Copy,
                                   scale=cols[:, gain + k:gain + k + 1]).then_inc(acthi_ready, 1)

            def gate_groups(turns, dst, bias, tile0=0):
                with n.loop(act, turns, unit=2, weights_used=1, half_ready=2, half_freed=2) as i:
                    split(2)
                    for b in range(4):
                        if b % 2 == 0:
                            complete()
                        a = act.activation(dst[:, bass.ds(i * 4 + (b + tile0), 1), :], ps[:, b:b + 1, :], ACT.Sigmoid,
                                           bias=cols[:, bass.ds(i * 4 + (b + bias), 1)])
                        if b % 2:
                            a.then_inc(half_freed, 1)
                            n.next("half_freed")

            def gate_up(i, tile0):
                split(2)
                complete()
                act.activation(tmp[:, 0], ps[:, 0:2, :], ACT.Silu).then_inc(half_freed, 1)
                n.next("half_ready")
                act.wait_ge(half_freed, n.next("half_freed", 2))
                act.activation(hid_hi[:, bass.ds(i * 2 + tile0, 2), :], tmp[:, 1], ACT.Copy).then_inc(acthi_ready, 1)

            def gates_up(turns, tile0):
                with n.loop(act, turns, unit=2, weights_used=1, half_ready=2, half_freed=2) as i:
                    gate_up(i, tile0)

            def ffn(gain, first=0):
                norm(x, TT, gain)
                if first:
                    gate_up(0, 0)
                gates_up(8 - first, 2 * first)
                dve_groups(2, 4)
                gates_up(3, 0)
                dve_groups(2, 2)

            act.wait_ge(raw_ready[0], n.unit()[2])
            act.activation(w_hi[:, 0], raw[:, 0], ACT.Copy).then_inc(hi_ready, 1)
            act.wait_ge(x_in, 16 * TT)
            act.wait_ge(cols_ready, 2)
            ffn(COL["ff1_norm"], 1)

            norm(x, TT, COL["mix_norm"])
            with n.loop(act, 2, unit=2, weights_used=1, half_ready=2, half_freed=2) as i:
                split(2)
                for t in range(TT):
                    if t % 2 == 0:
                        complete()
                    a = act.activation(vg[:, bass.ds(i * 4, 4), t, :],
                                       ps[:, t, :].rearrange("p (c k) -> p c k", c=4), ACT.Gelu)
                    if t % 2:
                        a.then_inc(half_freed, 1)
                        n.next("half_freed")
            for dst in (qT, kT):
                with n.loop(act, 2, unit=2, weights_used=1, half_ready=2, half_freed=2, var_ready=1) as i:
                    split(2)
                    root()
                    for hf in range(2):
                        complete()
                        act.activation(dst[:, bass.ds(i * 4 + 2 * hf, 2), :], ps[:, 2 * hf:2 * hf + 2, :],
                                       ACT.Copy).then_inc(half_freed, 1)
                        n.next("half_freed")
            copy_groups(2, lambda i, hf: v_tok[:, 2 * hf:2 * hf + 2, bass.ds(i * BANK, BANK)])
            for j in range(KT):
                act.wait_ge(mix_ready, j + 1)
                act.activation(vg[:, j].rearrange("p n t -> p (n t)"), ps[:, 4 + j % 4, :], ACT.Copy).then_inc(mix_copied, 1)
            with n.loop(act, 2, unit=2, weights_used=1, half_ready=2, half_freed=2, prod_ready=2) as i:
                split(2)
                for hf in range(2):
                    complete()
                    act.activation(tmp[:, 0], ps[:, 2 * hf:2 * hf + 2, :], ACT.Gelu).then_inc(half_freed, 1)
                    n.next("half_freed")
                    high(ya_hi[:, bass.ds(i * 4 + 2 * hf, 2), :], tmp[:, 1])
            act.wait_ge(operand_ready, 8 + 11 + 8 + 4)
            gate_groups(2, merged, COL["b_gate"])
            dve_groups(2, 2)

            def sigmoids(hh):
                for b in range(TT):
                    nk = P * (b + 1)
                    act.wait_ge(z_ready, n.next("z_ready"))
                    act.activation(beta[:, hh, OB[b]:OB[b] + nk], ps[:, 4 + b, 0:nk], ACT.Sigmoid, scale=SCALE)
                    act.activation(keep[:, hh, OB[b] + b:OB[b] + b + nk], ps[:, 4 + b, 0:nk], ACT.Sigmoid,
                                   scale=-SCALE).then_inc(sig_ready, 1)

            def weights_out():
                act.wait_ge(wT_ready, n.next("wT_ready"))
                act.wait_ge(pv_done, n.now("pv_done"))
                n.next("pv_done")
                act.activation(wT[:, 0:512], ps[:, 0, :], ACT.Copy)
                act.activation(wT[:, 512:1280].rearrange("p (a b) -> p a b", a=2), ps[:, 1:3, 0:384],
                               ACT.Copy).then_inc(wT_copied, 1)

            sigmoids(0)
            with n.loop(act, KT - 1, z_ready=8, wT_ready=2, pv_done=2):
                for hh in range(2):
                    sigmoids(1 - hh)
                    weights_out()
            sigmoids(1)
            weights_out()
            weights_out()

            gate_groups(2, gate_b, COL["b_gate"] + 8)
            act.wait_ge(o_copied, 1 + KT)
            for j in range(2):
                act.activation(h_hi[:, 4 * j:4 * j + 4, :], qT[:, 4 * j:4 * j + 4, :], ACT.Copy).then_inc(acthi_ready, 1)
            with n.loop(act, 2, unit=2, weights_used=1, half_ready=2, half_freed=2, prod_ready=2) as i:
                split(2)
                for hf in range(2):
                    passed(1)
                    high(m_hi[:, bass.ds(i * 4 + 2 * hf, 2), :], merged[:, bass.ds(i * 4 + 2 * hf, 2), :])
            dve_groups(2, 2)
            ffn(COL["ff2_norm"])

            squares(x)
            act.wait_ge(rows_in, 48)
            act.wait_ge(out_ready, TT)
            norm(mem_tok, M_LEN // P, COL["g_mem_2"])
            split(2)
            complete()
            act.activation(memT[:], ps[:, 0:2, 0:256], ACT.Copy).then_inc(half_freed, 1)
            complete()
            act.activation(memv[:], ps[:, 2:4, 0:256], ACT.Copy).then_inc(half_freed, 1)
            n.next("half_freed", 2)
            norm(x, TT, COL["g_mix_2"])
            copy_groups(2, lambda i, hf: proj[:, 2 * hf:2 * hf + 2, bass.ds(i * BANK, BANK)])
            copy_groups(2, lambda i, hf: proj[:, 2 * hf:2 * hf + 2, bass.ds(i * 354 + 1024, 354)])

            act.wait_ge(trig_ready, 1)
            act.activation(sin_t, r_sin, ACT.Sin)
            act.activation(cos_t, r_cos, ACT.Sin).then_inc(sin_ready, 1)
            for j in range(len(TILE_COLS)):
                act.wait_ge(tr_ready, j + 1)
                act.activation(qkT[:, j, :], ps[:, j % 8, :], ACT.Copy).then_inc(tr_copied, 1)

            between = [0, 0]

            def stream(done):
                while between[0] < 2 * GROUPS_BETWEEN and 4 * between[0] <= done:
                    if between[0] and between[0] % 2 == 0:
                        gates_out(between[1])
                        between[1] += 1
                    between[0] += 1
                    _, slot, landed = n.unit()
                    if between[0] % 2 == 0:
                        act.wait_ge(weights_used, n.next("weights_used"))
                    else:
                        act.wait_ge(half_ready, n.now("half_ready"))
                    act.wait_ge(raw_ready[slot], landed)
                    act.activation(w_hi[:, slot], raw[:, slot], ACT.Copy).then_inc(hi_ready, 1)

            def gates_out(i):
                for b in range(4):
                    if b % 2 == 0:
                        complete()
                    c = COL["b_gate_2"] + 4 * i + b
                    a = act.activation(gates2[:, 4 * i + b, :], ps[:, b, :], ACT.Sigmoid, bias=cols[:, c:c + 1])
                    if b % 2:
                        a.then_inc(half_freed, 1)
                        n.next("half_freed")

            z0 = n.now("z_ready")
            for j, (kind, b, c, nk) in enumerate(JOBS):
                stream(DONE[j])
                if kind == "index":
                    act.wait_ge(z_ready, z0 + j + 1)
                    act.wait_ge(prob_ready, n.now("prob_ready"))
                    act.activation(flat.rearrange("p (h s) -> p h s", h=4)[:, 2 * c:2 * c + 2, 0:nk],
                                   ps[:, 4:6, 0:nk], ACT.Relu).then_inc(z_freed, 1)
                    continue
                heads = heads_of(kind, c)
                act.wait_ge(logit_ready, n.next("logit_ready"))
                for g, (_, at) in enumerate(sorted(heads, key=lambda x: x[1])):
                    e = act.activation(logits[:, at:at + nk], logits[:, at:at + nk], ACT.Exp,
                                       bias=neg[:, g:g + 1], accum_out=tot[:, g:g + 1])
                if kind == "window":
                    e = act.activation(snk_e[:, 0:4], snk_e[:, 0:4], ACT.Exp)
                e.then_inc(exp_ready, 1)
                n.next("prob_ready")
                act.wait_ge(pT_ready, n.next("pT_ready"))
                w = (nk // P) * len(heads) * P
                act.activation(pT[:, 0:w], ps[:, 6:8, :].rearrange("p a b -> p (a b)")[:, 0:w],
                               ACT.Copy).then_inc(pT_copied, 1)
            gates_out(GROUPS_BETWEEN - 1)

            act.wait_ge(o_copied, 1 + KT + 20)
            for j in range(2):
                act.activation(o_hi[:, 4 * j:4 * j + 4, :], oT[:, 4 * j:4 * j + 4, :], ACT.Copy).then_inc(acthi_ready, 1)
            for c in range(2):
                for kind in range(3):
                    split(1)
                    for hf in range(2):
                        passed(1)
                        if kind == 2:
                            t = slice(4 * c + 2 * hf, 4 * c + 2 * hf + 2)
                            high(m2_hi[:, t, :], merged2[:, t, :])
            dve_groups(2, 2)
            norm(x, TT, COL["g_mlp_2"])
            for c in range(2):
                with n.loop(act, 4, unit=2, weights_used=1, half_ready=2, half_freed=2, prod_ready=2) as i:
                    split(2)
                    for hf in range(2):
                        complete()
                        act.activation(tmp[:, 0], ps[:, 2 * hf:2 * hf + 2, :], ACT.Relu).then_inc(half_freed, 1)
                        n.next("half_freed")
                        high(hid_hi[:, bass.ds(i * 4 + 2 * hf, 2), :], tmp[:, 1])
                if c == 0:
                    dve_groups(2, 4)
                else:
                    split(4)
                    passed()
                    split(3)
                    passed()
            squares(x)

        @block.vector
        def _(dve):
            n = Tally()

            def step(ins):
                ins.then_inc(dve_step, 1)
                dve.wait_ge(dve_step, n.next("dve_step"))

            def split(units):
                for _ in range(units):
                    _, slot, _ = n.unit()
                    dve.wait_ge(hi_ready, n.next("hi_ready"))
                    dve.tensor_tensor(w_lo[:, slot], raw[:, slot], w_hi[:, slot].bitcast(F32),
                                      ALU.subtract).then_inc(lo_ready, 1)

            def complete():
                dve.wait_ge(half_ready, n.next("half_ready"))

            def freed(ins):
                ins.then_inc(half_freed, 1)
                n.next("half_freed")

            def low(dst, src, hi):
                dve.wait_ge(acthi_ready, n.next("acthi_ready"))
                dve.tensor_tensor(dst, src, hi.bitcast(F32), ALU.subtract).then_inc(operand_ready, 1)
                n.next("operand_ready")

            def act_groups(turns):
                with n.loop(dve, turns, unit=2, hi_ready=2, half_ready=2, half_freed=2):
                    split(2)
                    n.next("half_ready", 2)
                    n.next("half_freed", 2)

            def rsqrt(w, src, scale):
                V, C, Q, N_, O = (a[:, 0:w] for a in (VAR, REC, ROOT, NEW, R))
                step(dve.tensor_scalar(V, src, scale, EPS, ALU.mult, ALU.add))
                dve.reciprocal(C, V).then_inc(var_ready, 1)
                dve.wait_ge(root_ready, n.next("root_ready"))
                step(dve.tensor_tensor(N_, Q, Q, ALU.mult))
                step(dve.tensor_tensor(N_, N_, V, ALU.mult))
                step(dve.tensor_scalar(N_, N_, -0.5, 1.5, ALU.mult, ALU.add))
                step(dve.tensor_tensor(O, Q, N_, ALU.mult))

            def squares(src, tiles):
                if tiles > 2 and n.now("half_freed"):
                    dve.wait_ge(half_freed, n.now("half_freed"))
                for t in range(2, tiles):
                    ins = dve.tensor_tensor_reduce(ps[:, 2 * t - 4:2 * t - 2, :].rearrange("p a b -> p (a b)"),
                                                   src[:, t, :], src[:, t, :], 1.0, 0.0, ALU.mult, ALU.add,
                                                   SS[:, t:t + 1])
                if tiles > 2:
                    step(ins)
                dve.wait_ge(sq_ready, n.next("sq_ready", 2))
                rsqrt(4, SS, 1.0 / D)

            def norm(src, tiles, gain):
                squares(src, tiles)
                for t in range(tiles):
                    if t >= 2:
                        dve.wait_ge(xn_used, n.now("xn_used", t - 1))
                    dve.tensor_scalar(tmp[:, t % 2].rearrange("p a b -> p (a b)"), src[:, t, :], R[:, t:t + 1],
                                      None, ALU.mult).then_inc(xn_ready, 1)
                n.next("xn_used", tiles)
                for k in range(KT):
                    dve.wait_ge(acthi_ready, n.next("acthi_ready"))
                    dve.scalar_tensor_tensor(out=h_lo[:, k, 0:tiles * P], in0=ps[:, k, 0:tiles * P],
                                             scalar=cols[:, gain + k:gain + k + 1],
                                             in1=h_hi[:, k, 0:tiles * P].bitcast(F32), op0=ALU.mult,
                                             op1=ALU.subtract).then_inc(operand_ready, 1)
                    n.next("operand_ready")

            def last_norm(rows_at):
                squares(x, TT)
                dve.wait_ge(rows_in, rows_at)
                for t in range(TT):
                    dve.scalar_tensor_tensor(out=x[:, t, :], in0=x[:, t, :], scalar=R[:, t:t + 1], in1=rows[:],
                                             op0=ALU.mult, op1=ALU.mult).then_inc(out_ready, 1)

            def gate_up(turns):
                with n.loop(dve, turns, unit=2, hi_ready=2, half_ready=2, half_freed=2, acthi_ready=1, operand_ready=1) as i:
                    split(2)
                    dve.wait_ge(half_freed, n.next("half_freed"))
                    n.next("half_ready")
                    complete()
                    freed(dve.tensor_tensor(tmp[:, 1], tmp[:, 0], ps[:, 2:4, :], ALU.mult))
                    low(hid_lo[:, bass.ds(i * 2, 2), :], tmp[:, 1], hid_hi[:, bass.ds(i * 2, 2), :])

            def residual(turns, units, scale):
                with n.loop(dve, turns, unit=units, hi_ready=units, half_ready=2, half_freed=2) as i:
                    split(units)
                    add(i, scale)

            def add(i, scale):
                for hf in range(2):
                    complete()
                    to = x[:, 2 * hf:2 * hf + 2, bass.ds(i * BANK, BANK)]
                    freed(dve.scalar_tensor_tensor(out=to, in0=ps[:, 2 * hf:2 * hf + 2, :], scalar=scale, in1=to,
                                                   op0=ALU.mult, op1=ALU.add))

            def ffn(gain):
                norm(x, TT, gain)
                gate_up(8)
                residual(2, 4, 0.5)
                gate_up(3)
                residual(2, 2, 0.5)

            dve.wait_ge(cols_tr, 1)
            dve.tensor_copy(cols[:], ps[:, 4, 0:NCOLS]).then_inc(cols_ready, 1)
            wsrc = ps[:, 5, :].rearrange("p (g t) -> p g t", g=4)
            dve.tensor_copy(wsT[0:64], wsrc[0:64]).then_inc(wT_copied, 1)
            dve.memset(wsT[64:128, :, 0:64], 0.0).then_inc(o_copied, 1)
            dve.tensor_copy(wsT[64:128, :, 64:128], wsrc[64:128, :, 64:128]).then_inc(cols_ready, 1)
            split(1)
            dve.wait_ge(x_in, 16 * TT)
            ffn(COL["ff1_norm"])

            norm(x, TT, COL["mix_norm"])
            act_groups(2)
            with n.loop(dve, 4, unit=2, hi_ready=2, half_ready=2, half_freed=2, dve_step=9, root_ready=1) as i:
                split(1)
                dve.wait_ge(half_freed, 34)
                tiles = [vg[:, 2 * g:2 * g + 2, bass.ds(i, 1), :].rearrange("p c o k -> p (c o) k") for g in range(4)]
                for g in range(4):
                    ins = dve.bn_stats(bn[:, g, :], tiles[g])
                step(ins)
                dve.tensor_copy(NEW, SS)
                for g in range(4):
                    ins = dve.bn_aggr(mv[:, 2 * g:2 * g + 2], bn[:, g, :])
                step(ins)
                rsqrt(4, mv.rearrange("p (g s) -> p g s", s=2)[:, :, 1], 1.0)
                for g in range(4):
                    ins = dve.tensor_scalar(tiles[g], tiles[g], mv[:, 2 * g:2 * g + 1], R[:, g:g + 1],
                                            ALU.subtract, ALU.mult)
                step(ins)
                whole = vg[:, :, bass.ds(i, 1), :].rearrange("p c o k -> p (c o) k")
                step(dve.tensor_tensor(whole, whole, ln_g[:].rearrange("p (c k) -> p c k", c=KT), ALU.mult))
                dve.tensor_tensor(whole, whole, ln_b[:].rearrange("p (c k) -> p c k", c=KT),
                                  ALU.add).then_inc(ln_ready, 1)
                split(1)
                n.next("half_ready", 2)
                n.next("half_freed", 2)
            act_groups(2)
            with n.loop(dve, 2, unit=2, hi_ready=2, half_ready=2, half_freed=2, acthi_ready=2, operand_ready=2) as i:
                split(2)
                for hf in range(2):
                    t = bass.ds(i * 4 + 2 * hf, 2)
                    dve.wait_ge(mix_copied, KT)
                    n.next("half_ready")
                    dve.wait_ge(half_freed, n.next("half_freed"))
                    dve.wait_ge(operand_ready, n.now("operand_ready"))
                    dve.tensor_tensor(tmp[:, 1], tmp[:, 0], merged[:, t, :], ALU.mult).then_inc(prod_ready, 1)
                    low(ya_lo[:, t, :], tmp[:, 1], ya_hi[:, t, :])
            act_groups(2)
            with n.loop(dve, 2, unit=2, hi_ready=2, half_ready=2, half_freed=2) as i:
                split(2)
                for hf in range(2):
                    t = bass.ds(i * 4 + 2 * hf, 2)
                    complete()
                    freed(dve.tensor_tensor(merged[:, t, :], merged[:, t, :], ps[:, 2 * hf:2 * hf + 2, :], ALU.mult))

            for hh in range(2):
                for b in range(TT):
                    at = OB[b] + b + P * (b + 1)
                    ins = dve.memset(keep[:, hh, at:at + 1], 1.0)
            step(ins)

            def scans(hh):
                for b in range(TT):
                    nk, at = P * (b + 1), OB[b] + b
                    dve.wait_ge(masked_ready, n.next("masked_ready", 2))
                    k = keep[:, hh, at:at + nk][:, ::-1]
                    step(dve.tensor_tensor_scan(k, k, k, 1.0, ALU.mult, ALU.bypass))
                    w = beta[:, hh, OB[b]:OB[b] + nk]
                    dve.tensor_tensor(w, w, keep[:, hh, at + 1:at + 1 + nk], ALU.mult).then_inc(w_ready, 1)

            def pair_out(tile):
                dve.wait_ge(pv_done, n.next("pv_done", 2))
                dve.tensor_copy(qT[:, tile, :], ps[:, 3:4, :]).then_inc(o_copied, 1)

            scans(0)
            scans(1)
            with n.loop(dve, KT - 1, masked_ready=16, dve_step=8, pv_done=2) as i:
                scans(0)
                pair_out(bass.ds(i, 1))
                scans(1)
            pair_out(slice(KT - 1, KT))

            act_groups(2)
            for j in range(2):
                t = slice(4 * j, 4 * j + 4)
                low(h_lo[:, t, :], qT[:, t, :], h_hi[:, t, :])
            with n.loop(dve, 2, unit=2, hi_ready=2, half_ready=2, half_freed=2, acthi_ready=2, operand_ready=2) as i:
                split(2)
                for hf in range(2):
                    t = bass.ds(i * 4 + 2 * hf, 2)
                    complete()
                    dve.tensor_tensor(tmp[:, 0], gate_b[:, t, :], ps[:, 2 * hf:2 * hf + 2, :],
                                      ALU.mult).then_inc(half_freed, 1)
                    dve.wait_ge(half_freed, n.next("half_freed"))
                    dve.tensor_tensor(merged[:, t, :], merged[:, t, :], tmp[:, 0], ALU.add).then_inc(prod_ready, 1)
                    low(m_lo[:, t, :], merged[:, t, :], m_hi[:, t, :])
            residual(2, 2, 1.0)
            ffn(COL["ff2_norm"])

            last_norm(48)
            norm(mem_tok, M_LEN // P, COL["g_mem_2"])
            split(2)
            n.next("half_ready", 2)
            n.next("half_freed", 2)
            norm(x, TT, COL["g_mix_2"])
            step(dve.tensor_copy(pos_f, pos_i[:]))
            for t in range(TT):
                ins = dve.tensor_scalar(ang[:, 32 * t:32 * t + 32], freq, pos_f[:, t:t + 1], None, ALU.mult)
            step(ins)
            step(dve.tensor_scalar(turns, ang, 1.0 / (2 * 3.141592653589793), ROUND, ALU.mult, ALU.add))
            step(dve.tensor_scalar(turns, turns, -ROUND, None, ALU.add))
            for part in TWO_PI:
                step(dve.scalar_tensor_tensor(out=ang, in0=turns, scalar=-part, in1=ang, op0=ALU.mult, op1=ALU.add))
            dve.tensor_scalar(r_sin, ang, PI, -PI, ALU.min, ALU.max)
            step(dve.tensor_scalar(r_cos, ang, 3.141592653589793 / 2, None, ALU.add))
            step(dve.tensor_scalar(turns, r_cos, 3.141592653589793, -2 * 3.141592653589793, ALU.is_gt, ALU.mult))
            step(dve.tensor_tensor(r_cos, r_cos, turns, ALU.add))
            dve.tensor_scalar(r_cos, r_cos, PI, -PI, ALU.min, ALU.max).then_inc(trig_ready, 1)
            act_groups(4)

            dve.wait_ge(sin_ready, 1)
            dve.wait_ge(half_freed, n.now("half_freed"))
            for c0, heads in ((0, 10), (768, 5), (Q_I, 5)):
                both = proj[:, :, c0:c0 + HD * heads].rearrange("p t (h w) -> p t h w", w=HD)
                x1, x2 = both[:, :, :, 0:32], both[:, :, :, 32:64]
                c, s = (a.rearrange("p (t w) -> p t w", t=TT).unsqueeze(2).broadcast_to([P, TT, heads, 32])
                        for a in (cos_t, sin_t))
                a1, a2, a3, a4 = (rope_t[:, j, 0:TT * heads * 32].rearrange("p (t h w) -> p t h w", t=TT, h=heads)
                                  for j in range(4))
                dve.tensor_tensor(a1, x1, c, ALU.mult)
                dve.tensor_tensor(a2, x2, s, ALU.mult)
                dve.tensor_tensor(a3, x2, c, ALU.mult)
                step(dve.tensor_tensor(a4, x1, s, ALU.mult))
                dve.tensor_tensor(x1, a1, a2, ALU.subtract)
                step(dve.tensor_tensor(x2, a3, a4, ALU.add))
            for j, c0 in enumerate((512, 576, K_D, K_I)):
                for r in range(2):
                    dve.tensor_copy(proj[:, :, KDUP + P * j + HD * r:KDUP + P * j + HD * r + HD], proj[:, :, c0:c0 + HD])
            dve.tensor_copy(vals[:, :, 0:2 * HD], proj[:, :, V_S:V_S + 2 * HD])
            dve.tensor_copy(vals[:, :, 2 * HD:3 * HD], proj[:, :, V_D:V_D + HD])
            dve.tensor_scalar(w_idx, proj[:, :, W_I:W_I + 4], 1.0 / 16, None, ALU.mult).then_inc(rope_ready, 1)

            z0 = 8 * KT

            def outputs(j):
                kind, b, c, nk = JOBS[j]
                dve.wait_ge(o_ready, n.next("o_ready"))
                tiles = 1 if kind == "chosen" else 2
                t0 = {"window": 2 * c, "chosen": 4 + c, "memory": 6}[kind]
                src = ps[0:HD, 6, 0:2 * P * tiles].rearrange("p (a e t) -> p a e t", a=tiles, e=2)
                for e in range(2):
                    ins = dve.tensor_copy(oT[HD * e:HD * e + HD, t0:t0 + tiles, b * P:(b + 1) * P], src[:, :, e, :])
                ins.then_inc(o_copied, 1)

            between = [0, 0]

            def stream(done):
                while between[0] < 2 * GROUPS_BETWEEN and 4 * between[0] <= done:
                    between[0] += 1
                    split(1)

            def choose(b, rounds, last):
                if not rounds:
                    return
                dve.wait_ge(causal_ready, b + 1)
                sc = flat[:, 0:P * (b + 1)]
                for r in range(rounds):
                    step(dve.max(mx8, sc))
                    step(dve.match_replace(sc, mx8, sc, TAKEN))
                if last:
                    step(dve.tensor_scalar(mask[:, 0:P * (b + 1)], sc, 10 * OUT_OF_REACH, MASKED, ALU.is_gt, ALU.mult))

            before = None
            for j, (kind, b, c, nk) in enumerate(JOBS):
                if kind == "index":
                    stream(DONE[j])
                    if c == 0:
                        continue
                    dve.wait_ge(z_freed, j + 1)
                    sc = flat[:, 0:nk]
                    step(dve.tensor_scalar(sc, sc, w_idx[:, b, 0:1], None, ALU.mult))
                    for g in range(1, 4):
                        ins = dve.scalar_tensor_tensor(out=sc, in0=flat[:, g * BANK:g * BANK + nk],
                                                       scalar=w_idx[:, b, g:g + 1], in1=sc, op0=ALU.mult, op1=ALU.add)
                        if g < 3:
                            step(ins)
                    ins.then_inc(iscore_ready, 1)
                    if before is not None:
                        outputs(before)
                        before = None
                    continue
                heads, row = (2, BANK) if kind == "chosen" else (4, 256)
                lg = logits[:].rearrange("p (h s) -> p h s", s=row)[:, :, 0:nk]
                z = ps[:, 4:6, :].rearrange("p a (c s) -> p (a c) s", s=row)[:, :, 0:nk]
                dve.wait_ge(z_ready, z0 + j + 1)
                dve.wait_ge(pT_ready, n.now("pT_ready"))
                n.next("pT_ready")
                if kind == "memory":
                    ins = dve.tensor_scalar(lg, z, SCALE, None, ALU.mult)
                else:
                    if kind == "chosen" and b == 0:
                        dve.wait_ge(causal_ready, 1)
                    if kind == "window":
                        dve.wait_ge(masks_made, 3)
                    m = swa_mask[:, 256 - nk:256] if kind == "window" else mask[:, 0:nk]
                    ins = dve.scalar_tensor_tensor(out=lg, in0=z, scalar=SCALE,
                                                   in1=m.unsqueeze(1).broadcast_to([P, heads, nk]),
                                                   op0=ALU.mult, op1=ALU.add)
                ins.then_inc(z_freed, 1)
                dve.wait_ge(z_freed, j + 1)
                step(dve.tensor_reduce(mx[:, 0:heads], lg, AX.X, ALU.max))
                if kind == "window":
                    sink = snk[:, 4 * c:4 * c + 4]
                    step(dve.tensor_tensor(mx[:, 0:4], mx[:, 0:4], sink, ALU.max))
                    dve.tensor_tensor(snk_e[:, 0:4], sink, mx[:, 0:4], ALU.subtract)
                dve.tensor_scalar(neg[:, 0:heads], mx[:, 0:heads], -1.0, None, ALU.mult).then_inc(logit_ready, 1)
                stream(DONE[j])
                choose(b + 1, CHOICE[j], kind == "memory")
                if before is not None:
                    outputs(before)
                before = j
                dve.wait_ge(exp_ready, n.next("exp_ready"))
                if kind == "window":
                    step(dve.tensor_tensor(tot[:, 0:4], tot[:, 0:4], snk_e[:, 0:4], ALU.add))
                step(dve.reciprocal(rec[:, 0:heads], tot[:, 0:heads]))
                dve.tensor_tensor(lg, lg, rec[:, 0:heads].unsqueeze(2).broadcast_to([P, heads, nk]),
                                  ALU.mult).then_inc(prob_ready, 1)
            outputs(before)
            n.next("half_ready", 2 * GROUPS_BETWEEN)
            n.next("half_freed", 2 * GROUPS_BETWEEN)

            for j in range(2):
                t = slice(4 * j, 4 * j + 4)
                low(o_lo[:, t, :], oT[:, t, :], o_hi[:, t, :])
            for c in range(2):
                for kind in range(3):
                    split(1)
                    for hf in range(2):
                        complete()
                        t = slice(4 * c + 2 * hf, 4 * c + 2 * hf + 2)
                        g = slice(8 * kind + 4 * c + 2 * hf, 8 * kind + 4 * c + 2 * hf + 2)
                        banks = ps[:, 2 * hf:2 * hf + 2, :]
                        if kind == 0:
                            freed(dve.tensor_tensor(merged2[:, t, :], gates2[:, g, :], banks, ALU.mult))
                            continue
                        dve.tensor_tensor(tmp[:, 0], gates2[:, g, :], banks, ALU.mult).then_inc(half_freed, 1)
                        dve.wait_ge(half_freed, n.next("half_freed"))
                        ins = dve.tensor_tensor(merged2[:, t, :], merged2[:, t, :], tmp[:, 0], ALU.add)
                        if kind == 1:
                            step(ins)
                        else:
                            ins.then_inc(prod_ready, 1)
                            low(m2_lo[:, t, :], merged2[:, t, :], m2_hi[:, t, :])
            residual(2, 2, 1.0)
            norm(x, TT, COL["g_mlp_2"])
            for c in range(2):
                with n.loop(dve, 4, unit=2, hi_ready=2, half_ready=2, half_freed=2, acthi_ready=2, operand_ready=2) as i:
                    split(2)
                    for hf in range(2):
                        t = bass.ds(i * 4 + 2 * hf, 2)
                        n.next("half_ready")
                        dve.wait_ge(half_freed, n.next("half_freed"))
                        dve.wait_ge(operand_ready, n.now("operand_ready"))
                        dve.tensor_tensor(tmp[:, 1], tmp[:, 0], tmp[:, 0], ALU.mult).then_inc(prod_ready, 1)
                        low(hid_lo[:, t, :], tmp[:, 1], hid_hi[:, t, :])
                if c == 0:
                    residual(2, 4, 1.0)
                else:
                    for i in range(2):
                        split(4 - i)
                        add(i, 1.0)
            last_norm(64)


_INS = ["x", "ff1_norm", "ff1_w_gate", "ff1_w_up", "ff1_w_down", "mix_norm", "w_in", "b_gate",
        "gmlp_ln_g", "gmlp_ln_b", "gmlp_w_s", "gmlp_b_s", "w_branch_a", "w_branch_b", "w_out",
        "ff2_norm", "ff2_w_gate", "ff2_w_up", "ff2_w_down", "final_norm", "mem_2", "positions_2",
        "g_mix_2", "w_in_2", "b_gate_2", "sinks_2", "g_mem_2", "w_mem_kv_2", "w_proj_swa_2",
        "w_proj_dsa_2", "w_proj_mem_2", "w_out_2", "g_mlp_2", "w_mlp_in_2", "w_mlp_out_2", "g_final_2"]


def kernel(**inputs):
    import numpy as np
    import concourse.bacc as bacc
    from concourse.bass_utils import run_bass_kernel_spmd

    nc = bacc.Bacc("TRN2", target_bir_lowering=False, num_devices=1)
    arrays, aps = {}, {}

    def give(name, a):
        arrays[f"in_{name}"] = a
        aps[name] = nc.dram_tensor(f"in_{name}", a.shape, mybir.dt.from_np(a.dtype), kind="ExternalInput").ap()

    for name in _INS:
        give(name, np.ascontiguousarray(inputs[name]))
    half = HD // 2
    give("inv_freq", np.power(np.float32(10000.0), -np.arange(half, dtype=np.float32) / np.float32(half)).astype(np.float32))
    shape = tuple(inputs["x"].shape)
    out = nc.dram_tensor("out_0", shape, F32, kind="ExternalOutput").ap()
    build(nc, aps, out)
    r = run_bass_kernel_spmd(nc, [arrays], core_ids=[0])
    return r.results[0]["out_0"]
```

```python
from contextlib import ExitStack

import concourse.bass as bass
from concourse import mybir
from concourse.alu_op_type import AluOpType as ALU

ACT = mybir.ActivationFunctionType
AX = mybir.AxisListType
F32 = mybir.dt.float32
FR = mybir.dt.float32r
I32 = mybir.dt.int32

P = 128
BANK = 512
HD = 64
EPS = 1e-6
SCALE = HD ** -0.5
MASKED = -1e30
OUT_OF_REACH = -1e37
TAKEN = -3e38
ROUND = 1.5 * 2.0 ** 23
TWO_PI = (6.28125, 1.9350051879882812e-03, 3.0199159819567e-07)
PI = 3.1415925


CREDIT = ("pv_done", "wT_copied", "o_copied")


class Tally:

    def __init__(self):
        self.steps, self.i, self.per = dict.fromkeys(CREDIT, 1), None, {}

    def now(self, key, add=0):
        per = self.per.get(key, 0)
        return self.i * per + (self.steps.get(key, 0) + add) if per else self.steps.get(key, 0) + add

    def next(self, key, by=1):
        assert self.i is None or key in self.per, key
        self.steps[key] = self.steps.get(key, 0) + by
        return self.now(key)

    def unit(self):
        u = self.next("unit") - 1
        c, per = self.steps["unit"] - 1, self.per.get("unit", 0)
        assert per % 2 == 0
        landed = self.i * (16 * per) + 32 * (c // 2 + 1) if per else 32 * (c // 2 + 1)
        return u, c % 2, landed

    def loop(self, eng, turns, **per):
        return _Loop(self, eng, turns, per)


class _Loop:
    def __init__(self, tally, eng, turns, per):
        self.t, self.turns, self.per = tally, turns, per
        self.ctx = eng.Fori(0, turns)

    def __enter__(self):
        self.t.i, self.t.per = self.ctx.__enter__(), self.per
        self.before = dict(self.t.steps)
        return self.t.i

    def __exit__(self, *a):
        t = self.t
        if a[0] is None:
            made = {k: n - self.before.get(k, 0) for k, n in t.steps.items()}
            assert {k: n for k, n in made.items() if n} == self.per, (made, self.per)
            for k, n in self.per.items():
                t.steps[k] = self.before.get(k, 0) + n * self.turns
        t.i, t.per = None, {}
        return self.ctx.__exit__(*a)


def build(nc, A, out):
    D, S = A["x"].shape[2], A["x"].shape[1]
    KT, TT = D // P, S // P
    M_LEN = A["mem_2"].shape[1]
    PCOLS = 1732
    V_S, K_D, V_D, Q_I, K_I, W_I, Q_M = 640, 1024, 1088, 1152, 1408, 1472, 1476
    KDUP = PCOLS
    TILE_COLS = [0, 128, 256, 384, 768, 896, Q_I, Q_I + 128, Q_M, Q_M + 128] + [KDUP + P * j for j in range(4)]
    QS, QD, QI, QM, KS, KD, KI = 0, 4, 6, 8, 10, 12, 13
    ROWS = [("ff1_norm", 8), ("mix_norm", 8), ("ff2_norm", 8), ("g_mix_2", 8), ("g_mem_2", 8),
            ("g_mlp_2", 8), ("b_gate", 16), ("b_gate_2", 24)]
    COL = {name: sum(r for _, r in ROWS[:j]) for j, (name, _) in enumerate(ROWS)}
    NCOLS = sum(r for _, r in ROWS)
    HALVES_FF2, HALVES_MLP = 70, 138
    OB = [P * b * (b + 1) // 2 for b in range(TT)]

    ctx = ExitStack()
    with ctx:
        def sb(name, shape, dt=F32):
            return ctx.enter_context(nc.sbuf_tensor(name, shape, dt))

        def sem(name):
            return ctx.enter_context(nc.semaphore(name))

        x = sb("resid", [P, TT, D])
        h_hi = sb("h_hi", [P, KT, S], FR)
        h_lo = sb("h_lo", [P, KT, S], FR)
        raw = sb("raw", [P, 2, 4, BANK])
        w_hi = sb("w_hi", [P, 2, 4, BANK], FR)
        w_lo = sb("w_lo", [P, 2, 4, BANK], FR)
        tmp = sb("tmp", [P, 2, 2, BANK])
        ident = sb("ident", [P, P])
        cols = sb("cols", [P, NCOLS])
        wsT = sb("wsT", [P, 4, P])
        swa_mask = wsT[:, 0:2, :].rearrange("p a b -> p (a b)")
        before, after = wsT[:, 0, :], wsT[:, 1, :]
        stat = sb("stat", [P, 100])
        pos_i = sb("pos_i", [P, TT], I32)
        memT = sb("memT", [P, 2, M_LEN])
        memv = sb("memv", [P, 2, 4 * HD])
        SS, VAR, REC, ROOT, NEW, R = (stat[:, 4 * j:4 * j + 4] for j in range(6))
        mv = stat[:, 24:32]
        bn = stat[:, 32:56].rearrange("p (g s) -> p g s", g=4)
        mx, neg, tot, snk, snk_e = (stat[:, 56 + 8 * j:64 + 8 * j] for j in range(5))
        rec, mx8 = stat[:, 24:32], stat[:, 48:56]
        w_idx = stat[:, 32:48].rearrange("p (t h) -> p t h", t=TT)

        def layout(gap, *tensors):
            with ExitStack() as c:
                if gap:
                    c.enter_context(nc.sbuf_tensor("gap_" + tensors[0][0], [P, gap], F32))
                return [c.enter_context(nc.sbuf_tensor(n, s, d)) for n, s, d in tensors]

        T16 = KT * S
        hid_hi, hid_lo, rows, mem_tok = layout(
            0, ("hid_hi", [P, 16, S], FR), ("hid_lo", [P, 16, S], FR), ("rows", [P, D], F32),
            ("mem_tok", [P, 2, D], F32))
        qT, kT, v_tok, vg, ya_hi, ya_lo = layout(
            0, ("qT", [P, KT, S], F32), ("kT", [P, KT, S], F32), ("v_tok", [P, TT, D], F32),
            ("vg", [P, KT, TT, P], F32), ("ya_hi", [P, KT, S], FR), ("ya_lo", [P, KT, S], FR))
        ln_g, ln_b, col_rows, ws_raw, bs_row, ones_row = layout(
            4 * T16, ("ln_g", [P, D], F32), ("ln_b", [P, D], F32), ("col_rows", [P, P], F32),
            ("ws_raw", [P, 4, P], F32), ("bs_row", [1, 4 * P], F32), ("ones_row", [1, P], F32))
        beta, keep, wT, pair = layout(
            4 * T16, ("beta", [P, 2, 1280], F32), ("keep", [P, 2, 1284], F32), ("wT", [P, 1280], F32),
            ("pair", [P, 3, S], F32))
        pairs = [pair, tmp[:, :, :, :].rearrange("p a b c -> p (a b) c")]
        m_hi, m_lo = layout(T16, ("m_hi", [P, KT, S], FR), ("m_lo", [P, KT, S], FR))
        gate_b, = layout(4 * T16, ("gate_b", [P, KT, S], F32))
        merged = vg[:, :, :, :].rearrange("p k n t -> p k (n t)")
        proj, qkT = layout(0, ("proj", [P, TT, PCOLS + 512], F32), ("qkT", [P, 14, S], F32))
        rope_t, trig = layout(4 * T16, ("rope_t", [P, 4, 1280], F32), ("trig", [P, 7, TT * 32], F32))
        logits, pT, vals = layout(
            4 * T16, ("logits", [P, 1024], F32), ("pT", [P, 1024], F32), ("vals", [P, TT, 3 * HD], F32))
        mask, = layout(4 * T16 + 2048 + 3 * TT * HD, ("mask", [P, S], F32))
        oT, = layout(4 * T16 + 4096, ("oT", [P, 8, S], F32))
        o_hi, o_lo = layout(4 * T16, ("o_hi", [P, 8, S], FR), ("o_lo", [P, 8, S], FR))
        gates2, merged2 = layout(0, ("gates2", [P, 24, S], F32), ("merged2", [P, KT, S], F32))
        m2_hi, m2_lo = layout(0, ("m2_hi", [P, KT, S], FR), ("m2_lo", [P, KT, S], FR))
        flat = tmp[:, :, :, :].rearrange("p a b c -> p (a b c)")
        ang, turns, r_sin, r_cos, sin_t, cos_t, misc = (trig[:, j, :] for j in range(7))
        freq, pos_f = misc[:, 0:32], misc[:, 32:36]

        ps = ctx.enter_context(nc.psum_tensor("ps", [P, 8, BANK], F32))

        x_in = sem("x_in")
        const_in = sem("const_in")
        late_in = sem("late_in")
        rows_in = sem("rows_in")
        raw_ready = [sem("raw_ready0"), sem("raw_ready1")]
        hi_ready = sem("hi_ready")
        lo_ready = sem("lo_ready")
        weights_used = sem("weights_used")
        half_ready = sem("half_ready")
        half_freed = sem("half_freed")
        prod_ready = sem("prod_ready")
        acthi_ready = sem("acthi_ready")
        operand_ready = sem("operand_ready")
        made = sem("made")
        masks_made = sem("masks_made")
        cols_tr = sem("cols_tr")
        cols_ready = sem("cols_ready")
        sq_ready = sem("sq_ready")
        var_ready = sem("var_ready")
        root_ready = sem("root_ready")
        xn_ready = sem("xn_ready")
        xn_used = sem("xn_used")
        out_ready = sem("out_ready")
        dve_step = sem("dve_step")
        ln_ready = sem("ln_ready")
        mix_ready = sem("mix_ready")
        mix_copied = sem("mix_copied")
        pair_ready = sem("pair_ready")
        v_ready = sem("v_ready")
        z_ready = sem("z_ready")
        sig_ready = sem("sig_ready")
        masked_ready = sem("masked_ready")
        w_ready = sem("w_ready")
        wT_ready = sem("wT_ready")
        wT_copied = sem("wT_copied")
        pv_done = sem("pv_done")
        o_copied = sem("o_copied")
        trig_ready = sem("trig_ready")
        sin_ready = sem("sin_ready")
        rope_ready = sem("rope_ready")
        tr_ready = sem("tr_ready")
        tr_copied = sem("tr_copied")
        z_freed = sem("z_freed")
        iscore_ready = sem("iscore_ready")
        choice_made = sem("choice_made")
        causal_ready = sem("causal_ready")
        logit_ready = sem("logit_ready")
        exp_ready = sem("exp_ready")
        prob_ready = sem("prob_ready")
        pT_ready = sem("pT_ready")
        pT_copied = sem("pT_copied")
        o_ready = sem("o_ready")
        stored = sem("stored")

        def kpn(name):
            return A[name][0].rearrange("(k p) n -> p k n", p=P)

        JOBS, CHOICE = [], []
        for b in range(TT):
            last = b == TT - 1
            if not last:
                JOBS += [("index", b + 1, c, P * (b + 2)) for c in range(2)]
                CHOICE += [0, 0]
            JOBS += [("window", b, c, P * min(b + 1, 2)) for c in range(2)]
            JOBS += [("chosen", b, c, P * (b + 1)) for c in range(2)] + [("memory", b, 0, M_LEN)]
            CHOICE += [0] * 5 if last else [3, 3, 3, 3, 4]
        EARLY = [0, 0, 1, 1, 1, 1, 0] + [0, 1, 1, 1, 1, 1, 0] + [0, 1, 1, 1, 0, 1, 1] + [1, 0, 1, 1, 1]
        LATE = [0, 0, 1, 1, 1, 1, 1] + [0, 0, 1, 1, 1, 1, 2] + [0, 0, 1, 0, 2, 1, 1] + [1, 2, 1, 1, 1]
        DONE = [8 + sum(EARLY[:j]) + sum(LATE[:j]) for j in range(len(JOBS) + 1)]
        GROUPS_BETWEEN = 6
        assert DONE[-1] == 8 * GROUPS_BETWEEN and all(8 * g in DONE for g in range(1, GROUPS_BETWEEN))

        def heads_of(kind, c):
            if kind in ("chosen", "index"):
                return [(2 * c + e, BANK * e) for e in range(2)]
            return [(4 * c + g, BANK * (g % 2) + 256 * (g // 2)) for g in range(4)]

        def normed(tiles, k):
            return ps[:, k, :] if tiles == TT else ps[:, 4 + k // 2, (k % 2) * M_LEN:(k % 2 + 1) * M_LEN]

        block = ctx.enter_context(nc.Block())

        @block.sync
        def _(sp):
            n = Tally()

            def unit(parts):
                u, slot, _ = n.unit()
                if n.i is not None or u >= 2:
                    sp.wait_ge(lo_ready, u - 1)
                for dst, src in parts(raw[:, slot]):
                    sp.dma_start(dst, src).then_inc(raw_ready[slot], 16)

            def slabs(w, k0, m, c0, width=BANK):
                a = (m + 1) // 2
                unit(lambda r: [(r[:, 0:a, 0:width], w[:, k0:k0 + a, bass.ds(c0, width)]),
                                (r[:, a:m, 0:width], w[:, k0 + a:k0 + m, bass.ds(c0, width)])])

            def gate_up(name, c0):
                gate, up = kpn(name + "_w_gate"), kpn(name + "_w_up")
                for k0 in (0, 4):
                    unit(lambda r: [(r[:, :, 0:256], gate[:, k0:k0 + 4, bass.ds(c0, 256)]),
                                    (r[:, :, 256:512], up[:, k0:k0 + 4, bass.ds(c0, 256)])])

            def groups(name, turns, c0, width=BANK, k0=0, kt=KT):
                w = kpn(name)
                with n.loop(sp, turns, unit=kt // 4) as i:
                    for k in range(k0, k0 + kt, 4):
                        slabs(w, k, 4, i * width + c0, width)

            def ffn(name, first):
                down = kpn(name + "_w_down")
                if first:
                    gate_up(name, 0)
                with n.loop(sp, 8 - first, unit=2) as i:
                    gate_up(name, i * 256 + 256 * first)
                groups(name + "_w_down", 2, 0, kt=16)
                with n.loop(sp, 3, unit=2) as i:
                    gate_up(name, i * 256 + 2048)
                with n.loop(sp, 2, unit=2) as i:
                    for k0 in (16, 19):
                        slabs(down, k0, 3, i * BANK)

            for t in range(TT):
                sp.dma_start(x[:, t, :], A["x"][0, t * P:(t + 1) * P, :]).then_inc(x_in, 16)
            ffn("ff1", 1)
            groups("w_in", 2, 1024)
            groups("w_in", 4, 2048)
            groups("w_in", 2, 4096)
            groups("w_in", 2, 0)
            groups("w_in", 2, 5120)
            groups("w_branch_a", 2, 0)
            groups("w_in", 2, 6144)
            groups("w_branch_b", 2, 0)
            groups("w_out", 2, 0)
            ffn("ff2", 0)
            for k0 in (0, 4):
                slabs(kpn("w_mem_kv_2"), k0, 4, 0)
            groups("w_in_2", 2, 0)
            groups("w_in_2", 2, 1024, 354)
            groups("w_in_2", 6, PCOLS)
            for c0 in (0, BANK):
                slabs(kpn("w_proj_swa_2"), 0, 4, c0)
                slabs(kpn("w_proj_dsa_2"), 0, 2, c0)
                slabs(kpn("w_proj_mem_2"), 0, 2, c0)
            groups("w_out_2", 2, 0)
            for c in range(2):
                groups("w_mlp_in_2", 4, c * 2048)
                groups("w_mlp_out_2", 2, 0, k0=16 * c, kt=16)
            for t in range(TT):
                sp.wait_ge(out_ready, TT + t + 1)
                sp.dma_start(out[0, t * P:(t + 1) * P, :], x[:, t, :]).then_inc(stored, 16)
            sp.wait_ge(stored, 16 * TT)

        @block.gpsimd
        def _(pool):
            n = Tally()
            pool.memset(ident[:], 0.0).then_inc(made, 1)
            pool.memset(ones_row[:], 1.0).then_inc(made, 1)
            pool.wait_ge(made, n.next("made", 2))
            pool.affine_select(out=ident[:], in_=ident[:], compare_op=ALU.not_equal, fill=1.0, base=0,
                               pattern=[[-1, P]], channel_multiplier=1).then_inc(made, 1)
            row = 0
            for name, r in ROWS:
                pool.dma_start(col_rows[row:row + r, :], A[name][0].rearrange("(r p) -> r p", p=P)).then_inc(const_in, 16)
                row += r
            pool.dma_start(ws_raw[:], A["gmlp_w_s"][0].rearrange("g t s -> t g s")).then_inc(const_in, 16)
            pool.dma_start(bs_row[:], A["gmlp_b_s"].rearrange("a g t -> a (g t)")).then_inc(late_in, 16)
            pool.dma_start(ln_g[:], A["gmlp_ln_g"][0].rearrange("g c -> (g c)").partition_broadcast(P)).then_inc(late_in, 16)
            pool.dma_start(ln_b[:], A["gmlp_ln_b"][0].rearrange("g c -> (g c)").partition_broadcast(P)).then_inc(late_in, 16)
            for e in range(2):
                for c in range(2):
                    pool.dma_start(snk[:, 4 * c + 2 * e:4 * c + 2 * e + 2],
                                   A["sinks_2"][0].rearrange("(c a e) -> e c a", c=2, e=2)[e, c].partition_broadcast(P),
                                   allow_slow_non_contiguous=True).then_inc(late_in, 16)
            pool.dma_start(pos_i[:], A["positions_2"][0].rearrange("(t p) -> p t", p=P),
                           allow_slow_non_contiguous=True).then_inc(late_in, 16)

            n.next("half_freed", 30 + 28)
            pool.wait_ge(half_freed, n.now("half_freed"))
            pool.memset(before, 1.0).then_inc(made, 1)
            pool.memset(after, 0.0).then_inc(made, 1)
            pool.wait_ge(made, 5)
            pool.affine_select(out=before, in_=before, compare_op=ALU.is_gt, fill=0.0, base=0,
                               pattern=[[-1, P]], channel_multiplier=1).then_inc(made, 1)
            pool.affine_select(out=after, in_=after, compare_op=ALU.is_gt, fill=1.0, base=0,
                               pattern=[[-1, P]], channel_multiplier=1).then_inc(made, 1)
            pool.wait_ge(made, 7)

            def stage_qk(to, tile):
                pool.tensor_copy(to[:, 0, :], qT[:, tile(1), :]).then_inc(pair_ready, 1)
                pool.tensor_copy(to[:, 1, :], kT[:, tile(1), :]).then_inc(pair_ready, 1)

            def stage_v(to, tile):
                pool.wait_ge(pv_done, n.now("pv_done"))
                pool.tensor_copy(to[:, 2, :].rearrange("p (t c) -> p t c", t=TT),
                                 v_tok[:, :, tile(P)]).then_inc(v_ready, 1)

            def diagonals(hh):
                for b in range(TT):
                    pool.wait_ge(sig_ready, n.next("sig_ready"))
                    w = beta[:, hh, OB[b] + P * b:OB[b] + P * b + P]
                    pool.tensor_tensor(w, w, before, ALU.mult).then_inc(masked_ready, 1)

            first = lambda w: slice(0, w)
            last = lambda w: slice(w * (KT - 1), w * KT)
            stage_qk(pairs[0], first)
            stage_v(pairs[0], first)
            with n.loop(pool, KT // 2 - 1, pv_done=4, sig_ready=16) as i:
                for c in range(2):
                    to, tile = pairs[(c + 1) % 2], lambda w: bass.ds(i * (2 * w) + w * (c + 1), w)
                    diagonals(0)
                    stage_qk(to, tile)
                    diagonals(1)
                    stage_v(to, tile)
                    n.next("pv_done", 2)
            diagonals(0)
            stage_qk(pairs[1], last)
            diagonals(1)
            stage_v(pairs[1], last)
            diagonals(0)
            diagonals(1)

            pool.wait_ge(half_freed, HALVES_FF2)
            pool.dma_start(rows[:], A["final_norm"].partition_broadcast(P)).then_inc(rows_in, 16)
            pool.dma_start(mem_tok[:], A["mem_2"][0].rearrange("(t p) d -> p t d", p=P)).then_inc(rows_in, 16)
            pool.dma_start(freq, A["inv_freq"].partition_broadcast(P)).then_inc(rows_in, 16)
            pool.memset(swa_mask, 0.0).then_inc(masks_made, 1)
            pool.wait_ge(masks_made, 1)
            pool.affine_select(out=swa_mask, in_=swa_mask, compare_op=ALU.is_ge, fill=MASKED, base=P,
                               pattern=[[-1, 2 * P]], channel_multiplier=1).then_inc(masks_made, 1)
            pool.wait_ge(masks_made, 2)
            pool.affine_select(out=swa_mask, in_=swa_mask, compare_op=ALU.is_gt, fill=MASKED, base=0,
                               pattern=[[1, 2 * P]], channel_multiplier=-1).then_inc(masks_made, 1)
            pool.wait_ge(rope_ready, 1)
            pool.memset(mask[:, 0:P], 0.0).then_inc(masks_made, 1)
            pool.wait_ge(masks_made, 4)
            pool.affine_select(out=mask[:, 0:P], in_=mask[:, 0:P], compare_op=ALU.is_ge, fill=MASKED, base=0,
                               pattern=[[-1, P]], channel_multiplier=1).then_inc(causal_ready, 1)
            for b in range(1, TT):
                pool.wait_ge(iscore_ready, n.next("iscore_ready"))
                diag = flat[:, P * b:P * b + P]
                pool.affine_select(out=diag, in_=diag, compare_op=ALU.is_ge, fill=OUT_OF_REACH, base=0,
                                   pattern=[[-1, P]], channel_multiplier=1).then_inc(causal_ready, 1)
            pool.wait_ge(half_freed, HALVES_MLP)
            pool.dma_start(rows[:], A["g_final_2"].partition_broadcast(P)).then_inc(rows_in, 16)

        @block.tensor
        def _(pe):
            n = Tally()

            def three(out_, w, a, weights_first, first, last):
                (wh, wl), (ah, al) = w, a
                for j, (p, q) in enumerate(((wh, ah), (wh, al), (wl, ah))):
                    lhs, rhs = (p, q) if weights_first else (q, p)
                    mm = pe.matmul(out_, lhs, rhs, start=first and j == 0, stop=last and j == 2)
                return mm

            def group(act, units, weights_first, width=BANK, first_group=False, operands=()):
                k, kt = 0, sum(units)
                for j, m in enumerate(units):
                    u, slot, _ = n.unit()
                    pe.wait_ge(lo_ready, u + 1)
                    for s in range(m):
                        if operands and k % (kt // len(operands)) == 0:
                            pe.wait_ge(operand_ready, operands[k // (kt // len(operands))])
                        for b in range(4):
                            if k == 0 and b in (0, 2) and not first_group:
                                pe.wait_ge(half_freed, n.now("half_freed", -1 if b == 0 else 0))
                            wc = slice(b * P, (b + 1) * P) if weights_first else slice(0, width)
                            ac = slice(0, S) if weights_first else slice(b * P, (b + 1) * P)
                            mm = three(ps[:, b, 0:S if weights_first else width],
                                       (w_hi[:, slot, s, wc], w_lo[:, slot, s, wc]),
                                       (act[0][:, k, ac], act[1][:, k, ac]), weights_first, k == 0, k == kt - 1)
                            if k == kt - 1 and b in (1, 3):
                                mm.then_inc(half_ready, 1)
                        k += 1
                    if j < len(units) - 1:
                        mm.then_inc(weights_used, 1)
                n.next("half_freed", 2)

            def groups(turns, act, units, weights_first, width=BANK, new=()):
                operands = fresh(*new)
                with n.loop(pe, turns, unit=len(units), half_freed=2):
                    group(act, units, weights_first, width, operands=operands)

            def fresh(*new):
                before = n.now("operand_ready")
                if new:
                    n.next("operand_ready", new[-1])
                return [before + k for k in new]

            def norm_transposes(tiles):
                for t in range(tiles):
                    pe.wait_ge(xn_ready, n.next("xn_ready"))
                    for k in range(KT):
                        tr = pe.transpose(normed(tiles, k)[:, t * P:(t + 1) * P],
                                          tmp[:, t % 2, k // 4, (k % 4) * P:(k % 4 + 1) * P], ident[:])
                    tr.then_inc(xn_used, 1)

            h = (h_hi, h_lo)
            hid = (hid_hi, hid_lo)

            def ffn(first):
                norm_transposes(TT)
                if first:
                    group(h, (4, 4), True, first_group=True, operands=fresh(4, 8))
                    groups(7, h, (4, 4), True)
                else:
                    groups(8, h, (4, 4), True, new=(4, 8))
                groups(2, hid, (4, 4, 4, 4), False, new=(2, 4, 6, 8))
                groups(3, h, (4, 4), True)
                if first:
                    groups(2, hid, (3, 3), False, new=(2, 3))
                else:
                    operands = fresh(2, 3)
                    group(hid, (3, 3), False, operands=operands)
                    norm_transposes(M_LEN // P)
                    group(hid, (3, 3), False, operands=operands)

            pe.wait_ge(made, 3)
            pe.wait_ge(const_in, 16 * (len(ROWS) + 1))
            pe.transpose(ps[:, 4, 0:NCOLS], col_rows[0:NCOLS, :], ident[0:NCOLS, 0:NCOLS]).then_inc(pv_done, 1)
            for g in range(4):
                tr = pe.transpose(ps[:, 5, g * P:(g + 1) * P], ws_raw[:, g, :], ident[:])
            tr.then_inc(cols_tr, 1)
            pe.wait_ge(cols_ready, 2)

            ffn(True)

            norm_transposes(TT)
            groups(2, h, (4, 4), False, new=(4, 8))
            groups(4, h, (4, 4), True)
            groups(2, h, (4, 4), False)
            pe.wait_ge(ln_ready, TT)
            for j in range(KT):
                if j >= 4:
                    pe.wait_ge(mix_copied, j - 3)
                for t in range(TT):
                    o = ps[:, 4 + j % 4, t * P:(t + 1) * P]
                    pe.matmul(o, vg[:, j, t, :], wsT[:, j // 2, :], start=True, stop=False)
                    mm = pe.matmul(o, ones_row[0:1, :], bs_row[0:1, (j // 2) * P:(j // 2 + 1) * P],
                                   start=False, stop=True)
                mm.then_inc(mix_ready, 1)
            groups(2, h, (4, 4), True)
            groups(2, h, (4, 4), True)
            groups(2, (ya_hi, ya_lo), (4, 4), True, new=(2, 4))

            pe.wait_ge(half_freed, n.now("half_freed"))

            def logits1(c, hh, first=False):
                if hh == 0:
                    pe.wait_ge(pair_ready, n.next("pair_ready", 2))
                half = slice(HD * hh, HD * hh + HD)
                for b in range(TT):
                    if not first:
                        pe.wait_ge(sig_ready, n.next("sig_ready"))
                    pe.matmul(ps[:, 4 + b, 0:P * (b + 1)], pairs[c][half, 0, b * P:(b + 1) * P],
                              pairs[c][half, 1, 0:P * (b + 1)], start=True, stop=True).then_inc(z_ready, 1)

            def transposes1(hh):
                pe.wait_ge(wT_copied, n.now("wT_copied"))
                n.next("wT_copied")
                for b in range(TT):
                    pe.wait_ge(w_ready, n.next("w_ready"))
                    for s in range(b + 1):
                        bank, col = ((0, b), (1, b - 1), (2, b - 2), (2, 2))[s]
                        tr = pe.transpose(ps[:, bank, col * P:(col + 1) * P],
                                          beta[:, hh, OB[b] + s * P:OB[b] + (s + 1) * P], ident[:])
                tr.then_inc(wT_ready, 1)

            def values1(c, hh, behind):
                pe.wait_ge(wT_copied, n.now("wT_copied", -behind))
                if hh == 0:
                    pe.wait_ge(v_ready, n.next("v_ready"))
                    pe.wait_ge(o_copied, n.now("o_copied"))
                    n.next("o_copied")
                for s, at in enumerate((0, 512, 896, 1152)):
                    mm = pe.matmul(ps[HD * hh:HD * hh + HD, 3, s * P:S],
                                   pairs[c][:, 2, s * P + HD * hh:s * P + HD * hh + HD],
                                   wT[:, at:at + S - s * P], start=s == 0, stop=s == TT - 1,
                                   skip_group_check=True)
                mm.then_inc(pv_done, 1)

            heads4 = [(c, hh) for c in range(2) for hh in range(2)]
            logits1(0, 0, True)
            logits1(0, 1)
            transposes1(0)
            with n.loop(pe, KT // 2 - 1, pair_ready=4, sig_ready=16, w_ready=16, wT_copied=4, v_ready=2, o_copied=2):
                for g in range(1, 5):
                    logits1(*heads4[(g + 1) % 4])
                    transposes1(g % 2)
                    values1(*heads4[g - 1], 1)
            for g in range(1, 4):
                if g < 3:
                    logits1(*heads4[g + 1])
                transposes1(g % 2)
                values1(*heads4[g - 1], 1)
            values1(*heads4[3], 0)
            pe.wait_ge(o_copied, n.now("o_copied"))

            groups(2, h, (4, 4), True)
            groups(2, h, (4, 4), True, new=(1, 2, 3, 4))
            groups(2, (m_hi, m_lo), (4, 4), False, new=(2, 4))

            ffn(False)

            operands = fresh(4, 8)
            for j in range(2):
                u, slot, _ = n.unit()
                pe.wait_ge(lo_ready, u + 1)
                pe.wait_ge(operand_ready, operands[j])
                for s in range(4):
                    k = 4 * j + s
                    for b in range(4):
                        if k == 0 and b in (0, 2):
                            pe.wait_ge(half_freed, n.now("half_freed", -1 if b == 0 else 0))
                        keys = b < 2
                        wc = slice(b * P, (b + 1) * P) if keys else slice(256, 512)
                        ac = slice(0, M_LEN) if keys else slice((b - 2) * P, (b - 1) * P)
                        mm = three(ps[:, b, 0:256], (w_hi[:, slot, s, wc], w_lo[:, slot, s, wc]),
                                   (h_hi[:, k, ac], h_lo[:, k, ac]), keys, k == 0, k == KT - 1)
                        if k == KT - 1 and b in (1, 3):
                            mm.then_inc(half_ready, 1)
                if j == 0:
                    mm.then_inc(weights_used, 1)
            n.next("half_freed", 2)

            pe.wait_ge(half_freed, n.now("half_freed"))
            norm_transposes(TT)
            groups(2, h, (4, 4), False, new=(4, 8))
            groups(2, h, (4, 4), False, 354)

            def scores(j):
                kind, b, c, nk = JOBS[j]
                if j:
                    pe.wait_ge(z_freed, j)
                for g, at in heads_of(kind, c):
                    half = slice(HD * (g % 2), HD * (g % 2) + HD)
                    q0 = {"window": QS, "chosen": QD, "index": QI, "memory": QM}[kind] + g // 2
                    if kind == "window":
                        k = qkT[half, KS + c, (b + 1) * P - nk:(b + 1) * P]
                    elif kind == "memory":
                        k = memT[half, g // 2, :]
                    else:
                        k = qkT[half, KI if kind == "index" else KD, 0:nk]
                    mm = pe.matmul(ps[:, 4 + at // BANK, at % BANK:at % BANK + nk],
                                   qkT[half, q0, b * P:(b + 1) * P], k, start=True, stop=True)
                mm.then_inc(z_ready, 1)

            def transposes(j):
                kind, b, c, nk = JOBS[j]
                pe.wait_ge(prob_ready, n.next("prob_ready"))
                pe.wait_ge(o_copied, n.now("o_copied"))
                heads = heads_of(kind, c)
                for g, at in heads:
                    for kb in range(nk // P):
                        to = kb * len(heads) * P + (g % len(heads)) * P
                        tr = pe.transpose(ps[:, 6 + to // BANK, to % BANK:to % BANK + P],
                                          logits[:, at + kb * P:at + (kb + 1) * P], ident[:])
                tr.then_inc(pT_ready, 1)

            def values(j):
                kind, b, c, nk = JOBS[j]
                pe.wait_ge(pT_copied, n.next("pT_copied"))
                for g in range(4 if kind == "memory" else 1):
                    for kb in range(nk // P):
                        if kind == "window":
                            v = vals[:, b + 1 - nk // P + kb, HD * c:HD * c + HD]
                            w = slice(kb * BANK, (kb + 1) * BANK)
                        elif kind == "chosen":
                            v, w = vals[:, kb, 2 * HD:3 * HD], slice(kb * 256, (kb + 1) * 256)
                        else:
                            v = memv[:, kb, HD * g:HD * g + HD]
                            w = slice(kb * BANK + g * P, kb * BANK + (g + 1) * P)
                        mm = pe.matmul(ps[0:HD, 6, g * P:g * P + w.stop - w.start], v, pT[:, w],
                                       start=kb == 0, stop=kb == nk // P - 1)
                mm.then_inc(o_ready, 1)
                n.next("o_copied")

            def slab(at):
                nonlocal slot
                k = at % KT
                if k % 4 == 0:
                    u, slot, _ = n.unit()
                    pe.wait_ge(lo_ready, u + 1)
                for b in range(4):
                    if k == 0 and b in (0, 2):
                        pe.wait_ge(half_freed, n.now("half_freed", -1 if b == 0 else 0))
                    mm = three(ps[:, b, :], (w_hi[:, slot, k % 4, b * P:(b + 1) * P], w_lo[:, slot, k % 4, b * P:(b + 1) * P]),
                               (h_hi[:, k, :], h_lo[:, k, :]), True, k == 0, k == KT - 1)
                    if k == KT - 1 and b in (1, 3):
                        mm.then_inc(half_ready, 1)
                if k == 3:
                    mm.then_inc(weights_used, 1)
                if k == KT - 1:
                    n.next("half_freed", 2)

            slot = 0
            for at in range(DONE[0]):
                slab(at)
            pe.wait_ge(rope_ready, 1)
            for j, c in enumerate(TILE_COLS):
                if j >= 4:
                    pe.wait_ge(tr_copied, j - 3)
                for t in range(TT):
                    tr = pe.transpose(ps[:, 4 + j % 4, t * P:(t + 1) * P], proj[:, t, c:c + P], ident[:])
                tr.then_inc(tr_ready, 1)
            pe.wait_ge(tr_copied, len(TILE_COLS))

            scores(0)
            for j, job in enumerate(JOBS):
                if j + 1 < len(JOBS):
                    scores(j + 1)
                for at in range(DONE[j], DONE[j] + EARLY[j]):
                    slab(at)
                if job[0] != "index":
                    transposes(j)
                    for at in range(DONE[j] + EARLY[j], DONE[j + 1]):
                        slab(at)
                    values(j)

            swa, rest = fresh(1, 2)
            for _ in range(2):
                group((o_hi[:, 0:4, :], o_lo[:, 0:4, :]), (4,), True, operands=[swa])
                group((o_hi[:, 4:6, :], o_lo[:, 4:6, :]), (2,), True, operands=[rest])
                group((o_hi[:, 6:8, :], o_lo[:, 6:8, :]), (2,), True)
            groups(2, (m2_hi, m2_lo), (4, 4), False, new=(2, 4))
            norm_transposes(TT)
            for c in range(2):
                groups(4, h, (4, 4), True, new=() if c else (4, 8))
                groups(2, hid, (4, 4, 4, 4), False, new=(2, 4, 6, 8))

        @block.scalar
        def _(act):
            n = Tally()

            def split(units, done=0):
                for j in range(done, units):
                    u, slot, landed = n.unit()
                    if j:
                        act.wait_ge(weights_used, n.next("weights_used"))
                    elif n.i is not None or n.now("half_ready"):
                        act.wait_ge(half_ready, n.now("half_ready"))
                    act.wait_ge(raw_ready[slot], landed)
                    act.activation(w_hi[:, slot], raw[:, slot], ACT.Copy).then_inc(hi_ready, 1)
                return u

            def complete():
                act.wait_ge(half_ready, n.next("half_ready"))

            def passed(halves=2):
                n.next("half_ready", halves)
                n.next("half_freed", halves)

            def dve_groups(turns, units):
                with n.loop(act, turns, unit=units, weights_used=units - 1, half_ready=2, half_freed=2):
                    split(units)
                    passed()

            def copy_groups(turns, dst):
                with n.loop(act, turns, unit=2, weights_used=1, half_ready=2, half_freed=2) as i:
                    split(2)
                    for hf in range(2):
                        complete()
                        to = dst(i, hf)
                        act.activation(to, ps[:, 2 * hf:2 * hf + 2, 0:to.shape[2]], ACT.Copy).then_inc(half_freed, 1)
                        n.next("half_freed")

            def high(dst, src):
                act.wait_ge(prod_ready, n.next("prod_ready"))
                act.activation(dst, src, ACT.Copy).then_inc(acthi_ready, 1)

            def functions(func):
                u = split(2)
                act.wait_ge(lo_ready, u + 1)
                for hf in range(2):
                    complete()
                    act.activation(tmp[:, hf], ps[:, 2 * hf:2 * hf + 2, :], func).then_inc(half_freed, 1)
                    n.next("half_freed")

            def root():
                act.wait_ge(var_ready, n.next("var_ready"))
                act.activation(ROOT, REC, ACT.Sqrt).then_inc(root_ready, 1)

            def squares(src):
                act.activation(stat[:, 96:97], ident[:, 0:1], ACT.Sqrt)
                if n.now("half_freed"):
                    act.wait_ge(half_freed, n.now("half_freed", -1))
                for t in range(2):
                    act.activation(ps[:, 4 + 2 * t:6 + 2 * t, :],
                                   src[:, t, :].rearrange("p (a b) -> p a b", a=2), ACT.Square,
                                   accum_out=SS[:, t:t + 1]).then_inc(sq_ready, 1)
                root()

            def norm(src, tiles, gain):
                squares(src)
                normed_high(tiles, gain)

            def normed_high(tiles, gain):
                act.wait_ge(xn_used, n.next("xn_used", tiles))
                for k in range(KT):
                    act.activation(h_hi[:, k, 0:tiles * P], normed(tiles, k)[:, 0:tiles * P], ACT.Copy,
                                   scale=cols[:, gain + k:gain + k + 1]).then_inc(acthi_ready, 1)

            def gate_groups(turns, dst, bias, tile0=0):
                with n.loop(act, turns, unit=2, weights_used=1, half_ready=2, half_freed=2) as i:
                    split(2)
                    for b in range(4):
                        if b % 2 == 0:
                            complete()
                        a = act.activation(dst[:, bass.ds(i * 4 + (b + tile0), 1), :], ps[:, b:b + 1, :], ACT.Sigmoid,
                                           bias=cols[:, bass.ds(i * 4 + (b + bias), 1)])
                        if b % 2:
                            a.then_inc(half_freed, 1)
                            n.next("half_freed")

            def gate_up(i, tile0):
                split(2)
                complete()
                act.activation(tmp[:, 0], ps[:, 0:2, :], ACT.Silu).then_inc(half_freed, 1)
                n.next("half_ready")
                act.wait_ge(half_freed, n.next("half_freed", 2))
                act.activation(hid_hi[:, bass.ds(i * 2 + tile0, 2), :], tmp[:, 1], ACT.Copy).then_inc(acthi_ready, 1)

            def gates_up(turns, tile0):
                with n.loop(act, turns, unit=2, weights_used=1, half_ready=2, half_freed=2) as i:
                    gate_up(i, tile0)

            def ffn(gain, first=0):
                norm(x, TT, gain)
                if first:
                    gate_up(0, 0)
                gates_up(8 - first, 2 * first)
                dve_groups(2, 4)
                gates_up(3, 0)
                if first:
                    dve_groups(2, 2)
                    return
                split(2)
                act.wait_ge(rows_in, 48)
                squares(mem_tok)
                passed()
                split(2)
                normed_high(M_LEN // P, COL["g_mem_2"])
                passed()

            act.wait_ge(raw_ready[0], n.unit()[2])
            act.activation(w_hi[:, 0], raw[:, 0], ACT.Copy).then_inc(hi_ready, 1)
            act.wait_ge(x_in, 16 * TT)
            act.wait_ge(cols_ready, 2)
            ffn(COL["ff1_norm"], 1)

            norm(x, TT, COL["mix_norm"])
            with n.loop(act, 2, unit=2, weights_used=1, half_ready=2, half_freed=2) as i:
                split(2)
                for t in range(TT):
                    if t % 2 == 0:
                        complete()
                    a = act.activation(vg[:, bass.ds(i * 4, 4), t, :],
                                       ps[:, t, :].rearrange("p (c k) -> p c k", c=4), ACT.Gelu)
                    if t % 2:
                        a.then_inc(half_freed, 1)
                        n.next("half_freed")
            for dst in (qT, kT):
                with n.loop(act, 2, unit=2, weights_used=1, half_ready=2, half_freed=2, var_ready=1) as i:
                    split(2)
                    root()
                    for hf in range(2):
                        complete()
                        act.activation(dst[:, bass.ds(i * 4 + 2 * hf, 2), :], ps[:, 2 * hf:2 * hf + 2, :],
                                       ACT.Copy).then_inc(half_freed, 1)
                        n.next("half_freed")
            copy_groups(2, lambda i, hf: v_tok[:, 2 * hf:2 * hf + 2, bass.ds(i * BANK, BANK)])
            for j in range(KT):
                act.wait_ge(mix_ready, j + 1)
                act.activation(vg[:, j].rearrange("p n t -> p (n t)"), ps[:, 4 + j % 4, :], ACT.Copy).then_inc(mix_copied, 1)
            with n.loop(act, 2, unit=2, weights_used=1, half_ready=2, half_freed=2, prod_ready=2) as i:
                functions(ACT.Gelu)
                for hf in range(2):
                    high(ya_hi[:, bass.ds(i * 4 + 2 * hf, 2), :], tmp[:, hf])
            act.wait_ge(operand_ready, 8 + 11 + 8 + 4)
            gate_groups(2, merged, COL["b_gate"])
            dve_groups(2, 2)

            def sigmoids(hh):
                for b in range(TT):
                    nk = P * (b + 1)
                    act.wait_ge(z_ready, n.next("z_ready"))
                    act.activation(beta[:, hh, OB[b]:OB[b] + nk], ps[:, 4 + b, 0:nk], ACT.Sigmoid, scale=SCALE)
                    act.activation(keep[:, hh, OB[b] + b:OB[b] + b + nk], ps[:, 4 + b, 0:nk], ACT.Sigmoid,
                                   scale=-SCALE).then_inc(sig_ready, 1)

            def weights_out():
                act.wait_ge(wT_ready, n.next("wT_ready"))
                act.wait_ge(pv_done, n.now("pv_done"))
                n.next("pv_done")
                act.activation(wT[:, 0:512], ps[:, 0, :], ACT.Copy)
                act.activation(wT[:, 512:1280].rearrange("p (a b) -> p a b", a=2), ps[:, 1:3, 0:384],
                               ACT.Copy).then_inc(wT_copied, 1)

            sigmoids(0)
            with n.loop(act, KT - 1, z_ready=8, wT_ready=2, pv_done=2):
                for hh in range(2):
                    sigmoids(1 - hh)
                    weights_out()
            sigmoids(1)
            weights_out()
            weights_out()

            gate_groups(2, gate_b, COL["b_gate"] + 8)
            act.wait_ge(o_copied, 1 + KT)
            for j in range(4):
                act.activation(h_hi[:, 2 * j:2 * j + 2, :], qT[:, 2 * j:2 * j + 2, :], ACT.Copy).then_inc(acthi_ready, 1)
            with n.loop(act, 2, unit=2, weights_used=1, half_ready=2, half_freed=2, prod_ready=2) as i:
                split(2)
                for hf in range(2):
                    passed(1)
                    high(m_hi[:, bass.ds(i * 4 + 2 * hf, 2), :], merged[:, bass.ds(i * 4 + 2 * hf, 2), :])
            dve_groups(2, 2)
            ffn(COL["ff2_norm"])

            split(1)
            squares(x)
            split(2, 1)
            act.wait_ge(out_ready, TT)
            squares(x)
            complete()
            act.activation(memT[:], ps[:, 0:2, 0:256], ACT.Copy).then_inc(half_freed, 1)
            complete()
            act.activation(memv[:], ps[:, 2:4, 0:256], ACT.Copy).then_inc(half_freed, 1)
            n.next("half_freed", 2)
            normed_high(TT, COL["g_mix_2"])
            copy_groups(2, lambda i, hf: proj[:, 2 * hf:2 * hf + 2, bass.ds(i * BANK, BANK)])
            copy_groups(2, lambda i, hf: proj[:, 2 * hf:2 * hf + 2, bass.ds(i * 354 + 1024, 354)])

            between = [0, 0]

            def stream(done):
                while between[0] < 2 * GROUPS_BETWEEN and 4 * between[0] <= done:
                    if between[0] and between[0] % 2 == 0:
                        gates_out(between[1])
                        between[1] += 1
                    between[0] += 1
                    _, slot, landed = n.unit()
                    if between[0] % 2 == 0:
                        act.wait_ge(weights_used, n.next("weights_used"))
                    else:
                        act.wait_ge(half_ready, n.now("half_ready"))
                    act.wait_ge(raw_ready[slot], landed)
                    act.activation(w_hi[:, slot], raw[:, slot], ACT.Copy).then_inc(hi_ready, 1)

            def gates_out(i):
                for b in range(4):
                    if b % 2 == 0:
                        complete()
                    c = COL["b_gate_2"] + 4 * i + b
                    a = act.activation(gates2[:, 4 * i + b, :], ps[:, b, :], ACT.Sigmoid, bias=cols[:, c:c + 1])
                    if b % 2:
                        a.then_inc(half_freed, 1)
                        n.next("half_freed")

            stream(0)
            act.wait_ge(trig_ready, 1)
            act.activation(sin_t, r_sin, ACT.Sin)
            act.activation(cos_t, r_cos, ACT.Sin).then_inc(sin_ready, 1)
            stream(4)
            for j in range(len(TILE_COLS)):
                act.wait_ge(tr_ready, j + 1)
                act.activation(qkT[:, j, :], ps[:, 4 + j % 4, :], ACT.Copy).then_inc(tr_copied, 1)

            z0 = n.now("z_ready")
            for j, (kind, b, c, nk) in enumerate(JOBS):
                if kind == "index":
                    stream(DONE[j])
                    act.wait_ge(z_ready, z0 + j + 1)
                    if b > 1:
                        act.wait_ge(choice_made, b - 1)
                    act.activation(flat.rearrange("p (h s) -> p h s", h=4)[:, 2 * c:2 * c + 2, 0:nk],
                                   ps[:, 4:6, 0:nk], ACT.Relu).then_inc(z_freed, 1)
                    continue
                heads = heads_of(kind, c)
                act.wait_ge(logit_ready, n.next("logit_ready"))
                for g, (_, at) in enumerate(sorted(heads, key=lambda x: x[1])):
                    e = act.activation(logits[:, at:at + nk], logits[:, at:at + nk], ACT.Exp,
                                       bias=neg[:, g:g + 1], accum_out=tot[:, g:g + 1])
                if kind == "window":
                    e = act.activation(snk_e[:, 0:4], snk_e[:, 0:4], ACT.Exp)
                e.then_inc(exp_ready, 1)
                stream(DONE[j])
                n.next("prob_ready")
                act.wait_ge(pT_ready, n.next("pT_ready"))
                w = (nk // P) * len(heads) * P
                act.activation(pT[:, 0:w], ps[:, 6:8, :].rearrange("p a b -> p (a b)")[:, 0:w],
                               ACT.Copy).then_inc(pT_copied, 1)
            gates_out(GROUPS_BETWEEN - 1)

            act.wait_ge(o_copied, 1 + KT + 20)
            for j in range(2):
                act.activation(o_hi[:, 4 * j:4 * j + 4, :], oT[:, 4 * j:4 * j + 4, :], ACT.Copy).then_inc(acthi_ready, 1)
            for c in range(2):
                for kind in range(3):
                    split(1)
                    for hf in range(2):
                        passed(1)
                        if kind == 2:
                            t = slice(4 * c + 2 * hf, 4 * c + 2 * hf + 2)
                            high(m2_hi[:, t, :], merged2[:, t, :])
            dve_groups(2, 2)
            norm(x, TT, COL["g_mlp_2"])
            for c in range(2):
                with n.loop(act, 4, unit=2, weights_used=1, half_ready=2, half_freed=2, prod_ready=2) as i:
                    functions(ACT.Relu)
                    for hf in range(2):
                        high(hid_hi[:, bass.ds(i * 4 + 2 * hf, 2), :], tmp[:, hf])
                if c == 0:
                    dve_groups(2, 4)
                else:
                    split(4)
                    passed()
                    split(3)
                    passed()
            squares(x)

        @block.vector
        def _(dve):
            n = Tally()

            def step(ins):
                ins.then_inc(dve_step, 1)
                dve.wait_ge(dve_step, n.next("dve_step"))

            def split(units):
                for _ in range(units):
                    _, slot, _ = n.unit()
                    dve.wait_ge(hi_ready, n.next("hi_ready"))
                    dve.tensor_tensor(w_lo[:, slot], raw[:, slot], w_hi[:, slot].bitcast(F32),
                                      ALU.subtract).then_inc(lo_ready, 1)

            def complete():
                dve.wait_ge(half_ready, n.next("half_ready"))

            def freed(ins):
                ins.then_inc(half_freed, 1)
                n.next("half_freed")

            def low(dst, src, hi):
                dve.wait_ge(acthi_ready, n.next("acthi_ready"))
                dve.tensor_tensor(dst, src, hi.bitcast(F32), ALU.subtract).then_inc(operand_ready, 1)
                n.next("operand_ready")

            def act_groups(turns):
                with n.loop(dve, turns, unit=2, hi_ready=2, half_ready=2, half_freed=2):
                    split(2)
                    n.next("half_ready", 2)
                    n.next("half_freed", 2)

            def rsqrt(w, src, scale):
                V, C, Q, N_, O = (a[:, 0:w] for a in (VAR, REC, ROOT, NEW, R))
                step(dve.tensor_scalar(V, src, scale, EPS, ALU.mult, ALU.add))
                dve.reciprocal(C, V).then_inc(var_ready, 1)
                dve.wait_ge(root_ready, n.next("root_ready"))
                step(dve.tensor_tensor(N_, Q, Q, ALU.mult))
                step(dve.tensor_tensor(N_, N_, V, ALU.mult))
                step(dve.tensor_scalar(N_, N_, -0.5, 1.5, ALU.mult, ALU.add))
                step(dve.tensor_tensor(O, Q, N_, ALU.mult))

            def squares(src, tiles, spare=None):
                spare = ps[:, 0:4, :].rearrange("p (a b) c -> p a (b c)", a=2) if spare is None else spare
                if tiles > 2 and n.now("half_freed"):
                    dve.wait_ge(half_freed, n.now("half_freed"))
                for t in range(2, tiles):
                    ins = dve.tensor_tensor_reduce(spare[:, t - 2, :],
                                                   src[:, t, :], src[:, t, :], 1.0, 0.0, ALU.mult, ALU.add,
                                                   SS[:, t:t + 1])
                if tiles > 2:
                    step(ins)
                dve.wait_ge(sq_ready, n.next("sq_ready", 2))
                rsqrt(4, SS, 1.0 / D)

            def norm(src, tiles, gain, spare=None):
                normed_tokens(src, tiles, spare)
                normed_low(tiles, gain)

            def normed_tokens(src, tiles, spare=None):
                squares(src, tiles, spare)
                for t in range(tiles):
                    if t >= 2:
                        dve.wait_ge(xn_used, n.now("xn_used", t - 1))
                    dve.tensor_scalar(tmp[:, t % 2].rearrange("p a b -> p (a b)"), src[:, t, :], R[:, t:t + 1],
                                      None, ALU.mult).then_inc(xn_ready, 1)
                n.next("xn_used", tiles)

            def normed_low(tiles, gain):
                if tiles < TT:
                    dve.wait_ge(acthi_ready, n.next("acthi_ready", KT))
                for k in range(KT):
                    if tiles == TT:
                        dve.wait_ge(acthi_ready, n.next("acthi_ready"))
                    dve.scalar_tensor_tensor(out=h_lo[:, k, 0:tiles * P], in0=normed(tiles, k)[:, 0:tiles * P],
                                             scalar=cols[:, gain + k:gain + k + 1],
                                             in1=h_hi[:, k, 0:tiles * P].bitcast(F32), op0=ALU.mult,
                                             op1=ALU.subtract).then_inc(operand_ready, 1)
                    n.next("operand_ready")

            def last_norm(rows_at, spare=None):
                squares(x, TT, spare)
                dve.wait_ge(rows_in, rows_at)
                for t in range(TT):
                    dve.scalar_tensor_tensor(out=x[:, t, :], in0=x[:, t, :], scalar=R[:, t:t + 1], in1=rows[:],
                                             op0=ALU.mult, op1=ALU.mult).then_inc(out_ready, 1)

            def gate_up(turns):
                with n.loop(dve, turns, unit=2, hi_ready=2, half_ready=2, half_freed=2, acthi_ready=1, operand_ready=1) as i:
                    split(2)
                    dve.wait_ge(half_freed, n.next("half_freed"))
                    n.next("half_ready")
                    complete()
                    freed(dve.tensor_tensor(tmp[:, 1], tmp[:, 0], ps[:, 2:4, :], ALU.mult))
                    low(hid_lo[:, bass.ds(i * 2, 2), :], tmp[:, 1], hid_hi[:, bass.ds(i * 2, 2), :])

            def residual(turns, units, scale):
                with n.loop(dve, turns, unit=units, hi_ready=units, half_ready=2, half_freed=2) as i:
                    split(units)
                    add(i, scale)

            def add(i, scale):
                for hf in range(2):
                    complete()
                    to = x[:, 2 * hf:2 * hf + 2, bass.ds(i * BANK, BANK)]
                    freed(dve.scalar_tensor_tensor(out=to, in0=ps[:, 2 * hf:2 * hf + 2, :], scalar=scale, in1=to,
                                                   op0=ALU.mult, op1=ALU.add))

            def ffn(gain):
                norm(x, TT, gain)
                gate_up(8)
                residual(2, 4, 0.5)
                gate_up(3)
                if gain == COL["ff1_norm"]:
                    residual(2, 2, 0.5)
                    return
                split(2)
                normed_tokens(mem_tok, M_LEN // P)
                add(0, 0.5)
                split(2)
                normed_low(M_LEN // P, COL["g_mem_2"])
                add(1, 0.5)

            dve.wait_ge(cols_tr, 1)
            dve.tensor_copy(cols[:], ps[:, 4, 0:NCOLS]).then_inc(cols_ready, 1)
            wsrc = ps[:, 5, :].rearrange("p (g t) -> p g t", g=4)
            dve.tensor_copy(wsT[0:64], wsrc[0:64]).then_inc(wT_copied, 1)
            dve.memset(wsT[64:128, :, 0:64], 0.0).then_inc(o_copied, 1)
            dve.tensor_copy(wsT[64:128, :, 64:128], wsrc[64:128, :, 64:128]).then_inc(cols_ready, 1)
            split(1)
            dve.wait_ge(x_in, 16 * TT)
            ffn(COL["ff1_norm"])

            norm(x, TT, COL["mix_norm"])
            dve.wait_ge(late_in, 16 * 8)
            act_groups(2)
            with n.loop(dve, 4, unit=2, hi_ready=2, half_ready=2, half_freed=2, dve_step=9, root_ready=1) as i:
                split(1)
                dve.wait_ge(half_freed, 34)
                tiles = [vg[:, 2 * g:2 * g + 2, bass.ds(i, 1), :].rearrange("p c o k -> p (c o) k") for g in range(4)]
                for g in range(4):
                    ins = dve.bn_stats(bn[:, g, :], tiles[g])
                step(ins)
                dve.tensor_copy(NEW, SS)
                for g in range(4):
                    ins = dve.bn_aggr(mv[:, 2 * g:2 * g + 2], bn[:, g, :])
                step(ins)
                rsqrt(4, mv.rearrange("p (g s) -> p g s", s=2)[:, :, 1], 1.0)
                for g in range(4):
                    ins = dve.tensor_scalar(tiles[g], tiles[g], mv[:, 2 * g:2 * g + 1], R[:, g:g + 1],
                                            ALU.subtract, ALU.mult)
                step(ins)
                whole = vg[:, :, bass.ds(i, 1), :].rearrange("p c o k -> p (c o) k")
                step(dve.tensor_tensor(whole, whole, ln_g[:].rearrange("p (c k) -> p c k", c=KT), ALU.mult))
                dve.tensor_tensor(whole, whole, ln_b[:].rearrange("p (c k) -> p c k", c=KT),
                                  ALU.add).then_inc(ln_ready, 1)
                split(1)
                n.next("half_ready", 2)
                n.next("half_freed", 2)
            act_groups(2)
            with n.loop(dve, 2, unit=2, hi_ready=2, half_ready=2, half_freed=2, acthi_ready=2, operand_ready=2) as i:
                split(2)
                for hf in range(2):
                    t = bass.ds(i * 4 + 2 * hf, 2)
                    dve.wait_ge(mix_copied, KT)
                    n.next("half_ready")
                    dve.wait_ge(half_freed, n.next("half_freed"))
                    dve.tensor_tensor(tmp[:, hf], tmp[:, hf], merged[:, t, :], ALU.mult).then_inc(prod_ready, 1)
                for hf in range(2):
                    t = bass.ds(i * 4 + 2 * hf, 2)
                    low(ya_lo[:, t, :], tmp[:, hf], ya_hi[:, t, :])
            act_groups(2)
            with n.loop(dve, 2, unit=2, hi_ready=2, half_ready=2, half_freed=2) as i:
                split(2)
                for hf in range(2):
                    t = bass.ds(i * 4 + 2 * hf, 2)
                    complete()
                    freed(dve.tensor_tensor(merged[:, t, :], merged[:, t, :], ps[:, 2 * hf:2 * hf + 2, :], ALU.mult))

            for hh in range(2):
                for b in range(TT):
                    at = OB[b] + b + P * (b + 1)
                    ins = dve.memset(keep[:, hh, at:at + 1], 1.0)
            step(ins)

            def scans(hh):
                for b in range(TT):
                    nk, at = P * (b + 1), OB[b] + b
                    dve.wait_ge(sig_ready, n.next("sig_ready"))
                    k = keep[:, hh, at + P * b:at + nk]
                    step(dve.tensor_tensor(k, k, after, ALU.max))
                    k = keep[:, hh, at:at + nk][:, ::-1]
                    step(dve.tensor_tensor_scan(k, k, k, 1.0, ALU.mult, ALU.bypass))
                    w = beta[:, hh, OB[b]:OB[b] + nk]
                    dve.wait_ge(masked_ready, n.next("masked_ready"))
                    dve.tensor_tensor(w, w, keep[:, hh, at + 1:at + 1 + nk], ALU.mult).then_inc(w_ready, 1)

            def pair_out(tile):
                dve.wait_ge(pv_done, n.next("pv_done", 2))
                dve.tensor_copy(qT[:, tile, :], ps[:, 3:4, :]).then_inc(o_copied, 1)

            dve.wait_ge(made, 7)
            scans(0)
            scans(1)
            with n.loop(dve, KT - 1, sig_ready=8, masked_ready=8, dve_step=16, pv_done=2) as i:
                scans(0)
                scans(1)
                pair_out(bass.ds(i, 1))
            pair_out(slice(KT - 1, KT))

            act_groups(2)
            for j in range(4):
                t = slice(2 * j, 2 * j + 2)
                low(h_lo[:, t, :], qT[:, t, :], h_hi[:, t, :])
            with n.loop(dve, 2, unit=2, hi_ready=2, half_ready=2, half_freed=2, acthi_ready=2, operand_ready=2) as i:
                split(2)
                for hf in range(2):
                    t = bass.ds(i * 4 + 2 * hf, 2)
                    complete()
                    freed(dve.tensor_tensor(tmp[:, hf], gate_b[:, t, :], ps[:, 2 * hf:2 * hf + 2, :], ALU.mult))
                dve.wait_ge(half_freed, n.now("half_freed"))
                for hf in range(2):
                    t = bass.ds(i * 4 + 2 * hf, 2)
                    dve.tensor_tensor(merged[:, t, :], merged[:, t, :], tmp[:, hf], ALU.add).then_inc(prod_ready, 1)
                for hf in range(2):
                    t = bass.ds(i * 4 + 2 * hf, 2)
                    low(m_lo[:, t, :], merged[:, t, :], m_hi[:, t, :])
            residual(2, 2, 1.0)
            ffn(COL["ff2_norm"])

            spare = tmp[:, :, :, :].rearrange("p a b c -> p a (b c)")
            split(1)
            last_norm(48, spare)
            split(1)
            dve.wait_ge(out_ready, TT)
            norm(x, TT, COL["g_mix_2"], spare)
            n.next("half_ready", 2)
            n.next("half_freed", 2)
            step(dve.tensor_copy(pos_f, pos_i[:]))
            for t in range(TT):
                ins = dve.tensor_scalar(ang[:, 32 * t:32 * t + 32], freq, pos_f[:, t:t + 1], None, ALU.mult)
            step(ins)
            step(dve.tensor_scalar(turns, ang, 1.0 / (2 * 3.141592653589793), ROUND, ALU.mult, ALU.add))
            step(dve.tensor_scalar(turns, turns, -ROUND, None, ALU.add))
            for part in TWO_PI:
                step(dve.scalar_tensor_tensor(out=ang, in0=turns, scalar=-part, in1=ang, op0=ALU.mult, op1=ALU.add))
            dve.tensor_scalar(r_sin, ang, PI, -PI, ALU.min, ALU.max)
            step(dve.tensor_scalar(r_cos, ang, 3.141592653589793 / 2, None, ALU.add))
            step(dve.tensor_scalar(turns, r_cos, 3.141592653589793, -2 * 3.141592653589793, ALU.is_gt, ALU.mult))
            step(dve.tensor_tensor(r_cos, r_cos, turns, ALU.add))
            dve.tensor_scalar(r_cos, r_cos, PI, -PI, ALU.min, ALU.max).then_inc(trig_ready, 1)
            act_groups(4)

            between = [0]

            def stream(done):
                while between[0] < 2 * GROUPS_BETWEEN and 4 * between[0] <= done:
                    between[0] += 1
                    split(1)

            stream(0)
            dve.wait_ge(sin_ready, 1)
            dve.wait_ge(half_freed, n.now("half_freed"))
            for c0, heads in ((0, 10), (768, 5), (Q_I, 5)):
                both = proj[:, :, c0:c0 + HD * heads].rearrange("p t (h w) -> p t h w", w=HD)
                x1, x2 = both[:, :, :, 0:32], both[:, :, :, 32:64]
                c, s = (a.rearrange("p (t w) -> p t w", t=TT).unsqueeze(2).broadcast_to([P, TT, heads, 32])
                        for a in (cos_t, sin_t))
                a1, a2, a3, a4 = (rope_t[:, j, 0:TT * heads * 32].rearrange("p (t h w) -> p t h w", t=TT, h=heads)
                                  for j in range(4))
                dve.tensor_tensor(a1, x1, c, ALU.mult)
                dve.tensor_tensor(a2, x2, s, ALU.mult)
                dve.tensor_tensor(a3, x2, c, ALU.mult)
                step(dve.tensor_tensor(a4, x1, s, ALU.mult))
                dve.tensor_tensor(x1, a1, a2, ALU.subtract)
                step(dve.tensor_tensor(x2, a3, a4, ALU.add))
                if c0 == 0:
                    stream(4)
            for j, c0 in enumerate((512, 576, K_D, K_I)):
                for r in range(2):
                    dve.tensor_copy(proj[:, :, KDUP + P * j + HD * r:KDUP + P * j + HD * r + HD], proj[:, :, c0:c0 + HD])
            dve.tensor_copy(vals[:, :, 0:2 * HD], proj[:, :, V_S:V_S + 2 * HD])
            dve.tensor_copy(vals[:, :, 2 * HD:3 * HD], proj[:, :, V_D:V_D + HD])
            dve.tensor_scalar(w_idx, proj[:, :, W_I:W_I + 4], 1.0 / 16, None, ALU.mult).then_inc(rope_ready, 1)

            z0 = 8 * KT

            def outputs(j):
                kind, b, c, nk = JOBS[j]
                dve.wait_ge(o_ready, n.next("o_ready"))
                tiles = 1 if kind == "chosen" else 2
                t0 = {"window": 2 * c, "chosen": 4 + c, "memory": 6}[kind]
                src = ps[0:HD, 6, 0:2 * P * tiles].rearrange("p (a e t) -> p a e t", a=tiles, e=2)
                for e in range(2):
                    ins = dve.tensor_copy(oT[HD * e:HD * e + HD, t0:t0 + tiles, b * P:(b + 1) * P], src[:, :, e, :])
                ins.then_inc(o_copied, 1)

            def choose(b, rounds, last):
                if not rounds:
                    return
                dve.wait_ge(causal_ready, b + 1)
                sc = flat[:, 0:P * (b + 1)]
                for r in range(rounds):
                    step(dve.max(mx8, sc))
                    step(dve.match_replace(sc, mx8, sc, TAKEN))
                if last:
                    dve.tensor_scalar(mask[:, 0:P * (b + 1)], sc, 10 * OUT_OF_REACH, MASKED,
                                      ALU.is_gt, ALU.mult).then_inc(choice_made, 1)
                    dve.wait_ge(choice_made, b)

            unread = None
            for j, (kind, b, c, nk) in enumerate(JOBS):
                if kind == "index":
                    stream(DONE[j])
                    if c == 0:
                        continue
                    dve.wait_ge(z_freed, j + 1)
                    sc = flat[:, 0:nk]
                    step(dve.tensor_scalar(sc, sc, w_idx[:, b, 0:1], None, ALU.mult))
                    for g in range(1, 4):
                        ins = dve.scalar_tensor_tensor(out=sc, in0=flat[:, g * BANK:g * BANK + nk],
                                                       scalar=w_idx[:, b, g:g + 1], in1=sc, op0=ALU.mult, op1=ALU.add)
                        if g < 3:
                            step(ins)
                    ins.then_inc(iscore_ready, 1)
                    if unread is not None:
                        outputs(unread)
                        unread = None
                    continue
                heads, row = (2, BANK) if kind == "chosen" else (4, 256)
                lg = logits[:].rearrange("p (h s) -> p h s", s=row)[:, :, 0:nk]
                z = ps[:, 4:6, :].rearrange("p a (c s) -> p (a c) s", s=row)[:, :, 0:nk]
                dve.wait_ge(z_ready, z0 + j + 1)
                dve.wait_ge(pT_ready, n.now("pT_ready"))
                n.next("pT_ready")
                if kind == "memory":
                    ins = dve.tensor_scalar(lg, z, SCALE, None, ALU.mult)
                else:
                    if kind == "chosen" and b == 0:
                        dve.wait_ge(causal_ready, 1)
                    if kind == "window":
                        dve.wait_ge(masks_made, 3)
                    m = swa_mask[:, 256 - nk:256] if kind == "window" else mask[:, 0:nk]
                    ins = dve.scalar_tensor_tensor(out=lg, in0=z, scalar=SCALE,
                                                   in1=m.unsqueeze(1).broadcast_to([P, heads, nk]),
                                                   op0=ALU.mult, op1=ALU.add)
                ins.then_inc(z_freed, 1)
                dve.wait_ge(z_freed, j + 1)
                step(dve.tensor_reduce(mx[:, 0:heads], lg, AX.X, ALU.max))
                if kind == "window":
                    sink = snk[:, 4 * c:4 * c + 4]
                    step(dve.tensor_tensor(mx[:, 0:4], mx[:, 0:4], sink, ALU.max))
                    dve.tensor_tensor(snk_e[:, 0:4], sink, mx[:, 0:4], ALU.subtract)
                dve.tensor_scalar(neg[:, 0:heads], mx[:, 0:heads], -1.0, None, ALU.mult).then_inc(logit_ready, 1)
                if unread is not None:
                    outputs(unread)
                unread = j
                dve.wait_ge(exp_ready, n.next("exp_ready"))
                if kind == "window":
                    step(dve.tensor_tensor(tot[:, 0:4], tot[:, 0:4], snk_e[:, 0:4], ALU.add))
                step(dve.reciprocal(rec[:, 0:heads], tot[:, 0:heads]))
                dve.tensor_tensor(lg, lg, rec[:, 0:heads].unsqueeze(2).broadcast_to([P, heads, nk]),
                                  ALU.mult).then_inc(prob_ready, 1)
                stream(DONE[j])
                choose(b + 1, CHOICE[j], kind == "memory")
            outputs(unread)
            n.next("half_ready", 2 * GROUPS_BETWEEN)
            n.next("half_freed", 2 * GROUPS_BETWEEN)

            for j in range(2):
                t = slice(4 * j, 4 * j + 4)
                low(o_lo[:, t, :], oT[:, t, :], o_hi[:, t, :])
            for c in range(2):
                for kind in range(3):
                    split(1)
                    for hf in range(2):
                        complete()
                        t = slice(4 * c + 2 * hf, 4 * c + 2 * hf + 2)
                        g = slice(8 * kind + 4 * c + 2 * hf, 8 * kind + 4 * c + 2 * hf + 2)
                        banks = ps[:, 2 * hf:2 * hf + 2, :]
                        if kind == 0:
                            freed(dve.tensor_tensor(merged2[:, t, :], gates2[:, g, :], banks, ALU.mult))
                            continue
                        freed(dve.tensor_tensor(tmp[:, hf], gates2[:, g, :], banks, ALU.mult))
                    if kind == 0:
                        continue
                    dve.wait_ge(half_freed, n.now("half_freed"))
                    tiles = [slice(4 * c + 2 * hf, 4 * c + 2 * hf + 2) for hf in range(2)]
                    for hf, t in enumerate(tiles):
                        ins = dve.tensor_tensor(merged2[:, t, :], merged2[:, t, :], tmp[:, hf], ALU.add)
                        if kind == 2:
                            ins.then_inc(prod_ready, 1)
                    if kind == 1:
                        step(ins)
                        continue
                    for t in tiles:
                        low(m2_lo[:, t, :], merged2[:, t, :], m2_hi[:, t, :])
            residual(2, 2, 1.0)
            norm(x, TT, COL["g_mlp_2"])
            for c in range(2):
                with n.loop(dve, 4, unit=2, hi_ready=2, half_ready=2, half_freed=2, acthi_ready=2, operand_ready=2) as i:
                    split(2)
                    for hf in range(2):
                        n.next("half_ready")
                        dve.wait_ge(half_freed, n.next("half_freed"))
                        dve.tensor_tensor(tmp[:, hf], tmp[:, hf], tmp[:, hf], ALU.mult).then_inc(prod_ready, 1)
                    for hf in range(2):
                        t = bass.ds(i * 4 + 2 * hf, 2)
                        low(hid_lo[:, t, :], tmp[:, hf], hid_hi[:, t, :])
                if c == 0:
                    residual(2, 4, 1.0)
                else:
                    for i in range(2):
                        split(4 - i)
                        add(i, 1.0)
            last_norm(64)


_INS = ["x", "ff1_norm", "ff1_w_gate", "ff1_w_up", "ff1_w_down", "mix_norm", "w_in", "b_gate",
        "gmlp_ln_g", "gmlp_ln_b", "gmlp_w_s", "gmlp_b_s", "w_branch_a", "w_branch_b", "w_out",
        "ff2_norm", "ff2_w_gate", "ff2_w_up", "ff2_w_down", "final_norm", "mem_2", "positions_2",
        "g_mix_2", "w_in_2", "b_gate_2", "sinks_2", "g_mem_2", "w_mem_kv_2", "w_proj_swa_2",
        "w_proj_dsa_2", "w_proj_mem_2", "w_out_2", "g_mlp_2", "w_mlp_in_2", "w_mlp_out_2", "g_final_2"]


def kernel(**inputs):
    import numpy as np
    import concourse.bacc as bacc
    from concourse.bass_utils import run_bass_kernel_spmd

    nc = bacc.Bacc("TRN2", target_bir_lowering=False, num_devices=1)
    arrays, aps = {}, {}

    def give(name, a):
        arrays[f"in_{name}"] = a
        aps[name] = nc.dram_tensor(f"in_{name}", a.shape, mybir.dt.from_np(a.dtype), kind="ExternalInput").ap()

    for name in _INS:
        give(name, np.ascontiguousarray(inputs[name]))
    half = HD // 2
    give("inv_freq", np.power(np.float32(10000.0), -np.arange(half, dtype=np.float32) / np.float32(half)).astype(np.float32))
    shape = tuple(inputs["x"].shape)
    out = nc.dram_tensor("out_0", shape, F32, kind="ExternalOutput").ap()
    build(nc, aps, out)
    r = run_bass_kernel_spmd(nc, [arrays], core_ids=[0])
    return r.results[0]["out_0"]
```
